# Optimizing a Trainium2 kernel written in Bass

```python
import math
import jax, jax.numpy as jnp
from jax import lax
import numpy as np

D_MODEL = 1024
BATCH = 1
SEQ = 1024
DEPTH = 1

N_MEM = 256
EPS = 1e-5
Q_BLOCK = 128
NEG = -1e30
DIFF_HEADS = 8
DIFF_HD = 64
DIFF_W = DIFF_HEADS * 2 * DIFF_HD
DIL_GROUPS = ((128, 1), (512, 4), (2048, 16))
DIL_HEADS = 4
DIL_HD = 128
DIL_W = len(DIL_GROUPS) * DIL_HEADS * DIL_HD
DIL_OUT = DIL_HEADS * DIL_HD
X_HEADS = 4
X_HD = D_MODEL // X_HEADS
D_FF = 2816
CONV_W = 3
IN_SIZES = (DIFF_W, DIFF_W, DIFF_W, DIL_W, DIL_W, DIL_W, 2 * D_MODEL)
N_IN = sum(IN_SIZES)
SPLIT_POINTS = tuple(sum(IN_SIZES[:i + 1]) for i in range(len(IN_SIZES) - 1))

kernel_name = "hybrid_diff_dilated_gated_block"

def rmsnorm(x, g):
    x32 = x.astype(jnp.float32)
    y = x32 * lax.rsqrt(jnp.mean(x32 * x32, axis=-1, keepdims=True) + EPS)
    return (y * g.astype(jnp.float32)).astype(x.dtype)

def alibi_slopes(n):
    return jnp.exp2(-8.0 * jnp.arange(1, n + 1, dtype=jnp.float32) / n)

def diff_attention(q, k, v, lam, sub_g, lam_init):
    B, S, H, _, E = q.shape
    nb = S // Q_BLOCK
    scale = DIFF_HD ** -0.5
    kh = k.transpose(0, 2, 3, 1, 4)
    vh = v.transpose(0, 2, 1, 3)
    qblk = q.transpose(0, 2, 3, 1, 4).reshape(B, H, 2, nb, Q_BLOCK, E)
    qblk = jnp.moveaxis(qblk, 3, 0)
    slopes = alibi_slopes(H)
    kpos = jnp.arange(S)

    def one_block(args):
        qb, i = args
        qpos = i * Q_BLOCK + jnp.arange(Q_BLOCK)
        dist = qpos[:, None] - kpos[None, :]
        s = jnp.einsum('bhcqe,bhcke->bhcqk', qb, kh).astype(jnp.float32) * scale
        s = s - slopes[:, None, None, None] * dist.astype(jnp.float32)
        s = jnp.where(dist >= 0, s, NEG)
        p = jax.nn.softmax(s, axis=-1)
        a = p[:, :, 0] - lam * p[:, :, 1]
        return jnp.einsum('bhqk,bhke->bhqe', a.astype(vh.dtype), vh)

    o = lax.map(one_block, (qblk, jnp.arange(nb)))
    o = jnp.moveaxis(o, 0, 2).reshape(B, H, S, 2 * E).transpose(0, 2, 1, 3)
    o = rmsnorm(o, sub_g) * (1.0 - lam_init)
    return o.reshape(B, S, H * 2 * E)

def dilated_group(q, k, v, window, dil):
    B, S, H, E = q.shape
    blk = window // dil
    span = blk * dil
    Sp = -(-S // span) * span
    nb = Sp // span
    scale = E ** -0.5
    pad = ((0, 0), (0, Sp - S), (0, 0), (0, 0))

    def to_blocks(t):
        return jnp.pad(t, pad).reshape(B, nb, blk, dil, H, E)

    def with_prev(t):
        prev = jnp.pad(t, ((0, 0), (1, 0), (0, 0), (0, 0), (0, 0), (0, 0)))[:, :-1]
        return jnp.concatenate([prev, t], axis=2)

    qb = to_blocks(q)
    kk = with_prev(to_blocks(k))
    vv = with_prev(to_blocks(v))
    s = jnp.einsum('bnqrhe,bnkrhe->bnrhqk', qb, kk).astype(jnp.float32) * scale
    qi = jnp.arange(blk)[:, None]
    ki = jnp.arange(2 * blk)[None, :]
    step = blk + qi - ki
    n_idx = jnp.arange(nb)[:, None, None]
    valid = (step >= 0) & (step <= blk) & (n_idx * blk + ki - blk >= 0)
    slopes = alibi_slopes(H) / dil
    s = s - slopes[:, None, None] * (dil * step).astype(jnp.float32)
    s = jnp.where(valid[:, None, None], s, NEG)
    m = jnp.max(s, axis=-1, keepdims=True)
    p = jnp.exp(s - m)
    den = jnp.sum(p, axis=-1, keepdims=True)
    o = jnp.einsum('bnrhqk,bnkrhe->bnqrhe', (p / den).astype(v.dtype), vv)
    lse = (m + jnp.log(den))[..., 0]
    o = o.reshape(B, Sp, H, E)[:, :S]
    lse = lse.transpose(0, 1, 4, 2, 3).reshape(B, Sp, H)[:, :S]
    return o, lse

def dilated_mixer(q, k, v):
    B, S, G, H, E = q.shape
    outs, lses = [], []
    for g, (window, dil) in enumerate(DIL_GROUPS):
        o, lse = dilated_group(q[:, :, g], k[:, :, g], v[:, :, g], window, dil)
        outs.append(o)
        lses.append(lse)
    alpha = jax.nn.softmax(jnp.stack(lses, axis=0), axis=0)
    o = jnp.sum(alpha[..., None] * jnp.stack(outs, axis=0).astype(jnp.float32), axis=0)
    return o.astype(q.dtype).reshape(B, S, H * E)

def causal_dwconv(a, w, b):
    C = a.shape[-1]
    y = lax.conv_general_dilated(a, w[:, None, :], window_strides=(1,),
                                 padding=[(CONV_W - 1, 0)],
                                 dimension_numbers=('NWC', 'WIO', 'NWC'),
                                 feature_group_count=C)
    return y + b

def setup_inputs(seed: int = 0) -> dict:
    key = jax.random.key(seed)
    ks = jax.random.split(key, 24)
    f32 = jnp.float32

    def w(k, fan_in, fan_out):
        return jax.random.normal(k, (DEPTH, fan_in, fan_out), f32) * fan_in ** -0.5

    def gain(k, shape):
        return 1.0 + 0.02 * jax.random.normal(k, shape, f32)

    return {
        "x": jax.random.normal(ks[0], (BATCH, SEQ, D_MODEL), f32),
        "mem": jax.random.normal(ks[1], (BATCH, N_MEM, D_MODEL), f32),
        "mix_norm_g": gain(ks[2], (DEPTH, D_MODEL)),
        "w_in": w(ks[3], D_MODEL, N_IN),
        "b_gate": 0.02 * jax.random.normal(ks[4], (DEPTH, 2 * D_MODEL), f32),
        "lam_q1": 0.1 * jax.random.normal(ks[5], (DEPTH, DIFF_HD), f32),
        "lam_k1": 0.1 * jax.random.normal(ks[6], (DEPTH, DIFF_HD), f32),
        "lam_q2": 0.1 * jax.random.normal(ks[7], (DEPTH, DIFF_HD), f32),
        "lam_k2": 0.1 * jax.random.normal(ks[8], (DEPTH, DIFF_HD), f32),
        "diff_subln_g": gain(ks[9], (DEPTH, 2 * DIFF_HD)),
        "w_branch_diff": w(ks[10], DIFF_W, D_MODEL),
        "w_branch_dil": w(ks[11], DIL_OUT, D_MODEL),
        "w_out": w(ks[12], D_MODEL, D_MODEL),
        "cross_norm_g": gain(ks[13], (DEPTH, D_MODEL)),
        "mem_norm_g": gain(ks[14], (DEPTH, D_MODEL)),
        "w_cq": w(ks[15], D_MODEL, D_MODEL),
        "w_ckv": w(ks[16], D_MODEL, 2 * D_MODEL),
        "w_co": w(ks[17], D_MODEL, D_MODEL),
        "ffn_norm_g": gain(ks[18], (DEPTH, D_MODEL)),
        "w_up": w(ks[19], D_MODEL, 2 * D_FF),
        "conv_w": jax.random.normal(ks[20], (DEPTH, CONV_W, D_FF), f32) * CONV_W ** -0.5,
        "conv_b": 0.02 * jax.random.normal(ks[21], (DEPTH, D_FF), f32),
        "w_down": w(ks[22], D_FF, D_MODEL),
        "final_norm_g": gain(ks[23], (D_MODEL,)),
    }

def reference(x, mem, mix_norm_g, w_in, b_gate, lam_q1, lam_k1, lam_q2, lam_k2,
              diff_subln_g, w_branch_diff, w_branch_dil, w_out, cross_norm_g,
              mem_norm_g, w_cq, w_ckv, w_co, ffn_norm_g, w_up, conv_w, conv_b,
              w_down, final_norm_g):
    B, S, D = x.shape
    G = len(DIL_GROUPS)
    for l in range(DEPTH):
        lam_init = 0.8 - 0.6 * math.exp(-0.3 * l)
        h = rmsnorm(x, mix_norm_g[l])
        proj = h @ w_in[l]
        dq, dk, dv, sq, sk, sv, gcols = jnp.split(proj, SPLIT_POINTS, axis=-1)
        lam = (jnp.exp(jnp.sum(lam_q1[l].astype(jnp.float32) * lam_k1[l].astype(jnp.float32)))
               - jnp.exp(jnp.sum(lam_q2[l].astype(jnp.float32) * lam_k2[l].astype(jnp.float32)))
               + lam_init)
        o_diff = diff_attention(dq.reshape(B, S, DIFF_HEADS, 2, DIFF_HD),
                                dk.reshape(B, S, DIFF_HEADS, 2, DIFF_HD),
                                dv.reshape(B, S, DIFF_HEADS, 2 * DIFF_HD),
                                lam, diff_subln_g[l], lam_init)
        o_dil = dilated_mixer(sq.reshape(B, S, G, DIL_HEADS, DIL_HD),
                              sk.reshape(B, S, G, DIL_HEADS, DIL_HD),
                              sv.reshape(B, S, G, DIL_HEADS, DIL_HD))
        g_diff, g_dil = jnp.split(jax.nn.sigmoid(gcols + b_gate[l]), 2, axis=-1)
        y = g_diff * (o_diff @ w_branch_diff[l]) + g_dil * (o_dil @ w_branch_dil[l])
        x = x + y @ w_out[l]
        hq = rmsnorm(x, cross_norm_g[l])
        mn = rmsnorm(mem, mem_norm_g[l])
        q = (hq @ w_cq[l]).reshape(B, S, X_HEADS, X_HD)
        mk, mv = jnp.split(mn @ w_ckv[l], 2, axis=-1)
        mk = mk.reshape(B, -1, X_HEADS, X_HD)
        mv = mv.reshape(B, -1, X_HEADS, X_HD)
        s = jnp.einsum('bshe,bmhe->bhsm', q, mk).astype(jnp.float32) * X_HD ** -0.5
        p = jax.nn.softmax(s, axis=-1)
        o = jnp.einsum('bhsm,bmhe->bshe', p.astype(mv.dtype), mv).reshape(B, S, D)
        x = x + o @ w_co[l]
        h = rmsnorm(x, ffn_norm_g[l])
        a, b = jnp.split(h @ w_up[l], 2, axis=-1)
        a = causal_dwconv(a, conv_w[l], conv_b[l])
        x = x + (jax.nn.gelu(a, approximate=False) * b) @ w_down[l]
    return rmsnorm(x, final_norm_g)


_drawn_inputs = setup_inputs


def setup_inputs(seed=0):
    import zlib

    import numpy as np

    out = dict(_drawn_inputs(seed))
    spreads = {}
    factors = {'mix_norm_g': 3.422,
     'b_gate': 8.0,
     'lam_q1': 8.0,
     'lam_k2': 3.228,
     'diff_subln_g': 5.628,
     'cross_norm_g': 8.0,
     'mem_norm_g': 8.0,
     'ffn_norm_g': 3.913,
     'conv_b': 5.384,
     'final_norm_g': 2.907}
    for name, (base, spread) in spreads.items():
        noise = np.random.default_rng([zlib.crc32(name.encode()), seed]).standard_normal(out[name].shape)
        drawn = base * np.exp(spread * noise) if base else spread * noise
        out[name] = __import__('jax').numpy.asarray(drawn.astype(out[name].dtype))
    for name, factor in factors.items():
        out[name] = (out[name] * factor).astype(out[name].dtype)
    return out
```

```python
import math
from contextlib import ExitStack

import numpy as np

import concourse.bass as bass
from concourse import mybir

ALU = mybir.AluOpType
ACT = mybir.ActivationFunctionType
AX_X = mybir.AxisListType.X
F32 = mybir.dt.float32
F32R = mybir.dt.float32r

P = 128
D = 1024
S = 1024
MEM = 256
EPS = 1e-5
NK = D // P
NB = S // P
HALF = 512
DIFF_H = 8
DIL_H = 4
GROUPS = 3
X_H = 4
FF = 2816
FF_T = FF // P
CHUNK = 8
LAM_INIT = 0.8 - 0.6 * math.exp(-0.3 * 0)
DIFF_SCALE = 64 ** -0.5
DIL_SCALE = 128 ** -0.5
X_SCALE = 256 ** -0.5
NEG = -1e30

DIL_TILES = 3 * GROUPS + 1
W_DIL = 0
W_DIFF = W_DIL + DIL_H * DIL_TILES
W_GATE = W_DIFF + 3 * DIFF_H
W_BRANCH = W_GATE + 2 * NK - DIL_H
W_OUT = W_BRANCH + 2 * NK
W_MEM = W_OUT + NK
W_CQ = W_MEM + 2 * NK
W_CO = W_CQ + NK
W_FF = W_CO + NK
FF_CHUNKS = [(f, min(CHUNK, FF_T - f)) for f in range(0, FF_T, CHUNK)]
W_FF_AT = [W_FF + sum(2 * m + NK for _, m in FF_CHUNKS[:c]) for c in range(len(FF_CHUNKS))]
W_TOTAL = W_FF + sum(2 * m + NK for _, m in FF_CHUNKS)

U_MEM = 2 * W_MEM
U_CQ = U_MEM + 2 * NK


def unit_of(tile):
    if tile < W_MEM:
        return 2 * tile
    return U_MEM + tile - W_MEM if tile < W_CQ else U_CQ + 2 * (tile - W_CQ)


def dil_tiles(jb):
    return (4 if jb == 0 else 5) + 2 * (jb + 1)


def fills(n):
    return -(-n // 4)


DIL_FILLS = 2 * GROUPS + sum(fills(dil_tiles(b % 2)) for b in range(NB)) + 2
DIFF_FILLS = 2 + sum(fills(i + 1) for i in range(NB)) + 2
F_DIL = 0
F_DIFF = F_DIL + DIL_H * DIL_FILLS
F_MEM = F_DIFF + DIFF_H * DIFF_FILLS
F_CROSS = F_MEM + NK

C_MIX, C_CROSS, C_MEM, C_FFN, C_FINAL = (NK * i for i in range(5))
C_GATE = 5 * NK
C_CONVW = C_GATE + 2 * NK
C_CONVB = C_CONVW + 3 * FF_T
C_SUB = C_CONVB + FF_T
C_LAM = C_SUB + 1
C_ALL = C_LAM + 4 * 64

NEAR_W = 640 + 3
DIL_BIAS_W = NEAR_W + 1 + 256 + 512
REGION = 28928


def trunk_layer(nc, x, mem, w_stream, columns, ident, alibi_diff, alibi_dil, out):
    z_dram = nc.dram_tensor("gate_spill", [2 * NK, P, S], F32, kind="Internal").ap()
    x_spill = nc.dram_tensor("x_spill", [NK, P, S], F32, kind="Internal").ap()
    mem_rows = mem.rearrange("(j p) d -> p j d", p=P)
    x_cols = x.rearrange("(b p) (k d) -> k p b d", p=P, d=P)
    out_rows = out.rearrange("(b p) d -> b p d", p=P)

    with ExitStack() as ctx:
        def sb(name, shape, dt=F32, scope=ctx):
            return scope.enter_context(nc.sbuf_tensor(name, shape, dt))

        def sem(name):
            return ctx.enter_context(nc.semaphore(name))

        ps = ctx.enter_context(nc.psum_tensor("ps", [P, 8, HALF], F32))
        PJ = 0
        SC = 2
        TB = 6
        OB = 7

        h_hi = sb("h_hi", [P, NK, S], F32R)
        h_lo = sb("h_lo", [P, NK, S], F32R)
        w_raw = sb("w_raw", [P, 2, NK, P])
        w_hi = sb("w_hi", [P, 2, NK, P], F32R)
        w_lo = sb("w_lo", [P, 2, NK, P], F32R)
        rstd_bc = sb("rstd_bc", [P, S])
        idn = sb("idn", [P, P])
        col = sb("col", [P, C_ALL])
        lam_tmp = sb("lam_tmp", [P, 2, 64])
        small = sb("small", [P, 64])
        ones = small[:, 0:1]
        neg_half = small[:, 8:16]
        neglam = small[:, 16:17]
        sub_gain = small[:, 17:18]
        lam_dot = small[:, 20:22]
        lam_exp = small[:, 22:24]
        msq = small[:, 24:32]
        rstd_tok = small[:, 32:40]
        mem_ssq = small[:, 40:42]
        mem_msq = small[:, 42:44]
        mem_rstd = small[:, 44:46]
        spare = small[:, 56:63]
        zero_col = small[:, 52:53]

        def phase(*parts):
            with ExitStack() as scope:
                return [sb(p[0] or f"gap{nc.next_id()}", [P, p[1]], p[2] if len(p) > 2 else F32, scope)
                        for p in parts]

        def tiles(t, n):
            return t[:, :].rearrange("p (k s) -> p k s", k=n)

        LOW, OT, HIGH = 8 * S, (DIFF_H + DIL_H) * S, REGION - 20 * S
        TOP = REGION - 24 * S
        low, oT_, high = phase(("attn_low", LOW), ("oT", OT), ("attn_high", HIGH))
        oT = tiles(oT_, DIFF_H + DIL_H)
        od_hi, od_lo, y_hi, y_lo, top = phase(
            ("od_hi", 4 * S, F32R), ("od_lo", 4 * S, F32R), ("y_hi", 8 * S, F32R), ("y_lo", 8 * S, F32R), ("top", TOP))
        od_hi, od_lo, y_hi, y_lo = tiles(od_hi, DIL_H), tiles(od_lo, DIL_H), tiles(y_hi, NK), tiles(y_lo, NK)
        xt = tiles(phase(("xt", LOW))[0], NK)
        _, mn_hi, mn_lo, mem_x, _, = phase(
            (None, LOW), ("mn_hi", 2 * S, F32R), ("mn_lo", 2 * S, F32R), ("mem_x", 4 * S), (None, S))
        mn_hi, mn_lo = tiles(mn_hi, NK), tiles(mn_lo, NK)
        mem_x, mem_sq = mem_x[:, 0:2 * S].rearrange("p (j d) -> p j d", j=2), mem_x[:, 2 * S:3 * S]
        x_low, co_hi, co_lo, x_top = phase(
            ("x_low", LOW), ("co_hi", 8 * S, F32R), ("co_lo", 8 * S, F32R), ("x_top", TOP))
        co_hi, co_lo = tiles(co_hi, NK), tiles(co_lo, NK)
        _, m_hi, m_lo, ff = phase(
            (None, LOW), ("m_hi", 8 * S, F32R), ("m_lo", 8 * S, F32R), ("ff", TOP))
        m_hi, m_lo = tiles(m_hi, CHUNK), tiles(m_lo, CHUNK)
        o_rows = tiles(phase((None, LOW), ("o_rows", 8 * S))[1], 2 * NB)

        def view(t, at, n):
            return t[:, at:at + n]

        dl_q = [view(low, g * S, S) for g in range(3)]
        dl_k = [view(low, (3 + g) * S, S) for g in range(3)]
        dl_vT = view(low, 6 * S, S)
        dl_st = dl_vT.rearrange("p (b e) -> p b e", b=NB)
        dl_gate = view(low, 7 * S, S)
        dl_v = [view(high, g * S, S).rearrange("p (b e) -> p b e", b=NB) for g in range(3)]
        dl_p = [view(high, 3 * S + 1152 * i, 1152) for i in range(2)]
        dl_pT = view(high, 3 * S + 2304, 1152).rearrange("p (b q) -> p b q", b=9)
        dl_bias = view(high, 3 * S + 3456, DIL_BIAS_W)
        dl_near = dl_bias[:, 0:NEAR_W]
        dl_far = [dl_bias[:, NEAR_W + 1:NEAR_W + 257], dl_bias[:, NEAR_W + 257:NEAR_W + 769]]
        stat = view(high, 3 * S + 3456 + DIL_BIAS_W, 160)
        dl_mx, dl_nm, dl_den, dl_rd = stat[:, 0:16], stat[:, 16:24], stat[:, 24:32], stat[:, 32:40]
        df_q = [view(low, i * S, S) for i in range(2)]
        df_k = [view(low, (2 + i) * S, S) for i in range(2)]
        df_v = [view(low, (4 + i) * S, S).rearrange("p (b e) -> p b e", b=NB) for i in range(2)]
        df_p = [view(low, (6 + i) * S, S) for i in range(2)]
        df_vT = view(high, 0, S)
        df_a = view(high, S, S)
        df_aT = view(high, 2 * S, S).rearrange("p (b q) -> p b q", b=NB)
        df_bias = view(high, 3 * S, S)
        df_st = view(high, 4 * S, S).rearrange("p (b e) -> p b e", b=NB)
        df_sq = view(high, 5 * S, P)
        df_mx, df_nm, df_den, df_rd = (stat[:, 40 + 16 * i:56 + 16 * i] for i in range(4))
        df_cc, df_ssq, df_ms, df_rs = (stat[:, 104 + 8 * i:112 + 8 * i] for i in range(4))
        x0 = [view(low, i * S, S).rearrange("p (b d) -> p b d", b=NB) for i in range(2)]
        sq = [view(low, 2 * S, S), view(top, 2 * S, S), view(x_top, 2 * S, S), view(ff, S + 8, S)]
        acc = [view(low, 3 * S, S), view(top, 3 * S, S), view(x_top, 3 * S, S), view(ff, 2 * S + 8, S)]
        def head_parts(k):
            return (h_hi[:, k, :], h_lo[:, k, :]) if k < DIFF_H else (od_hi[:, k - DIFF_H, :], od_lo[:, k - DIFF_H, :])

        gate_st = [view(high, i * S, S) for i in range(2)]
        zb = [view(top, i * S, S) for i in range(2)]
        yd, yl = view(top, 2 * S, S), view(top, 3 * S, S)
        x_back = [[view(t, i * S, S) for i in range(2)] for t in (top, x_top)]
        mk = view(x_low, 0, 2 * S).rearrange("p (t m) -> p t m", t=NK)
        mv = view(x_low, 2 * S, 2 * S).rearrange("p (j e) -> p j e", j=2)
        qx = view(x_low, 4 * S, 2 * S).rearrange("p (j s) -> p j s", j=2)
        px = [view(x_low, (6 + i) * S, S).rearrange("p (b m) -> p b m", b=4) for i in range(2)]
        pxT = view(x_top, 0, S).rearrange("p (j q) -> p j q", j=2)
        mkh = view(x_top, S, HALF).rearrange("p (j m) -> p j m", j=2)
        mvh = view(x_top, S + HALF, HALF).rearrange("p (j e) -> p j e", j=2)
        mv_t = [view(x_top, 2 * S + i * MEM, MEM) for i in range(2)]
        x_st = view(x_top, 4 * S, 40)
        x_mx, x_nm, x_den, x_rd = (x_st[:, 8 * i:8 * i + 8] for i in range(4))
        a_pad = view(ff, 0, S + 2)
        c_buf = view(ff, S + 8, S)
        b_buf = view(ff, 2 * S + 8, S)

        const_in = sem("const_in")
        const_ok = sem("const_ok")
        lam_dots, lam_exps, lam_ok = sem("lam_dots"), sem("lam_exps"), sem("lam_ok")
        w_in = [sem("w_in0"), sem("w_in1")]
        w_rounded, w_ready = sem("w_rounded"), sem("w_ready")
        pj_ready, pj_free = sem("pj_ready"), sem("pj_free")
        tb_full, tb_free = sem("tb_full"), sem("tb_free")
        o_ready, o_free = sem("o_ready"), sem("o_free")
        x0_in = [sem("x0_in0"), sem("x0_in1")]
        x0_turned, x0_free = sem("x0_turned"), sem("x0_free")
        back_in = [[sem(f"back{i}_in{s}") for s in range(2)] for i in range(2)]
        feed_act = [sem(f"feed_act{i}") for i in range(4)]
        feed_dve = [sem(f"feed_dve{i}") for i in range(4)]
        nf_sum, nf_ms, nf_rstd = sem("nf_sum"), sem("nf_ms"), sem("nf_rstd")
        nf_turn, nf_bc = sem("nf_turn"), sem("nf_bc")
        bias_in = sem("bias_in")
        dl_s, dl_max, dl_neg, dl_exp = sem("dl_s"), sem("dl_max"), sem("dl_neg"), sem("dl_exp")
        dl_rec, dl_slope = sem("dl_rec"), sem("dl_slope")
        gate_out = sem("gate_out")
        df_s, df_max, df_neg, df_exp = sem("df_s"), sem("df_max"), sem("df_neg"), sem("df_exp")
        df_rec, df_coef, df_comb, df_slope = sem("df_rec"), sem("df_coef"), sem("df_comb"), sem("df_slope")
        df_mean, df_pow, df_norm = sem("df_mean"), sem("df_pow"), sem("df_norm")
        split_hi, split_lo = sem("split_hi"), sem("split_lo")
        z_in, z_sig, y_sum, y_round, y_done = sem("z_in"), sem("z_sig"), sem("y_sum"), sem("y_round"), sem("y_done")
        x_spilled = sem("x_spilled")
        mem_in, mem_sums, mem_mean, mem_pow = sem("mem_in"), sem("mem_sums"), sem("mem_mean"), sem("mem_pow")
        mem_norm, mem_turn, mem_hi, mem_lo = sem("mem_norm"), sem("mem_turn"), sem("mem_hi"), sem("mem_lo")
        x_head, x_s, x_max, x_neg, x_exp = sem("x_head"), sem("x_s"), sem("x_max"), sem("x_neg"), sem("x_exp")
        x_rec, x_norm, x_av, x_hi, x_lo = sem("x_rec"), sem("x_norm"), sem("x_av"), sem("x_hi"), sem("x_lo")
        conv0, conv1, conv2, gelu_ok = sem("conv0"), sem("conv1"), sem("conv2"), sem("gelu_ok")
        m_prod, m_round, m_done = sem("m_prod"), sem("m_round"), sem("m_done")
        fin_scaled, fin_turn, fin_row, fin_out = sem("fin_scaled"), sem("fin_turn"), sem("fin_row"), sem("fin_out")


        block = ctx.enter_context(nc.Block())

        def bank(b, n=HALF):
            return ps[:, b, 0:n]

        def banks(b, n):
            return ps[:, b:b + -(-n // HALF), :].rearrange("p b n -> p (b n)")[:, 0:n]

        def by_residue(ap):
            return ap.rearrange("p (j r) -> p r j", r=4)

        def half_by_residue(ap, half):
            return ap.rearrange("p (r j) -> p r j", r=4)[:, :, half * P:(half + 1) * P]

        @block.sync
        def _(sp):
            sp.dma_start(x0[0], x_cols[0]).then_inc(x0_in[0], 16)
            sp.dma_start(idn[:, :], ident).then_inc(const_in, 16)
            sp.dma_start(x0[1], x_cols[1]).then_inc(x0_in[1], 16)
            sp.dma_start(col[:, :], columns).then_inc(const_in, 16)
            with sp.Fori(1, NK // 2) as t:
                for s in range(2):
                    sp.wait_ge(x0_turned, t * 2 + (s - 1))
                    sp.dma_start(x0[s], x_cols[t * 2 + s]).then_inc(x0_in[s], 16)
            for n in range(2):
                sp.dma_start(w_raw[:, n], w_stream[n]).then_inc(w_in[n], 16)
            sp.dma_start(dl_bias, alibi_dil).then_inc(bias_in, 16)

            def load_weights(first, last):
                with sp.Fori(first // 2, last // 2) as t:
                    for s in range(2):
                        sp.wait_ge(w_ready, t * 2 + (s - 1))
                        sp.dma_start(w_raw[:, s], w_stream[t * 2 + s]).then_inc(w_in[s], 16)

            load_weights(2, W_DIFF)
            sp.wait_ge(tb_free, F_DIFF + 1)
            sp.dma_start(df_bias, alibi_diff).then_inc(bias_in, 16)
            load_weights(W_DIFF, W_TOTAL)
            for r in range(2 * NB):
                sp.wait_ge(fin_row, r + 1)
                sp.dma_start(out_rows[r // 2, :, (r % 2) * HALF:(r % 2 + 1) * HALF],
                             o_rows[:, r, :]).then_inc(fin_out, 16)
            sp.wait_ge(fin_out, 16 * 2 * NB)
            sp.wait_ge(gate_out, 16 * 2 * NK)
            sp.wait_ge(x_spilled, 16 * NK)

        @block.gpsimd
        def _(pool):
            def aside(value):
                pool.compute_val(value)
                pool.wait_ge(const_ok, 3)
                return value

            def split_tile(n, s, used):
                pool.wait_ge(w_in[s], (n - s) * 8 + 16)
                if used is not None:
                    pool.wait_ge(pj_ready, aside(used))
                pool.tensor_scalar(w_hi[:, s], w_raw[:, s], 1.0, 1.0, ALU.mult, ALU.mult).then_inc(w_rounded, 1)
                pool.wait_ge(w_rounded, n + 1)
                pool.tensor_tensor(w_lo[:, s], w_raw[:, s], w_hi[:, s].bitcast(F32),
                                   ALU.subtract).then_inc(w_ready, 1)

            def split_tiles(first, last):
                each = 1 if first >= W_MEM + 2 and last <= W_CQ + 2 else 2
                base = unit_of(first - 2) + each
                with pool.Fori(0, (last - first) // 2) as t:
                    for s in range(2):
                        split_tile(t * 2 + (first + s), s, t * (2 * each) + (base + s * each))

            def split_now(n):
                split_tile(n, n % 2, unit_of(n - 2) + (1 if W_MEM <= n - 2 < W_CQ else 2) if n >= 2 else None)

            def norm_root(i):
                pool.wait_ge(nf_ms, i + 1)
                pool.tensor_tensor(rstd_tok, msq, neg_half, ALU.pow).then_inc(nf_rstd, 1)

            def head_root(h):
                pool.wait_ge(o_free, aside(h * (2 * NB) + (DIL_H * NB + 2 * NB)))
                pool.tensor_scalar(df_ms, df_ssq, 1.0 / P, EPS, ALU.mult, ALU.add).then_inc(df_mean, 1)
                pool.wait_ge(df_mean, h + 1)
                pool.tensor_tensor(df_rs, df_ms, neg_half, ALU.pow).then_inc(df_pow, 1)

            pool.memset(ones, 1.0).then_inc(const_ok, 1)
            pool.memset(neg_half, -0.5).then_inc(const_ok, 1)
            pool.memset(zero_col, 0.0).then_inc(const_ok, 1)
            pool.wait_ge(const_ok, 3)
            split_now(0)
            split_now(1)
            norm_root(0)
            split_tiles(2, W_DIFF)
            for n in range(W_DIFF, W_DIFF + 3):
                split_now(n)
            with pool.Fori(0, DIFF_H // 2 - 1) as t:
                for par in range(2):
                    for j in range(3):
                        n = W_DIFF + 3 + 3 * par + j
                        split_tile(t * 6 + n, n % 2, t * 12 + unit_of(n - 1))
                    head_root(t * 2 + par)
            for n in range(W_GATE - 3, W_GATE):
                split_now(n)
            head_root(DIFF_H - 2)
            for n in range(W_GATE, W_GATE + 2):
                split_now(n)
            head_root(DIFF_H - 1)
            split_tiles(W_GATE + 2, W_MEM)
            for n in range(W_MEM, W_MEM + 2):
                split_now(n)
            norm_root(1)
            pool.wait_ge(mem_sums, 2)
            pool.tensor_scalar(mem_msq, mem_ssq, 1.0 / D, EPS, ALU.mult, ALU.add).then_inc(mem_mean, 1)
            pool.wait_ge(mem_mean, 1)
            pool.tensor_tensor(mem_rstd, mem_msq, neg_half[:, 0:2], ALU.pow).then_inc(mem_pow, 1)
            split_tiles(W_MEM + 2, W_CQ + 2)
            split_tiles(W_CQ + 2, W_FF)
            for n in range(W_FF, W_FF + 2):
                split_now(n)
            norm_root(2)
            split_tiles(W_FF + 2, W_TOTAL)
            norm_root(3)

        @block.tensor
        def _(pe):
            def product(n, s, half, u, hi=h_hi, lo=h_lo, kt=NK, cols=HALF, add_x=None):
                if half == 0:
                    pe.wait_ge(w_ready, n + 1)
                pe.wait_ge(pj_free, u + 1)
                b = half if cols == HALF else s
                at = slice(half * cols, half * cols + cols)
                for k in range(kt):
                    pe.matmul(bank(b, cols), w_hi[:, s, k, :], hi[:, k, at], start=(k == 0), stop=False)
                    pe.matmul(bank(b, cols), w_hi[:, s, k, :], lo[:, k, at], start=False, stop=False)
                    last = pe.matmul(bank(b, cols), w_lo[:, s, k, :], hi[:, k, at], start=False,
                                     stop=(k == kt - 1 and add_x is None))
                if add_x is not None:
                    for j in range(4):
                        last = pe.matmul(ps[:, b, j * P:(j + 1) * P], add_x[:, 4 * half + j, :], idn[:, :],
                                         start=False, stop=(j == 3))
                last.then_inc(pj_ready, 1)

            def products(first, tiles_n, **kw):
                with pe.Fori(0, tiles_n // 2) as t:
                    for s in range(2):
                        for half in range(2):
                            product(t * 2 + (first + s), s, half, t * 4 + (unit_of(first) + 2 * s + half), **kw)

            def turn_fill(f, sources):
                pe.wait_ge(tb_free, f + 1)
                for j, source in enumerate(sources):
                    last = pe.transpose(ps[:, TB, j * P:(j + 1) * P], source, idn[:, :])
                last.then_inc(tb_full, 1)

            def norm_sum(i):
                pe.wait_ge(feed_dve[i], (NK if i == 3 else 2 * NK) + 1)
                for b in range(NB):
                    last = pe.matmul(ps[:, OB, b:b + 1], acc[i][:, b * P:(b + 1) * P], ones, start=True, stop=True)
                last.then_inc(nf_sum, 1)

            def norm_spread(i):
                pe.wait_ge(nf_rstd, i + 1)
                for b in range(NB):
                    last = pe.transpose(ps[:, SC + b // 4, (b % 4) * P:(b % 4 + 1) * P],
                                        rstd_tok[:, b:b + 1].to_broadcast([P, P]), idn[:, :])
                last.then_inc(nf_turn, 1)

            pe.wait_ge(const_in, 32)
            pe.wait_ge(const_ok, 3)
            with pe.Fori(0, NK // 2) as t:
                for s in range(2):
                    pe.wait_ge(x0_in[s], t * 16 + 16)
                    pe.wait_ge(x0_free, t * 2 + (s + 1))
                    for b in range(NB):
                        last = pe.transpose(ps[:, SC + 2 * s + b // 4, (b % 4) * P:(b % 4 + 1) * P],
                                            x0[s][:, b, :], idn[:, :])
                    last.then_inc(x0_turned, 1)
            norm_sum(0)
            norm_spread(0)

            def dil_scores(b):
                rho, jb = b // 2, b % 2
                sc = banks(SC, 1152)
                near0, near = (0, 512) if jb == 0 else (384, 640)
                at = 0
                for g, k0, n in ((0, near0, near), (1, rho * 256, (jb + 1) * P), (2, rho * 256, (jb + 1) * P)):
                    while n:
                        m = min(n, HALF - at % HALF)
                        last = pe.matmul(sc[:, at:at + m], dl_q[g][:, b * P:(b + 1) * P], dl_k[g][:, k0:k0 + m],
                                         start=True, stop=True)
                        at, k0, n = at + m, k0 + m, n - m
                last.then_inc(dl_s, 1)

            def dil_values(b):
                rho, jb = b // 2, b % 2
                return ([dl_v[0][:, i, :] for i in (range(4) if jb == 0 else range(3, 8))]
                        + [dl_v[g][:, 2 * rho + j, :] for g in (1, 2) for j in range(jb + 1)])

            with pe.Fori(0, DIL_H) as t:
                f = t * DIL_FILLS
                for j in range(DIL_TILES):
                    for half in range(2):
                        product(t * DIL_TILES + j, j % 2, half, t * (2 * DIL_TILES) + (2 * j + half))
                        if half == 0 and j in (3, 6, 9):
                            pe.wait_ge(pj_free, t * (2 * DIL_TILES) + (2 * j + 2))
                            for part in range(2):
                                turn_fill(f, [dl_vT[:, (4 * part + i) * P:(4 * part + i + 1) * P] for i in range(4)])
                                f = f + 1
                pe.wait_ge(pj_free, t * (2 * DIL_TILES) + 2 * DIL_TILES)
                for b in range(NB + 1):
                    if b < NB:
                        if b >= 1:
                            pe.wait_ge(dl_max, t * (2 * NB) + 2 * b)
                        dil_scores(b)
                    if b >= 1:
                        n = dil_tiles((b - 1) % 2)
                        pe.wait_ge(dl_exp, t * NB + b)
                        for k in range(fills(n)):
                            turn_fill(f, [dl_p[(b - 1) % 2][:, i * P:(i + 1) * P]
                                          for i in range(4 * k, min(n, 4 * k + 4))])
                            f = f + 1
                        pe.wait_ge(tb_free, f + 1)
                        if b >= 2:
                            pe.wait_ge(o_free, t * NB + (b - 1))
                        for i, v in enumerate(dil_values(b - 1)):
                            last = pe.matmul(ps[:, OB, 0:P], dl_pT[:, i, :], v, start=(i == 0), stop=(i == n - 1))
                        last.then_inc(o_ready, 1)
                pe.wait_ge(o_free, t * NB + NB)
                for part in range(2):
                    turn_fill(f, [dl_st[:, 4 * part + i, :] for i in range(4)])
                    f = f + 1

            def df_scores(h, i, par):
                for m in range(2):
                    if i >= 1:
                        pe.wait_ge(df_max, h * (2 * NB) + (2 * i - 1 + m))
                    rows = slice(64 * m, 64 * m + 64)
                    n = (i + 1) * P
                    for at in range(0, n, HALF):
                        w = min(HALF, n - at)
                        last = pe.matmul(ps[:, SC + 2 * m + at // HALF, 0:w], df_q[par][rows, i * P:(i + 1) * P],
                                         df_k[par][rows, at:at + w], start=True, stop=True)
                    last.then_inc(df_s, 1)

            def df_output(h, i, par, f):
                pe.wait_ge(df_comb, h * NB + (i + 1))
                for k in range(fills(i + 1)):
                    turn_fill(f, [df_a[:, j * P:(j + 1) * P] for j in range(4 * k, min(i + 1, 4 * k + 4))])
                    f = f + 1
                pe.wait_ge(tb_free, f + 1)
                if i >= 1:
                    pe.wait_ge(o_free, h * (2 * NB) + (DIL_H * NB + 2 * i))
                for j in range(i + 1):
                    last = pe.matmul(ps[:, OB, 0:P], df_aT[:, j, :], df_v[par][:, j, :], start=(j == 0), stop=(j == i))
                last.then_inc(o_ready, 1)
                return f

            def df_turn_values(f, u):
                pe.wait_ge(pj_free, u + 3)
                for part in range(2):
                    turn_fill(f, [df_vT[:, (4 * part + i) * P:(4 * part + i + 1) * P] for i in range(4)])
                    f = f + 1
                return f

            def df_head(pair, par, f, project):
                h = pair * 2 + par
                todo = [(j, half) for j in range(3) for half in range(2)] if project else []

                def next_product():
                    j, half = todo.pop(0)
                    n = W_DIFF + 3 + 3 * par + j
                    product(pair * 6 + n, n % 2, half, pair * 12 + (unit_of(n) + half))

                pe.wait_ge(pj_free, pair * 12 + (unit_of(W_DIFF + 3 * par) + 3 + 3))
                for i in range(NB):
                    df_scores(h, i, par)
                    if i >= 3 and todo:
                        next_product()
                    if i >= 1:
                        f = df_output(h, i - 1, par, f)
                f = df_output(h, NB - 1, par, f)
                if todo:
                    next_product()
                    f = df_turn_values(f, pair * 12 + (unit_of(W_DIFF + 3 + 3 * par) + 5))
                pe.wait_ge(df_norm, h + 1)
                for part in range(2):
                    turn_fill(f, [df_st[:, 4 * part + i, :] for i in range(4)])
                    f = f + 1
                return f

            for j in range(3):
                for half in range(2):
                    product(W_DIFF + j, j % 2, half, unit_of(W_DIFF + j) + half)
            df_turn_values(F_DIFF, unit_of(W_DIFF) + 5)
            with pe.Fori(0, DIFF_H // 2 - 1) as t:
                f = t * (2 * DIFF_FILLS) + (F_DIFF + 2)
                for par in range(2):
                    f = df_head(t, par, f, True)
            f = df_head(DIFF_H // 2 - 1, 0, F_DIFF + 2 + (DIFF_H - 2) * DIFF_FILLS, True)
            f = df_head(DIFF_H // 2 - 1, 1, f, False)
            assert f == F_MEM

            products(W_GATE, W_BRANCH - W_GATE)

            pe.wait_ge(split_lo, DIFF_H + DIL_H)
            with pe.Fori(0, NK) as t:
                for half in range(2):
                    product(t * 2 + W_BRANCH, 0, half, t * 4 + (unit_of(W_BRANCH) + half))
                for half in range(2):
                    product(t * 2 + (W_BRANCH + 1), 1, half, t * 4 + (unit_of(W_BRANCH) + 2 + half),
                            hi=od_hi, lo=od_lo, kt=DIL_H)

            pe.wait_ge(y_done, NK + 1)
            with pe.Fori(0, NK // 2) as t:
                for s in range(2):
                    pe.wait_ge(back_in[0][s], t * 16 + 16)
                    for half in range(2):
                        product(t * 2 + (W_OUT + s), s, half, t * 4 + (unit_of(W_OUT) + 2 * s + half),
                                hi=y_hi, lo=y_lo, add_x=x_back[0][s].rearrange("p (b d) -> p b d", b=NB))
            norm_sum(1)

            pe.wait_ge(mem_norm, 2)
            for k in range(NK):
                for j in range(2):
                    at = (k % 2) * MEM + j * P
                    last = pe.transpose(ps[:, SC + k // 2, at:at + P], mem_x[:, j, k * P:(k + 1) * P], idn[:, :])
                if k % 2:
                    last.then_inc(mem_turn, 1)
            pe.wait_ge(mem_lo, NK)
            norm_spread(1)
            with pe.Fori(0, NK // 2) as t:
                for s in range(2):
                    product(t * 2 + (W_MEM + s), s, 0, t * 2 + (U_MEM + s), hi=mn_hi, lo=mn_lo, cols=MEM)
            with pe.Fori(0, NK // 2) as t:
                for s in range(2):
                    product(t * 2 + (W_MEM + NK + s), s, 0, t * 2 + (U_MEM + NK + s), hi=mn_hi, lo=mn_lo, cols=MEM)
                for s in range(2):
                    pe.wait_ge(pj_free, t * 2 + (U_MEM + NK + s + 3))
                    turn_fill(t * 2 + (F_MEM + s), [mv_t[s][:, j * P:(j + 1) * P] for j in range(2)])

            with pe.Fori(0, X_H) as t:
                for s in range(2):
                    for half in range(2):
                        product(t * 2 + (W_CQ + s), s, half, t * 4 + (U_CQ + 2 * s + half))
                pe.wait_ge(pj_free, t * 4 + (U_CQ + 6))
                pe.wait_ge(x_head, t * 2 + 2)
                for g in range(2):
                    for b in range(4):
                        q = 4 * g + b
                        for k in range(2):
                            last = pe.matmul(ps[:, SC + 2 * g + b // 2, (b % 2) * MEM:(b % 2 + 1) * MEM],
                                             qx[:, k, q * P:(q + 1) * P], mkh[:, k, :], start=(k == 0), stop=(k == 1))
                    last.then_inc(x_s, 1)
                for g in range(2):
                    pe.wait_ge(x_norm, t * 2 + (g + 1))
                    for j in range(2):
                        turn_fill(t * 4 + (F_CROSS + 2 * g + j), [px[g][:, b, j * P:(j + 1) * P] for b in range(4)])
                    pe.wait_ge(tb_free, t * 4 + (F_CROSS + 2 * g + 3))
                    for e in range(2):
                        if 2 * g + e:
                            pe.wait_ge(x_lo, t * 4 + (2 * g + e))
                        for j in range(2):
                            last = pe.matmul(bank(OB), mvh[:, j, e * P:(e + 1) * P], pxT[:, j, :],
                                             start=(j == 0), stop=(j == 1))
                        last.then_inc(x_av, 1)

            pe.wait_ge(x_lo, 4 * X_H)
            products(W_CO, NK, hi=co_hi, lo=co_lo)
            norm_sum(2)
            norm_spread(2)

            for c, (f0, m) in enumerate(FF_CHUNKS):
                products(W_FF_AT[c], 2 * m)
                pe.wait_ge(m_done, f0 + m + 1)
                products(W_FF_AT[c] + 2 * m, NK, hi=m_hi, lo=m_lo, kt=m)
            norm_sum(3)

            pe.wait_ge(fin_scaled, NK)
            for r in range(2 * NB):
                b, half = r // 2, r % 2
                if r >= 4:
                    pe.wait_ge(fin_row, r - 3)
                for j in range(4):
                    last = pe.transpose(ps[:, SC + r % 4, j * P:(j + 1) * P],
                                        xt[:, 4 * half + j, b * P:(b + 1) * P], idn[:, :])
                last.then_inc(fin_turn, 1)

        @block.vector
        def _(dve):
            def aside(value, loaded):
                dve.compute_val(value)
                dve.wait_ge(bias_in, loaded)
                return value

            def take(u, half, out, kind, scale=None, cols=HALF, other=None):
                dve.wait_ge(pj_ready, u + 1)
                src = bank(half, cols)
                if kind == "copy":
                    ins = dve.tensor_copy(out, src)
                elif kind == "add":
                    ins = dve.tensor_tensor(out, src, other, ALU.add)
                elif kind == "mult":
                    ins = dve.tensor_tensor(out, src, other, ALU.mult)
                else:
                    root = rstd_bc[:, half * HALF:(half + 1) * HALF]
                    if kind == "residue":
                        src, root = by_residue(src), by_residue(root)
                    if scale is None:
                        ins = dve.tensor_tensor(out, src, root, ALU.mult)
                    else:
                        ins = dve.scalar_tensor_tensor(out, src, scale, root, ALU.mult, ALU.mult)
                ins.then_inc(pj_free, 1)

            def halves(ap, half):
                return ap[:, half * HALF:(half + 1) * HALF]

            def norm_begin(i):
                dve.memset(acc[i], 0.0).then_inc(feed_dve[i], 1)

            def feed(i, k, gain, source, hi, lo):
                dve.wait_ge(feed_act[i], k * 2 + 2)
                dve.scalar_tensor_tensor(lo, source, gain, hi, ALU.mult, ALU.subtract).then_inc(feed_dve[i], 1)
                dve.wait_ge(feed_dve[i], k * 2 + 2)
                dve.tensor_tensor(acc[i], acc[i], sq[i], ALU.add).then_inc(feed_dve[i], 1)

            def norm_mean(i):
                dve.wait_ge(nf_sum, i + 1)
                dve.tensor_scalar(msq, ps[:, OB, 0:NB], 1.0 / D, EPS, ALU.mult, ALU.add).then_inc(nf_ms, 1)

            dve.memset(spare[:, 0:1], 0.0).then_inc(pj_free, 1)
            dve.memset(spare[:, 1:2], 0.0).then_inc(pj_free, 1)
            norm_begin(0)
            dve.memset(spare[:, 3:4], 0.0).then_inc(x0_free, 1)
            dve.memset(spare[:, 4:5], 0.0).then_inc(x0_free, 1)
            dve.wait_ge(const_in, 32)
            for i in range(2):
                q1, k1 = (col[:, C_LAM + 64 * (2 * i + j):C_LAM + 64 * (2 * i + j + 1)] for j in range(2))
                dve.tensor_tensor_reduce(lam_tmp[:, i, :], q1, k1, 1.0, 0.0, ALU.mult, ALU.add,
                                         lam_dot[:, i:i + 1]).then_inc(lam_dots, 1)
            dve.tensor_scalar(sub_gain, col[:, C_SUB:C_SUB + 1], 1.0 - LAM_INIT, None, ALU.mult).then_inc(lam_ok, 1)
            dve.wait_ge(lam_exps, 1)
            dve.scalar_tensor_tensor(neglam, lam_exp[:, 1:2], -LAM_INIT, lam_exp[:, 0:1], ALU.add,
                                     ALU.subtract).then_inc(lam_ok, 1)
            dve.wait_ge(feed_dve[0], 1)
            with dve.Fori(0, NK // 2) as t:
                for s in range(2):
                    k = t * 2 + s
                    dve.wait_ge(feed_act[0], t * 4 + (2 * s + 2))
                    dve.scalar_tensor_tensor(h_lo[:, k, :], banks(SC + 2 * s, S), col[:, bass.ds(t * 2 + (C_MIX + s), 1)],
                                             h_hi[:, k, :].bitcast(F32), ALU.mult, ALU.subtract).then_inc(x0_free, 1)
                    dve.tensor_tensor(acc[0], acc[0], sq[0], ALU.add).then_inc(feed_dve[0], 2)
                    dve.wait_ge(feed_dve[0], t * 4 + (2 * s + 3))
            norm_mean(0)

            dve.wait_ge(bias_in, 16)
            dve.tensor_scalar(dl_bias, dl_bias, 0.25, None, ALU.mult).then_inc(dl_slope, 1)
            dve.wait_ge(nf_bc, 1)
            with dve.Fori(0, DIL_H) as t:
                u = t * (2 * DIL_TILES)
                for j in range(DIL_TILES):
                    g, kind = j // 3, j % 3
                    for half in range(2):
                        if j == 9:
                            take(u + (2 * j + half), half, halves(dl_gate, half), "plain")
                        elif kind == 0:
                            take(u + (2 * j + half), half, half_by_residue(dl_q[g], half), "residue", DIL_SCALE)
                        else:
                            buf = dl_k[g] if kind == 1 else dl_vT
                            if g == 0:
                                take(u + (2 * j + half), half, halves(buf, half), "plain")
                            else:
                                take(u + (2 * j + half), half, half_by_residue(buf, half), "residue")
                dve.wait_ge(dl_slope, t + 1)
                for b in range(NB + 1):
                    if b < NB:
                        rho, jb = b // 2, b % 2
                        near, far = (512, 256) if jb == 0 else (640, 512)
                        near0 = 131 - rho if jb == 0 else 3 - rho
                        sc = banks(SC, near + far)
                        pb = dl_p[b % 2]
                        dve.wait_ge(dl_s, aside(t * NB + (b + 1), 16))
                        dve.tensor_tensor_reduce(pb[:, 0:near], sc[:, 0:near], dl_near[:, near0:near0 + near],
                                                 1.0, -3e38, ALU.add, ALU.max, dl_mx[:, 2 * b:2 * b + 1]).then_inc(dl_max, 1)
                        dve.tensor_tensor_reduce(pb[:, near:near + far], sc[:, near:near + far], dl_far[jb],
                                                 1.0, -3e38, ALU.add, ALU.max, dl_mx[:, 2 * b + 1:2 * b + 2]).then_inc(dl_max, 1)
                        dve.wait_ge(dl_max, t * (2 * NB) + (2 * b + 2))
                        dve.tensor_scalar(dl_nm[:, b:b + 1], dl_mx[:, 2 * b:2 * b + 1], dl_mx[:, 2 * b + 1:2 * b + 2],
                                          -1.0, ALU.max, ALU.mult).then_inc(dl_neg, 1)
                    if b >= 1:
                        dve.wait_ge(dl_exp, t * NB + b)
                        dve.reciprocal(dl_rd[:, b - 1:b], dl_den[:, b - 1:b]).then_inc(dl_rec, 1)
                dve.tensor_scalar(dl_bias, dl_bias, 0.25, None, ALU.mult).then_inc(dl_slope, 1)
                dve.wait_ge(gate_out, t * 16 + 16)

            def df_take(unit0, par, j, half):
                buf = (df_q[par], df_k[par], df_vT)[j]
                take(unit0 + (2 * j + half), half, halves(buf, half), "plain", DIFF_SCALE if j == 0 else None)

            def df_head(pair, par, f, project):
                h = pair * 2 + par
                unit0 = pair * 12 + unit_of(W_DIFF + 3 + 3 * par)
                todo = [(j, half) for j in range(3) for half in range(2)] if project else []
                dve.wait_ge(df_slope, h + 1)
                for i in range(NB):
                    n = (i + 1) * P
                    if i >= 1:
                        dve.wait_ge(df_comb, h * NB + i)
                    for m in range(2):
                        dve.wait_ge(df_s, aside(h * (2 * NB) + (2 * i + m + 1), 32))
                        dve.tensor_tensor_reduce(df_p[m][:, 0:n], banks(SC + 2 * m, n), df_bias[:, S - n:S],
                                                 1.0, -3e38, ALU.add, ALU.max,
                                                 df_mx[:, 2 * i + m:2 * i + m + 1]).then_inc(df_max, 1)
                    dve.wait_ge(df_max, h * (2 * NB) + (2 * i + 2))
                    two = slice(2 * i, 2 * i + 2)
                    dve.tensor_scalar(df_nm[:, two], df_mx[:, two], -1.0, None, ALU.mult).then_inc(df_neg, 1)
                    dve.wait_ge(df_exp, h * (2 * NB) + (2 * i + 2))
                    dve.reciprocal(df_rd[:, two], df_den[:, two]).then_inc(df_rec, 1)
                    dve.wait_ge(df_rec, h * NB + (i + 1))
                    dve.scalar_tensor_tensor(df_cc[:, i:i + 1], df_rd[:, 2 * i + 1:2 * i + 2], neglam,
                                             df_den[:, 2 * i:2 * i + 1], ALU.mult, ALU.mult).then_inc(df_coef, 1)
                    dve.wait_ge(df_coef, h * NB + (i + 1))
                    dve.wait_ge(tb_full, f)
                    dve.scalar_tensor_tensor(df_a[:, 0:n], df_p[1][:, 0:n], df_cc[:, i:i + 1], df_p[0][:, 0:n],
                                             ALU.mult, ALU.add).then_inc(df_comb, 1)
                    f = f + fills(i + 1)
                    if i >= 3 and todo:
                        df_take(unit0, 1 - par, *todo.pop(0))
                dve.wait_ge(df_comb, h * NB + NB)
                dve.tensor_scalar(df_bias, df_bias, 0.5, None, ALU.mult).then_inc(df_slope, 1)
                if todo:
                    df_take(unit0, 1 - par, *todo.pop(0))
                dve.wait_ge(df_pow, h + 1)
                dve.tensor_tensor(df_st, df_st, df_rs.unsqueeze(2).to_broadcast([P, NB, P]), ALU.mult).then_inc(df_norm, 1)
                return f + (4 if project else 2)

            for j in range(3):
                for half in range(2):
                    df_take(unit_of(W_DIFF), 0, j, half)
            dve.wait_ge(bias_in, 32)
            dve.tensor_scalar(df_bias, df_bias, 0.5, None, ALU.mult).then_inc(df_slope, 1)
            dve.wait_ge(lam_ok, 2)
            with dve.Fori(0, DIFF_H // 2 - 1) as t:
                f = t * (2 * DIFF_FILLS) + (F_DIFF + 2)
                for par in range(2):
                    f = df_head(t, par, f, True)
            f = df_head(DIFF_H // 2 - 1, 0, F_DIFF + 2 + (DIFF_H - 2) * DIFF_FILLS, True)
            df_head(DIFF_H // 2 - 1, 1, f, False)

            def split_heads(order):
                for n, k in order:
                    _, lo = head_parts(k)
                    dve.wait_ge(split_hi, n + 1)
                    dve.tensor_tensor(lo, oT[:, k, :], head_parts(k)[0].bitcast(F32), ALU.subtract).then_inc(split_lo, 1)

            split_heads([(n, DIFF_H + n) for n in range(DIL_H)])
            with dve.Fori(0, (W_BRANCH - W_GATE) // 2) as t:
                dve.wait_ge(gate_out, t * 32 + 16 * DIL_H)
                for s in range(2):
                    for half in range(2):
                        take(t * 4 + (unit_of(W_GATE) + 2 * s + half), half, halves(gate_st[s], half), "plain")
            split_heads([(DIL_H + k, k) for k in range(DIFF_H)])

            dve.memset(spare[:, 5:6], 0.0).then_inc(y_done, 1)
            with dve.Fori(0, NK) as t:
                u = t * 4 + unit_of(W_BRANCH)
                dve.wait_ge(z_sig, t * 2 + 2)
                dve.wait_ge(y_done, t + 1)
                for half in range(2):
                    take(u + half, half, halves(yd, half), "mult", other=halves(zb[0], half))
                for half in range(2):
                    take(u + (2 + half), half, halves(yl, half), "mult", other=halves(zb[1], half))
                dve.wait_ge(pj_free, u + 6)
                dve.tensor_tensor(yd, yd, yl, ALU.add).then_inc(y_sum, 1)
                dve.wait_ge(y_round, t + 1)
                dve.tensor_tensor(y_lo[:, t, :], yd, y_hi[:, t, :].bitcast(F32), ALU.subtract).then_inc(y_done, 1)

            dve.wait_ge(y_done, NK + 1)
            norm_begin(1)
            dve.wait_ge(feed_dve[1], 1)
            with dve.Fori(0, NK) as k:
                for half in range(2):
                    take(k * 2 + (unit_of(W_OUT) + half), half, xt[:, k, half * HALF:(half + 1) * HALF], "copy")
                dve.wait_ge(pj_free, k * 2 + (unit_of(W_OUT) + 4))
                feed(1, k, col[:, bass.ds(k + C_CROSS, 1)], xt[:, k, :], h_hi[:, k, :].bitcast(F32), h_lo[:, k, :])
            norm_mean(1)

            dve.wait_ge(mem_pow, 1)
            for j in range(2):
                dve.tensor_scalar(mem_x[:, j, :], mem_x[:, j, :], mem_rstd[:, j:j + 1], None,
                                  ALU.mult).then_inc(mem_norm, 1)
            for k in range(NK):
                dve.wait_ge(mem_hi, (k | 1) + 1)
                dve.scalar_tensor_tensor(mn_lo[:, k, :], ps[:, SC + k // 2, (k % 2) * MEM:(k % 2 + 1) * MEM],
                                         col[:, C_MEM + k:C_MEM + k + 1], mn_hi[:, k, :].bitcast(F32),
                                         ALU.mult, ALU.subtract).then_inc(mem_lo, 1)
            dve.wait_ge(x_spilled, 16 * NK)
            with dve.Fori(0, NK // 2) as t:
                for s in range(2):
                    take(t * 2 + (U_MEM + s), s, mk[:, t * 2 + s, :], "copy", cols=MEM)
            with dve.Fori(0, NK // 2) as t:
                for s in range(2):
                    take(t * 2 + (U_MEM + NK + s), s, mv_t[s], "copy", cols=MEM)

            dve.wait_ge(nf_bc, 2)
            with dve.Fori(0, X_H) as t:
                for s in range(2):
                    for half in range(2):
                        take(t * 4 + (U_CQ + 2 * s + half), half, halves(qx[:, s, :], half), "plain", X_SCALE)
                for g in range(2):
                    four = slice(4 * g, 4 * g + 4)
                    dve.wait_ge(x_s, t * 2 + (g + 1))
                    dve.tensor_reduce(x_mx[:, four], banks(SC + 2 * g, S).rearrange("p (b m) -> p b m", b=4),
                                      AX_X, ALU.max).then_inc(x_max, 1)
                    dve.wait_ge(x_max, t * 2 + (g + 1))
                    dve.tensor_scalar(x_nm[:, four], x_mx[:, four], -1.0, None, ALU.mult).then_inc(x_neg, 1)
                for g in range(2):
                    four = slice(4 * g, 4 * g + 4)
                    dve.wait_ge(x_exp, t * 8 + (4 * g + 4))
                    dve.reciprocal(x_rd[:, four], x_den[:, four]).then_inc(x_rec, 1)
                    dve.wait_ge(x_rec, t * 2 + (g + 1))
                    dve.tensor_tensor(px[g], px[g], x_rd[:, four].unsqueeze(2).to_broadcast([P, 4, MEM]),
                                      ALU.mult).then_inc(x_norm, 1)
                for c in range(4):
                    dve.wait_ge(x_hi, t * 4 + (c + 1))
                    at = slice((c // 2) * HALF, (c // 2 + 1) * HALF)
                    dve.tensor_tensor(co_lo[:, t * 2 + c % 2, at], bank(OB), co_hi[:, t * 2 + c % 2, at].bitcast(F32),
                                      ALU.subtract).then_inc(x_lo, 1)

            norm_begin(2)
            dve.wait_ge(feed_dve[2], 1)
            with dve.Fori(0, NK // 2) as t:
                for s in range(2):
                    k = t * 2 + s
                    dve.wait_ge(back_in[1][s], t * 16 + 16)
                    for half in range(2):
                        take(t * 4 + (unit_of(W_CO) + 2 * s + half), half, xt[:, k, half * HALF:(half + 1) * HALF],
                             "add", other=halves(x_back[1][s], half))
                    dve.wait_ge(pj_free, t * 4 + (unit_of(W_CO) + 2 * s + 4))
                    feed(2, k, col[:, bass.ds(t * 2 + (C_FFN + s), 1)], xt[:, k, :], h_hi[:, k, :].bitcast(F32),
                         h_lo[:, k, :])
            norm_mean(2)

            dve.memset(a_pad[:, 0:2], 0.0).then_inc(conv2, 1)
            dve.memset(c_buf, 0.0).then_inc(m_prod, 1)
            dve.memset(spare[:, 6:7], 0.0).then_inc(m_done, 1)
            dve.wait_ge(nf_bc, 3)
            for c, (f0, m) in enumerate(FF_CHUNKS):
                with dve.Fori(0, m) as t:
                    u = t * 4 + unit_of(W_FF_AT[c])
                    dve.wait_ge(conv2, t + (f0 + 1))
                    for half in range(2):
                        take(u + half, half, a_pad[:, 2 + half * HALF:2 + (half + 1) * HALF], "plain")
                    dve.wait_ge(conv0, t + (f0 + 1))
                    for tap, done in ((1, conv1), (2, conv2)):
                        w_tap = col[:, bass.ds(t + (C_CONVW + tap * FF_T + f0), 1)]
                        dve.scalar_tensor_tensor(c_buf, a_pad[:, tap:tap + S], w_tap, c_buf, ALU.mult,
                                                 ALU.add).then_inc(done, 1)
                        if tap == 1:
                            dve.wait_ge(conv1, t + (f0 + 1))
                    dve.wait_ge(m_done, t + (f0 + 1))
                    for half in range(2):
                        take(u + (2 + half), half, halves(b_buf, half), "plain")
                    dve.wait_ge(pj_free, u + 6)
                    dve.wait_ge(gelu_ok, t + (f0 + 1))
                    dve.tensor_tensor(b_buf, b_buf, c_buf, ALU.mult).then_inc(m_prod, 1)
                    dve.wait_ge(m_round, t + (f0 + 1))
                    dve.tensor_tensor(m_lo[:, t, :], b_buf, m_hi[:, t, :].bitcast(F32), ALU.subtract).then_inc(m_done, 1)
                last_chunk = c == len(FF_CHUNKS) - 1
                if last_chunk:
                    dve.wait_ge(m_done, FF_T + 1)
                    norm_begin(3)
                    dve.wait_ge(feed_dve[3], 1)
                with dve.Fori(0, NK) as k:
                    for half in range(2):
                        at = slice(half * HALF, (half + 1) * HALF)
                        take(k * 2 + (unit_of(W_FF_AT[c] + 2 * m) + half), half, xt[:, k, at], "add",
                             other=xt[:, k, at])
                    if last_chunk:
                        dve.wait_ge(feed_act[3], k + 1)
                        dve.tensor_tensor(acc[3], acc[3], sq[3], ALU.add).then_inc(feed_dve[3], 1)
                        dve.wait_ge(feed_dve[3], k + 2)
            norm_mean(3)

        @block.scalar
        def _(act):
            def aside(value):
                act.compute_val(value)
                act.wait_ge(const_in, 32)
                return value

            def fill_out(f, out, n=HALF, scale=None, source=None, moving=False):
                act.wait_ge(tb_full, aside(f + 1) if moving else f + 1)
                source = bank(TB, n) if source is None else source
                if scale is None:
                    act.activation(out, source, ACT.Copy).then_inc(tb_free, 1)
                else:
                    act.activation(out, source, ACT.Copy, scale=scale).then_inc(tb_free, 1)

            def rstd_out(i):
                act.wait_ge(nf_turn, i + 1)
                act.activation(rstd_bc[:, :], banks(SC, S), ACT.Copy).then_inc(nf_bc, 1)

            act.wait_ge(const_ok, 3)
            act.activation(spare[:, 2:3], zero_col, ACT.Copy).then_inc(tb_free, 1)

            act.wait_ge(lam_dots, 2)
            act.activation(lam_exp, lam_dot, ACT.Exp).then_inc(lam_exps, 1)

            act.wait_ge(const_in, 32)
            with act.Fori(0, NK // 2) as t:
                for s in range(2):
                    act.wait_ge(x0_turned, aside(t * 2 + (s + 1)))
                    act.activation(h_hi[:, t * 2 + s, :], banks(SC + 2 * s, S), ACT.Copy,
                                   scale=col[:, bass.ds(t * 2 + (C_MIX + s), 1)]).then_inc(feed_act[0], 1)
                    act.wait_ge(feed_dve[0], t * 4 + (2 * s + 1))
                    act.activation(sq[0], banks(SC + 2 * s, S), ACT.Square).then_inc(feed_act[0], 1)
            rstd_out(0)

            with act.Fori(0, DIL_H) as t:
                f = t * DIL_FILLS
                for g in range(GROUPS):
                    for part in range(2):
                        fill_out(f, dl_v[g][:, 4 * part:4 * part + 4, :])
                        f = f + 1
                act.wait_ge(pj_free, t * (2 * DIL_TILES) + (2 * DIL_TILES + 2))
                act.dma_start(z_dram[t], dl_gate).then_inc(gate_out, 16)
                for b in range(NB + 1):
                    n = dil_tiles((b - 1) % 2)
                    if b >= 1:
                        for k in range(fills(n)):
                            m = min(4, n - 4 * k)
                            fill_out(f, dl_pT[:, 4 * k:4 * k + m, :], m * P)
                            f = f + 1
                    if b < NB:
                        act.wait_ge(dl_neg, t * NB + (b + 1))
                        pb = dl_p[b % 2][:, 0:dil_tiles(b % 2) * P]
                        act.activation(pb, pb, ACT.Exp, bias=dl_nm[:, b:b + 1],
                                       accum_out=dl_den[:, b:b + 1]).then_inc(dl_exp, 1)
                    if b >= 1:
                        act.wait_ge(dl_rec, t * NB + b)
                        act.wait_ge(o_ready, t * NB + b)
                        act.activation(dl_st[:, b - 1, :], ps[:, OB, 0:P], ACT.Copy,
                                       scale=dl_rd[:, b - 1:b]).then_inc(o_free, 1)
                for part in range(2):
                    fill_out(f, by_residue(oT[:, t + DIFF_H, :])[:, 2 * part:2 * part + 2, :],
                             source=bank(TB).rearrange("p (r j) -> p r j", r=2), moving=True)
                    f = f + 1

            def df_values(f, par):
                for part in range(2):
                    fill_out(f, df_v[par][:, 4 * part:4 * part + 4, :])
                    f = f + 1
                return f

            def df_head(pair, par, f, project):
                h = pair * 2 + par
                for i in range(NB + 1):
                    if i < NB:
                        n = (i + 1) * P
                        act.wait_ge(df_neg, h * NB + (i + 1))
                        for m in range(2):
                            at = slice(2 * i + m, 2 * i + m + 1)
                            act.activation(df_p[m][:, 0:n], df_p[m][:, 0:n], ACT.Exp, bias=df_nm[:, at],
                                           accum_out=df_den[:, at]).then_inc(df_exp, 1)
                    if i >= 1:
                        j = i - 1
                        for k in range(fills(i)):
                            m = min(4, i - 4 * k)
                            fill_out(f, df_aT[:, 4 * k:4 * k + m, :], m * P)
                            f = f + 1
                        act.wait_ge(df_rec, h * NB + i)
                        act.wait_ge(o_ready, h * NB + (DIL_H * NB + i))
                        scale = df_rd[:, 2 * j:2 * j + 1]
                        act.activation(df_st[:, j, :], ps[:, OB, 0:P], ACT.Copy, scale=scale).then_inc(o_free, 1)
                        act.wait_ge(o_free, h * (2 * NB) + (DIL_H * NB + 2 * j + 1))
                        act.activation(df_sq, ps[:, OB, 0:P], ACT.Square, scale=scale,
                                       accum_out=df_ssq[:, j:j + 1]).then_inc(o_free, 1)
                if project:
                    f = df_values(f, 1 - par)
                for part in range(2):
                    fill_out(f, oT[:, h, part * HALF:(part + 1) * HALF], scale=sub_gain, moving=True)
                    f = f + 1
                return f

            act.wait_ge(lam_ok, 2)
            df_values(F_DIFF, 0)
            with act.Fori(0, DIFF_H // 2 - 1) as t:
                f = t * (2 * DIFF_FILLS) + (F_DIFF + 2)
                for par in range(2):
                    f = df_head(t, par, f, True)
            f = df_head(DIFF_H // 2 - 1, 0, F_DIFF + 2 + (DIFF_H - 2) * DIFF_FILLS, True)
            df_head(DIFF_H // 2 - 1, 1, f, False)

            def round_heads(heads):
                for k in heads:
                    act.activation(head_parts(k)[0], oT[:, k, :], ACT.Copy).then_inc(split_hi, 1)

            act.wait_ge(tb_free, F_MEM + 1)
            round_heads(range(DIFF_H, DIFF_H + DIL_H))
            with act.Fori(0, (W_BRANCH - W_GATE) // 2) as t:
                for s in range(2):
                    act.wait_ge(pj_free, t * 4 + (unit_of(W_GATE) + 2 * s + 4))
                    act.dma_start(z_dram[t * 2 + (DIL_H + s)], gate_st[s]).then_inc(gate_out, 16)
            round_heads(range(DIFF_H))
            act.wait_ge(gate_out, 16 * 2 * NK)

            with act.Fori(0, NK) as t:
                for i in range(2):
                    act.dma_start(zb[i], z_dram[t + i * NK]).then_inc(z_in, 16)
                act.wait_ge(z_in, aside(t * 32 + 32))
                for i in range(2):
                    act.activation(zb[i], zb[i], ACT.Sigmoid,
                                   bias=col[:, bass.ds(t + (C_GATE + i * NK), 1)]).then_inc(z_sig, 1)
                act.wait_ge(y_sum, aside(t + 1))
                act.activation(y_hi[:, t, :], yd, ACT.Copy).then_inc(y_round, 1)

            def feed(i, k, gain):
                act.activation(h_hi[:, k, :], xt[:, k, :], ACT.Copy, scale=gain).then_inc(feed_act[i], 1)
                act.wait_ge(feed_dve[i], aside(k * 2 + 1))
                act.activation(sq[i], xt[:, k, :], ACT.Square).then_inc(feed_act[i], 1)

            def residual(i, first, gains, source):
                for s in range(2):
                    act.dma_start(x_slot(i, s), source(s)).then_inc(back_in[i][s], 16)

                def step(t, more):
                    for s in range(2):
                        act.wait_ge(pj_free, t * 4 + (unit_of(first) + 2 * s + 4))
                        if more:
                            act.dma_start(x_slot(i, s), source(t * 2 + (s + 2))).then_inc(back_in[i][s], 16)
                        if i == 0:
                            act.dma_start(x_spill[t * 2 + s], xt[:, t * 2 + s, :]).then_inc(x_spilled, 16)
                        feed(i + 1, t * 2 + s, col[:, bass.ds(t * 2 + (gains + s), 1)])

                with act.Fori(0, NK // 2 - 1) as t:
                    step(t, True)
                step(NK // 2 - 1, False)

            def x_slot(i, s):
                return x_back[i][s].rearrange("p (b d) -> p b d", b=NB) if i == 0 else x_back[i][s]

            act.wait_ge(y_done, NK + 1)
            residual(0, W_OUT, C_CROSS, lambda k: x_cols[k])

            act.dma_start(mem_x, mem_rows).then_inc(mem_in, 16)
            act.wait_ge(mem_in, 16)
            for j in range(2):
                if j:
                    act.wait_ge(mem_sums, 1)
                act.activation(mem_sq, mem_x[:, j, :], ACT.Square, accum_out=mem_ssq[:, j:j + 1]).then_inc(mem_sums, 1)
            for k in range(NK):
                act.wait_ge(mem_turn, k // 2 + 1)
                act.activation(mn_hi[:, k, :], ps[:, SC + k // 2, (k % 2) * MEM:(k % 2 + 1) * MEM], ACT.Copy,
                               scale=col[:, C_MEM + k:C_MEM + k + 1]).then_inc(mem_hi, 1)
            rstd_out(1)
            with act.Fori(0, NK // 2) as t:
                for s in range(2):
                    fill_out(t * 2 + (F_MEM + s), mv[:, :, bass.ds(t * MEM + s * P, P)],
                             source=bank(TB, MEM).rearrange("p (j e) -> p j e", j=2), moving=True)

            act.wait_ge(pj_free, U_CQ + 2)
            with act.Fori(0, X_H) as t:
                act.activation(mkh, mk[:, bass.ds(t * 2, 2), :], ACT.Copy).then_inc(x_head, 1)
                act.activation(mvh, mv[:, :, bass.ds(t * MEM, MEM)], ACT.Copy).then_inc(x_head, 1)
                for g in range(2):
                    act.wait_ge(x_neg, t * 2 + (g + 1))
                    for b in range(4):
                        at = slice(4 * g + b, 4 * g + b + 1)
                        act.activation(px[g][:, b, :], ps[:, SC + 2 * g + b // 2, (b % 2) * MEM:(b % 2 + 1) * MEM],
                                       ACT.Exp, bias=x_nm[:, at], accum_out=x_den[:, at]).then_inc(x_exp, 1)
                for g in range(2):
                    for j in range(2):
                        fill_out(t * 4 + (F_CROSS + 2 * g + j), pxT[:, j, :])
                    for e in range(2):
                        act.wait_ge(x_av, aside(t * 4 + (2 * g + e + 1)))
                        act.activation(co_hi[:, t * 2 + e, g * HALF:(g + 1) * HALF], bank(OB),
                                       ACT.Copy).then_inc(x_hi, 1)

            act.wait_ge(x_lo, 4 * X_H)
            residual(1, W_CO, C_FFN, lambda k: x_spill[k])
            rstd_out(2)

            for c, (f0, m) in enumerate(FF_CHUNKS):
                with act.Fori(0, m) as t:
                    act.wait_ge(pj_free, t * 4 + (unit_of(W_FF_AT[c]) + 4))
                    act.wait_ge(m_prod, aside(t + (f0 + 1)))
                    act.activation(c_buf, a_pad[:, 0:S], ACT.Identity, scale=col[:, bass.ds(t + (C_CONVW + f0), 1)],
                                   bias=col[:, bass.ds(t + (C_CONVB + f0), 1)]).then_inc(conv0, 1)
                    act.wait_ge(conv2, t + (f0 + 2))
                    act.activation(c_buf, c_buf, ACT.Gelu).then_inc(gelu_ok, 1)
                    act.wait_ge(m_prod, aside(t + (f0 + 2)))
                    act.activation(m_hi[:, t, :], b_buf, ACT.Copy).then_inc(m_round, 1)
            with act.Fori(0, NK) as k:
                act.wait_ge(pj_free, k * 2 + (unit_of(W_TOTAL - NK) + 4))
                act.wait_ge(feed_dve[3], aside(k + 1))
                act.activation(sq[3], xt[:, k, :], ACT.Square).then_inc(feed_act[3], 1)
                act.wait_ge(feed_act[3], aside(k + 1))
                act.activation(xt[:, k, :], xt[:, k, :], ACT.Copy,
                               scale=col[:, bass.ds(k + C_FINAL, 1)]).then_inc(fin_scaled, 1)

            act.wait_ge(nf_rstd, 4)
            for r in range(2 * NB):
                act.wait_ge(fin_turn, r + 1)
                act.activation(o_rows[:, r, :], bank(SC + r % 4), ACT.Copy,
                               scale=rstd_tok[:, r // 2:r // 2 + 1]).then_inc(fin_row, 1)


def tiles_of(w, cols):
    kt = w.shape[0] // P
    t = w.reshape(kt, P, -1, P).transpose(2, 1, 0, 3)[cols]
    if kt < NK:
        t = np.concatenate([t, np.zeros((t.shape[0], P, NK - kt, P), t.dtype)], axis=2)
    return t


def weight_stream(a):
    w_in, w_up, w_down, w_ckv = (a[n][0] for n in ("w_in", "w_up", "w_down", "w_ckv"))
    dil0, gate0 = 3 * DIFF_H, 3 * DIFF_H + 3 * GROUPS * DIL_H
    order = []
    for s in range(DIL_H):
        for g in range(GROUPS):
            order += [dil0 + kind * GROUPS * DIL_H + g * DIL_H + s for kind in range(3)]
        order.append(gate0 + s)
    for h in range(DIFF_H):
        order += [kind * DIFF_H + h for kind in range(3)]
    order += range(gate0 + DIL_H, gate0 + 2 * NK)
    parts = [tiles_of(w_in, order)]
    both = [tiles_of(a[n][0], slice(None)) for n in ("w_branch_diff", "w_branch_dil")]
    parts.append(np.stack(both, axis=1).reshape(2 * NK, P, NK, P))
    parts += [tiles_of(a["w_out"][0], slice(None)), tiles_of(w_ckv, slice(None)),
              tiles_of(a["w_cq"][0], slice(None)), tiles_of(a["w_co"][0], slice(None))]
    for f0, m in FF_CHUNKS:
        parts.append(tiles_of(w_up, [f for i in range(f0, f0 + m) for f in (i, FF_T + i)]))
        parts.append(tiles_of(w_down[f0 * P:(f0 + m) * P], slice(None)))
    return np.ascontiguousarray(np.concatenate(parts))


def alibi_tables():
    p = np.arange(P)[:, None]
    dist = p + S - P - np.arange(S)[None]
    diff = np.where(dist >= 0, -dist, NEG)
    dist = 4 * p + 131 - np.arange(NEAR_W + 1)[None]
    near = np.where((dist >= 0) & (dist <= 128), -dist, NEG)
    far = []
    for jb in range(2):
        step = p + P * jb - np.arange(P * (jb + 1))[None]
        far.append(np.where((step >= 0) & (step <= 128), -step, NEG))
        far.append(np.where((step >= 0) & (step % 4 == 0), -(step / 4), NEG))
    return diff.astype(np.float32), np.concatenate([near] + far, axis=1).astype(np.float32)


def column_table(a):
    def cols(v):
        return v.reshape(-1, P).T

    parts = [cols(a[n][0]) for n in ("mix_norm_g", "cross_norm_g", "mem_norm_g", "ffn_norm_g")]
    parts += [cols(a["final_norm_g"]), cols(a["b_gate"][0]), cols(a["conv_w"][0].reshape(-1)), cols(a["conv_b"][0]),
              cols(a["diff_subln_g"][0])]
    lam = np.concatenate([a[n][0] for n in ("lam_q1", "lam_k1", "lam_q2", "lam_k2")])
    parts.append(np.broadcast_to(lam[None], (P, 256)))
    return np.ascontiguousarray(np.concatenate(parts, axis=1))


def kernel(**inputs):
    import concourse.bacc as bacc
    from concourse.bass_utils import run_bass_kernel_spmd

    a = {k: np.asarray(v) for k, v in inputs.items()}
    diff, dil = alibi_tables()
    arrays = {
        "x_in": np.ascontiguousarray(a["x"][0]),
        "mem_in": np.ascontiguousarray(a["mem"][0]),
        "w_stream": weight_stream(a),
        "columns": column_table(a),
        "ident": np.eye(P, dtype=np.float32),
        "alibi_diff": diff,
        "alibi_dil": dil,
    }
    nc = bacc.Bacc("TRN2", target_bir_lowering=False, num_devices=1)
    args = [nc.dram_tensor(f"{n}_dram", v.shape, mybir.dt.from_np(v.dtype), kind="ExternalInput").ap()
            for n, v in arrays.items()]
    args.append(nc.dram_tensor("result_dram", (S, D), F32, kind="ExternalOutput").ap())
    trunk_layer(nc, *args)
    r = run_bass_kernel_spmd(nc, [{f"{n}_dram": v for n, v in arrays.items()}], core_ids=[0])
    return r.results[0]["result_dram"].reshape(1, S, D)
```

```python
import math
from contextlib import ExitStack

import numpy as np

import concourse.bass as bass
from concourse import mybir

ALU = mybir.AluOpType
ACT = mybir.ActivationFunctionType
AX_X = mybir.AxisListType.X
F32 = mybir.dt.float32
F32R = mybir.dt.float32r

P = 128
D = 1024
S = 1024
MEM = 256
EPS = 1e-5
NK = D // P
NB = S // P
HALF = 512
DIFF_H = 8
DIL_H = 4
GROUPS = 3
X_H = 4
FF = 2816
FF_T = FF // P
CHUNK = 8
LAM_INIT = 0.8 - 0.6 * math.exp(-0.3 * 0)
DIFF_SCALE = 64 ** -0.5
DIL_SCALE = 128 ** -0.5
X_SCALE = 256 ** -0.5
NEG = -1e30

DIL_GATES = 3
LAST_GATES = 2 * NK - DIL_H * DIL_GATES
QKV = 3 * GROUPS
DIL_TILES = QKV + DIL_GATES
W_DIL = 0
W_DIFF = W_DIL + DIL_H * DIL_TILES
W_GATE = W_DIFF + 3 * DIFF_H
W_BRANCH = W_GATE + LAST_GATES
W_OUT = W_BRANCH + 2 * NK
W_MEM = W_OUT + NK
W_CQ = W_MEM + 2 * NK
W_CO = W_CQ + NK
W_FF = W_CO + NK
FF_CHUNKS = [(f, min(CHUNK, FF_T - f)) for f in range(0, FF_T, CHUNK)]
W_FF_AT = [W_FF + sum(2 * m + NK for _, m in FF_CHUNKS[:c]) for c in range(len(FF_CHUNKS))]
W_TOTAL = W_FF + sum(2 * m + NK for _, m in FF_CHUNKS)

U_MEM = 2 * W_MEM
U_CQ = U_MEM + 2 * NK


def unit_of(tile):
    if tile < W_MEM:
        return 2 * tile
    return U_MEM + tile - W_MEM if tile < W_CQ else U_CQ + 2 * (tile - W_CQ)


def dil_tiles(jb):
    return (4 if jb == 0 else 5) + 2 * (jb + 1)


def fills(n):
    return -(-n // 4)


DIL_USES = 2 * GROUPS + sum(fills(dil_tiles(b % 2)) + 1 for b in range(NB)) + 2
DIFF_USES = 2 + sum(fills(i + 1) + 1 for i in range(NB)) + 2
F_DIL = 0
F_DIFF = F_DIL + DIL_H * DIL_USES
DF_LAST = sum(fills(i + 1) + 1 for i in range(NB)) - 1
F_MEM = F_DIFF + DIFF_H * DIFF_USES
F_CROSS = F_MEM + NK

UNDER_DIL = [(4, 0), (3, 2), (3, 2), (3, 2), (3, 2), (3, 2), (3, 2), (3, 2), (3, 3)]
UNDER_DIFF = [(4, 0), (3, 3), (3, 3), (3, 2), (2, 2), (2, 2), (2, 2), (2, 2), (2, 3)]


def done_by(under, block, part):
    return sum(a + b for a, b in under[:block]) + sum(under[block][:part + 1])


C_MIX, C_CROSS, C_MEM, C_FFN, C_FINAL = (NK * i for i in range(5))
C_GATE = 5 * NK
C_CONVW = C_GATE + 2 * NK
C_CONVB = C_CONVW + 3 * FF_T
C_SUB = C_CONVB + FF_T
C_LAM = C_SUB + 1
C_ALL = C_LAM + 4 * 64

NEAR_W = 640 + 3
DIL_BIAS_W = NEAR_W + 1 + 256 + 512
REGION = 28928


def trunk_layer(nc, x, mem, w_stream, columns, ident, alibi_diff, alibi_dil, out):
    z_dram = nc.dram_tensor("gate_spill", [2 * NK, P, S], F32, kind="Internal").ap()
    x_spill = nc.dram_tensor("x_spill", [NK, P, S], F32, kind="Internal").ap()
    mem_rows = mem.rearrange("(j p) d -> p j d", p=P)
    x_cols = x.rearrange("(b p) (k d) -> k p b d", p=P, d=P)
    out_rows = out.rearrange("(b p) d -> b p d", p=P)

    with ExitStack() as ctx:
        def sb(name, shape, dt=F32, scope=ctx):
            return scope.enter_context(nc.sbuf_tensor(name, shape, dt))

        def sem(name):
            return ctx.enter_context(nc.semaphore(name))

        ps = ctx.enter_context(nc.psum_tensor("ps", [P, 8, HALF], F32))
        PJ = 0
        SC = 2
        TB = 6
        NS = 5

        h_hi = sb("h_hi", [P, NK, S], F32R)
        h_lo = sb("h_lo", [P, NK, S], F32R)
        w_raw = sb("w_raw", [P, 2, NK, P])
        w_hi = sb("w_hi", [P, 2, NK, P], F32R)
        w_lo = sb("w_lo", [P, 2, NK, P], F32R)
        rstd_bc = sb("rstd_bc", [P, S])
        idn = sb("idn", [P, P])
        col = sb("col", [P, C_ALL])
        lam_tmp = sb("lam_tmp", [P, 2, 64])
        small = sb("small", [P, 64])
        ones = small[:, 0:1]
        neg_half = small[:, 8:16]
        neglam = small[:, 16:17]
        sub_gain = small[:, 17:18]
        lam_dot = small[:, 20:22]
        lam_exp = small[:, 22:24]
        msq = small[:, 24:32]
        rstd_tok = small[:, 32:40]
        mem_ssq = small[:, 40:42]
        mem_msq = small[:, 42:44]
        mem_rstd = small[:, 44:46]
        spare = small[:, 56:63]
        gate_spare = small[:, 48:50]
        zero_col = small[:, 52:53]

        def phase(*parts):
            with ExitStack() as scope:
                return [sb(p[0] or f"gap{nc.next_id()}", [P, p[1]], p[2] if len(p) > 2 else F32, scope)
                        for p in parts]

        def tiles(t, n):
            return t[:, :].rearrange("p (k s) -> p k s", k=n)

        LOW, OT, HIGH = 8 * S, (DIFF_H + DIL_H) * S, REGION - 20 * S
        TOP = REGION - 24 * S
        low, oT_, high = phase(("attn_low", LOW), ("oT", OT), ("attn_high", HIGH))
        oT = tiles(oT_, DIFF_H + DIL_H)
        od_hi, od_lo, y_hi, y_lo, top = phase(
            ("od_hi", 4 * S, F32R), ("od_lo", 4 * S, F32R), ("y_hi", 8 * S, F32R), ("y_lo", 8 * S, F32R), ("top", TOP))
        od_hi, od_lo, y_hi, y_lo = tiles(od_hi, DIL_H), tiles(od_lo, DIL_H), tiles(y_hi, NK), tiles(y_lo, NK)
        xt = tiles(phase(("xt", LOW))[0], NK)
        _, mn_hi, mn_lo, mem_x, _, = phase(
            (None, LOW), ("mn_hi", 2 * S, F32R), ("mn_lo", 2 * S, F32R), ("mem_x", 4 * S), (None, S))
        mn_hi, mn_lo = tiles(mn_hi, NK), tiles(mn_lo, NK)
        mem_x, mem_sq = mem_x[:, 0:2 * S].rearrange("p (j d) -> p j d", j=2), mem_x[:, 2 * S:3 * S]
        x_low, co_hi, co_lo, x_top = phase(
            ("x_low", LOW), ("co_hi", 8 * S, F32R), ("co_lo", 8 * S, F32R), ("x_top", TOP))
        co_hi, co_lo = tiles(co_hi, NK), tiles(co_lo, NK)
        _, m_hi, m_lo, ff = phase(
            (None, LOW), ("m_hi", 8 * S, F32R), ("m_lo", 8 * S, F32R), ("ff", TOP))
        m_hi, m_lo = tiles(m_hi, CHUNK), tiles(m_lo, CHUNK)
        o_rows = tiles(phase((None, LOW), ("o_rows", 8 * S))[1], 2 * NB)

        def view(t, at, n):
            return t[:, at:at + n]

        dl_q = [view(low, g * S, S) for g in range(3)]
        dl_k = [view(low, (3 + g) * S, S) for g in range(3)]
        dl_vT = view(low, 6 * S, S)
        dl_st = dl_vT.rearrange("p (b e) -> p b e", b=NB)
        dl_gate = view(low, 7 * S, S)
        df_gate = view(high, 6 * S, S)
        dl_v = [view(high, g * S, S).rearrange("p (b e) -> p b e", b=NB) for g in range(3)]
        dl_p = [view(high, 3 * S + 1152 * i, 1152) for i in range(2)]
        dl_pT = view(high, 3 * S + 2304, 1152).rearrange("p (b q) -> p b q", b=9)
        dl_bias = view(high, 3 * S + 3456, DIL_BIAS_W)
        dl_near = dl_bias[:, 0:NEAR_W]
        dl_far = [dl_bias[:, NEAR_W + 1:NEAR_W + 257], dl_bias[:, NEAR_W + 257:NEAR_W + 769]]
        stat = view(high, 3 * S + 3456 + DIL_BIAS_W, 160)
        dl_mx, dl_nm, dl_den, dl_rd = stat[:, 0:16], stat[:, 16:24], stat[:, 24:32], stat[:, 32:40]
        df_q = [view(low, i * S, S) for i in range(2)]
        df_k = [view(low, (2 + i) * S, S) for i in range(2)]
        df_v = [view(low, (4 + i) * S, S).rearrange("p (b e) -> p b e", b=NB) for i in range(2)]
        df_p = [view(low, (6 + i) * S, S) for i in range(2)]
        df_vT = view(high, 0, S)
        df_a = view(high, S, S)
        df_aT = view(high, 2 * S, S).rearrange("p (b q) -> p b q", b=NB)
        df_bias = view(high, 3 * S, S)
        df_st = view(high, 4 * S, S).rearrange("p (b e) -> p b e", b=NB)
        df_sq = view(high, 5 * S, P)
        df_mx, df_nm, df_den, df_rd = (stat[:, 40 + 16 * i:56 + 16 * i] for i in range(4))
        df_cc, df_ssq, df_ms, df_rs = (stat[:, 104 + 8 * i:112 + 8 * i] for i in range(4))
        x0 = [view(low, i * S, S).rearrange("p (b d) -> p b d", b=NB) for i in range(2)]
        sq = [view(low, 2 * S, S), view(top, 2 * S, S), view(x_top, 2 * S, S), view(ff, S + 8, S)]
        acc = [view(low, 3 * S, S), view(top, 3 * S, S), view(x_top, 3 * S, S), view(ff, 2 * S + 8, S)]
        def head_parts(k):
            return (h_hi[:, k, :], h_lo[:, k, :]) if k < DIFF_H else (od_hi[:, k - DIFF_H, :], od_lo[:, k - DIFF_H, :])

        zb = [view(top, i * S, S) for i in range(2)]
        yd, yl = view(top, 2 * S, S), view(top, 3 * S, S)
        x_back = [[view(t, i * S, S) for i in range(2)] for t in (top, x_top)]
        mk = view(x_low, 0, 2 * S).rearrange("p (t m) -> p t m", t=NK)
        mv = view(x_low, 2 * S, 2 * S).rearrange("p (j e) -> p j e", j=2)
        qx = view(x_low, 4 * S, 2 * S).rearrange("p (j s) -> p j s", j=2)
        px = [view(x_low, (6 + i) * S, S).rearrange("p (b m) -> p b m", b=4) for i in range(2)]
        pxT = view(x_top, 0, S).rearrange("p (j q) -> p j q", j=2)
        mkh = view(x_top, S, HALF).rearrange("p (j m) -> p j m", j=2)
        mvh = view(x_top, S + HALF, HALF).rearrange("p (j e) -> p j e", j=2)
        mv_t = [view(x_top, 2 * S + i * MEM, MEM) for i in range(2)]
        x_st = view(x_top, 4 * S, 40)
        x_mx, x_nm, x_den, x_rd = (x_st[:, 8 * i:8 * i + 8] for i in range(4))
        a_pad = view(ff, 0, S + 2)
        c_buf = view(ff, S + 8, S)
        b_buf = view(ff, 2 * S + 8, S)

        const_in = sem("const_in")
        const_ok = sem("const_ok")
        lam_dots, lam_exps, lam_ok = sem("lam_dots"), sem("lam_exps"), sem("lam_ok")
        w_in = [sem("w_in0"), sem("w_in1")]
        w_rounded, w_ready = sem("w_rounded"), sem("w_ready")
        pj_ready, pj_free = sem("pj_ready"), sem("pj_free")
        tb_full, tb_free = sem("tb_full"), sem("tb_free")
        x0_in = [sem("x0_in0"), sem("x0_in1")]
        x0_turned, x0_free = sem("x0_turned"), sem("x0_free")
        back_in = [[sem(f"back{i}_in{s}") for s in range(2)] for i in range(2)]
        feed_act = [sem(f"feed_act{i}") for i in range(4)]
        feed_dve = [sem(f"feed_dve{i}") for i in range(4)]
        nf_sum, nf_ms, nf_rstd = sem("nf_sum"), sem("nf_ms"), sem("nf_rstd")
        nf_turn, nf_bc = sem("nf_turn"), sem("nf_bc")
        bias_in = sem("bias_in")
        dl_s, dl_max, dl_neg, dl_exp = sem("dl_s"), sem("dl_max"), sem("dl_neg"), sem("dl_exp")
        dl_rec, dl_slope = sem("dl_rec"), sem("dl_slope")
        gate_out = [sem("gate_out0"), sem("gate_out1")]
        df_s, df_max, df_neg, df_exp = sem("df_s"), sem("df_max"), sem("df_neg"), sem("df_exp")
        df_rec, df_coef, df_comb, df_slope = sem("df_rec"), sem("df_coef"), sem("df_comb"), sem("df_slope")
        df_mean, df_pow, df_norm = sem("df_mean"), sem("df_pow"), sem("df_norm")
        split_hi, split_lo = sem("split_hi"), sem("split_lo")
        z_in, z_sig, y_sum, y_round, y_done = sem("z_in"), sem("z_sig"), sem("y_sum"), sem("y_round"), sem("y_done")
        x_spilled = sem("x_spilled")
        mem_in, mem_sums, mem_mean, mem_pow = sem("mem_in"), sem("mem_sums"), sem("mem_mean"), sem("mem_pow")
        mem_norm, mem_turn, mem_hi, mem_lo = sem("mem_norm"), sem("mem_turn"), sem("mem_hi"), sem("mem_lo")
        x_head, x_s, x_max, x_neg, x_exp = sem("x_head"), sem("x_s"), sem("x_max"), sem("x_neg"), sem("x_exp")
        x_rec, x_norm, x_lo = sem("x_rec"), sem("x_norm"), sem("x_lo")
        conv0, conv1, conv2, gelu_ok = sem("conv0"), sem("conv1"), sem("conv2"), sem("gelu_ok")
        m_prod, m_round, m_done = sem("m_prod"), sem("m_round"), sem("m_done")
        fin_scaled, fin_turn, fin_row, fin_out = sem("fin_scaled"), sem("fin_turn"), sem("fin_row"), sem("fin_out")


        block = ctx.enter_context(nc.Block())

        def bank(b, n=HALF):
            return ps[:, b, 0:n]

        def banks(b, n):
            return ps[:, b:b + -(-n // HALF), :].rearrange("p b n -> p (b n)")[:, 0:n]

        def by_residue(ap):
            return ap.rearrange("p (j r) -> p r j", r=4)

        def half_by_residue(ap, half):
            return ap.rearrange("p (r j) -> p r j", r=4)[:, :, half * P:(half + 1) * P]

        @block.sync
        def _(sp):
            sp.dma_start(x0[0], x_cols[0]).then_inc(x0_in[0], 16)
            sp.dma_start(idn[:, :], ident).then_inc(const_in, 16)
            sp.dma_start(x0[1], x_cols[1]).then_inc(x0_in[1], 16)
            sp.dma_start(col[:, :], columns).then_inc(const_in, 16)
            with sp.Fori(1, NK // 2) as t:
                for s in range(2):
                    sp.wait_ge(x0_turned, t * 2 + (s - 1))
                    sp.dma_start(x0[s], x_cols[t * 2 + s]).then_inc(x0_in[s], 16)
            for n in range(2):
                sp.dma_start(w_raw[:, n], w_stream[n]).then_inc(w_in[n], 16)
            sp.dma_start(dl_bias, alibi_dil).then_inc(bias_in, 16)

            def load_weights(first, last):
                with sp.Fori(first // 2, last // 2) as t:
                    for s in range(2):
                        sp.wait_ge(w_ready, t * 2 + (s - 1))
                        sp.dma_start(w_raw[:, s], w_stream[t * 2 + s]).then_inc(w_in[s], 16)

            load_weights(2, W_DIFF)
            sp.wait_ge(tb_free, F_DIFF + 2)
            sp.dma_start(df_bias, alibi_diff).then_inc(bias_in, 16)
            load_weights(W_DIFF, W_TOTAL)
            for r in range(2 * NB):
                sp.wait_ge(fin_row, r + 1)
                sp.dma_start(out_rows[r // 2, :, (r % 2) * HALF:(r % 2 + 1) * HALF],
                             o_rows[:, r, :]).then_inc(fin_out, 16)
            sp.wait_ge(fin_out, 16 * 2 * NB)
            for half in range(2):
                sp.wait_ge(gate_out[half], 16 * 2 * NK + 16)
            sp.wait_ge(x_spilled, 16 * NK)

        @block.gpsimd
        def _(pool):
            def aside(value):
                pool.compute_val(value)
                pool.wait_ge(const_ok, 3)
                return value

            def split_tile(n, s, used):
                pool.wait_ge(w_in[s], (n - s) * 8 + 16)
                if used is not None:
                    pool.wait_ge(pj_ready, aside(used))
                pool.tensor_scalar(w_hi[:, s], w_raw[:, s], 1.0, 1.0, ALU.mult, ALU.mult).then_inc(w_rounded, 1)
                pool.wait_ge(w_rounded, n + 1)
                pool.tensor_tensor(w_lo[:, s], w_raw[:, s], w_hi[:, s].bitcast(F32),
                                   ALU.subtract).then_inc(w_ready, 1)

            def split_tiles(first, last):
                each = 1 if first >= W_MEM + 2 and last <= W_CQ + 2 else 2
                base = unit_of(first - 2) + each
                with pool.Fori(0, (last - first) // 2) as t:
                    for s in range(2):
                        split_tile(t * 2 + (first + s), s, t * (2 * each) + (base + s * each))

            def split_now(n):
                split_tile(n, n % 2, unit_of(n - 2) + (1 if W_MEM <= n - 2 < W_CQ else 2) if n >= 2 else None)

            def norm_root(i):
                pool.wait_ge(nf_ms, i + 1)
                pool.tensor_tensor(rstd_tok, msq, neg_half, ALU.pow).then_inc(nf_rstd, 1)

            def head_root(h):
                pool.wait_ge(tb_free, aside(h * DIFF_USES + (F_DIFF + 2 + DF_LAST + 3)))
                pool.tensor_scalar(df_ms, df_ssq, 1.0 / P, EPS, ALU.mult, ALU.add).then_inc(df_mean, 1)
                pool.wait_ge(df_mean, h + 1)
                pool.tensor_tensor(df_rs, df_ms, neg_half, ALU.pow).then_inc(df_pow, 1)

            pool.memset(ones, 1.0).then_inc(const_ok, 1)
            pool.memset(neg_half, -0.5).then_inc(const_ok, 1)
            pool.memset(zero_col, 0.0).then_inc(const_ok, 1)
            pool.wait_ge(const_ok, 3)
            split_now(0)
            split_now(1)
            norm_root(0)
            split_tiles(2, W_DIFF)
            for n in range(W_DIFF, W_DIFF + 4):
                split_now(n)
            with pool.Fori(0, DIFF_H // 2 - 1) as t:
                for par in range(2):
                    for j in range(3):
                        n = W_DIFF + 4 + 3 * par + j
                        split_tile(t * 6 + n, n % 2, t * 12 + unit_of(n - 1))
                    head_root(t * 2 + par)
            for n in range(W_GATE - 2, W_GATE + 1):
                split_now(n)
            head_root(DIFF_H - 2)
            for n in range(W_GATE + 1, W_BRANCH):
                split_now(n)
            head_root(DIFF_H - 1)
            for n in range(W_BRANCH, W_BRANCH + 2):
                split_now(n)
            split_tiles(W_BRANCH + 2, W_MEM)
            for n in range(W_MEM, W_MEM + 2):
                split_now(n)
            norm_root(1)
            pool.wait_ge(mem_sums, 2)
            pool.tensor_scalar(mem_msq, mem_ssq, 1.0 / D, EPS, ALU.mult, ALU.add).then_inc(mem_mean, 1)
            pool.wait_ge(mem_mean, 1)
            pool.tensor_tensor(mem_rstd, mem_msq, neg_half[:, 0:2], ALU.pow).then_inc(mem_pow, 1)
            split_tiles(W_MEM + 2, W_CQ + 2)
            split_tiles(W_CQ + 2, W_FF)
            for n in range(W_FF, W_FF + 2):
                split_now(n)
            norm_root(2)
            split_tiles(W_FF + 2, W_TOTAL)
            norm_root(3)

        @block.tensor
        def _(pe):
            def product(n, s, half, u, hi=h_hi, lo=h_lo, kt=NK, cols=HALF, add_x=None, x_in=None, steps=None,
                        before=None):
                steps = range(kt) if steps is None else steps
                if half == 0 and steps[0] == 0:
                    pe.wait_ge(w_ready, n + 1)
                if steps[0] == 0:
                    pe.wait_ge(pj_free, u + 1)
                b = half if cols == HALF else s
                at = slice(half * cols, half * cols + cols)
                for k in steps:
                    if before is not None:
                        before(k)
                    pe.matmul(bank(b, cols), w_hi[:, s, k, :], hi[:, k, at], start=(k == 0), stop=False)
                    pe.matmul(bank(b, cols), w_hi[:, s, k, :], lo[:, k, at], start=False, stop=False)
                    last = pe.matmul(bank(b, cols), w_lo[:, s, k, :], hi[:, k, at], start=False,
                                     stop=(k == kt - 1 and add_x is None))
                if add_x is not None:
                    pe.wait_ge(back_in[0][s], x_in)
                    for j in range(4):
                        last = pe.matmul(ps[:, b, j * P:(j + 1) * P], add_x[:, 4 * half + j, :], idn[:, :],
                                         start=False, stop=(j == 3))
                if steps[-1] == kt - 1:
                    last.then_inc(pj_ready, 1)

            def products(first, tiles_n, **kw):
                with pe.Fori(0, tiles_n // 2) as t:
                    for s in range(2):
                        for half in range(2):
                            product(t * 2 + (first + s), s, half, t * 4 + (unit_of(first) + 2 * s + half), **kw)

            def turn(f, use, sources):
                pe.wait_ge(tb_free, f + (use + 1))
                for j, source in enumerate(sources):
                    last = pe.transpose(ps[:, TB + use % 2, j * P:(j + 1) * P], source, idn[:, :])
                last.then_inc(tb_full, 1)

            def turn_blocks(f, use, buf):
                for part in range(2):
                    turn(f, use + part, [buf[:, 4 * part + i, :] for i in range(4)])

            def norm_sum(i):
                pe.wait_ge(feed_dve[i], (NK if i == 3 else 2 * NK) + 1)
                for b in range(NB):
                    last = pe.matmul(ps[:, NS, b:b + 1], acc[i][:, b * P:(b + 1) * P], ones, start=True, stop=True)
                last.then_inc(nf_sum, 1)

            def norm_spread(i):
                pe.wait_ge(nf_rstd, i + 1)
                for b in range(NB):
                    last = pe.transpose(ps[:, SC + b // 4, (b % 4) * P:(b % 4 + 1) * P],
                                        rstd_tok[:, b:b + 1].to_broadcast([P, P]), idn[:, :])
                last.then_inc(nf_turn, 1)

            pe.wait_ge(const_in, 32)
            pe.wait_ge(const_ok, 3)
            with pe.Fori(0, NK // 2) as t:
                for s in range(2):
                    pe.wait_ge(x0_in[s], t * 16 + 16)
                    pe.wait_ge(x0_free, t * 2 + (s + 1))
                    for b in range(NB):
                        last = pe.transpose(ps[:, SC + 2 * s + b // 4, (b % 4) * P:(b % 4 + 1) * P],
                                            x0[s][:, b, :], idn[:, :])
                    last.then_inc(x0_turned, 1)
            norm_sum(0)
            norm_spread(0)

            def dil_scores(b):
                rho, jb = b // 2, b % 2
                sc = banks(SC, 1152)
                near0, near = (0, 512) if jb == 0 else (384, 640)
                at = 0
                for g, k0, n in ((0, near0, near), (1, rho * 256, (jb + 1) * P), (2, rho * 256, (jb + 1) * P)):
                    while n:
                        m = min(n, HALF - at % HALF)
                        last = pe.matmul(sc[:, at:at + m], dl_q[g][:, b * P:(b + 1) * P], dl_k[g][:, k0:k0 + m],
                                         start=True, stop=True)
                        at, k0, n = at + m, k0 + m, n - m
                last.then_inc(dl_s, 1)

            def dil_values(b):
                rho, jb = b // 2, b % 2
                return ([dl_v[0][:, i, :] for i in (range(4) if jb == 0 else range(3, 8))]
                        + [dl_v[g][:, 2 * rho + j, :] for g in (1, 2) for j in range(jb + 1)])

            with pe.Fori(0, DIL_H) as t:
                f = t * DIL_USES
                u = t * (2 * DIL_TILES)
                for j in range(QKV):
                    for half in range(2):
                        product(t * DIL_TILES + j, j % 2, half, u + (2 * j + half))
                        if half == 0 and j in (3, 6):
                            pe.wait_ge(pj_free, u + (2 * j + 2))
                            turn_blocks(f, 2 * (j // 3 - 1), dl_vT.rearrange("p (b e) -> p b e", b=NB))
                gates = [(QKV + j, half, k) for j in range(DIL_GATES) for half in range(2) for k in range(NK)]

                def gate_steps(count):
                    for _ in range(count):
                        j, half, k = gates.pop(0)
                        product(t * DIL_TILES + j, j % 2, half, u + (2 * j + half), steps=(k,))

                use = 2 * GROUPS
                for b in range(NB + 1):
                    if b < NB:
                        if b >= 1:
                            pe.wait_ge(dl_max, t * (2 * NB) + 2 * b)
                        dil_scores(b)
                    gate_steps(UNDER_DIL[b][0])
                    if b == 0:
                        pe.wait_ge(pj_free, u + (2 * QKV + 2))
                        turn_blocks(f, use - 2, dl_vT.rearrange("p (b e) -> p b e", b=NB))
                    if b >= 1:
                        n = dil_tiles((b - 1) % 2)
                        pe.wait_ge(dl_exp, t * NB + b)
                        for k in range(fills(n)):
                            turn(f, use, [dl_p[(b - 1) % 2][:, i * P:(i + 1) * P]
                                          for i in range(4 * k, min(n, 4 * k + 4))])
                            use += 1
                        gate_steps(UNDER_DIL[b][1])
                        pe.wait_ge(tb_free, f + (use + 2))
                        for i, v in enumerate(dil_values(b - 1)):
                            last = pe.matmul(ps[:, TB + use % 2, 0:P], dl_pT[:, i, :], v, start=(i == 0),
                                             stop=(i == n - 1))
                        last.then_inc(tb_full, 1)
                        use += 1
                gate_steps(len(gates))
                pe.wait_ge(tb_free, f + (use + 2))
                turn_blocks(f, use, dl_st)
                assert use + 2 == DIL_USES

            def df_scores(h, i, par):
                for m in range(2):
                    if i >= 1:
                        pe.wait_ge(df_max, h * (2 * NB) + (2 * i - 1 + m))
                    rows = slice(64 * m, 64 * m + 64)
                    n = (i + 1) * P
                    for at in range(0, n, HALF):
                        w = min(HALF, n - at)
                        last = pe.matmul(ps[:, SC + 2 * m + at // HALF, 0:w], df_q[par][rows, i * P:(i + 1) * P],
                                         df_k[par][rows, at:at + w], start=True, stop=True)
                    last.then_inc(df_s, 1)

            def df_turn_values(f, use, u):
                pe.wait_ge(pj_free, u + 3)
                turn_blocks(f, use, df_vT.rearrange("p (b e) -> p b e", b=NB))

            def df_head(pair, par, f, tiles_under, more):
                h = pair * 2 + par
                n0 = W_DIFF + 3 + 3 * par
                under = [(j, half, k) for j in range(tiles_under) for half in range(2) for k in range(NK)]
                use = 0

                def steps_under(count):
                    for _ in range(count):
                        j, half, k = under.pop(0)
                        product(pair * 6 + (n0 + j), (n0 + j) % 2, half, pair * 12 + (unit_of(n0 + j) + half), steps=(k,))

                pe.wait_ge(pj_free, pair * 12 + (unit_of(W_DIFF + 3 * par) + 3 + 3))
                for i in range(NB + 1):
                    if i < NB:
                        df_scores(h, i, par)
                    steps_under(UNDER_DIFF[i][0])
                    if i >= 1:
                        pe.wait_ge(df_comb, h * NB + i)
                        for k in range(fills(i)):
                            turn(f, use, [df_a[:, j * P:(j + 1) * P] for j in range(4 * k, min(i, 4 * k + 4))])
                            use += 1
                        steps_under(UNDER_DIFF[i][1])
                        pe.wait_ge(tb_free, f + (use + 2))
                        for j in range(i):
                            last = pe.matmul(ps[:, TB + use % 2, 0:P], df_aT[:, j, :], df_v[par][:, j, :],
                                             start=(j == 0), stop=(j == i - 1))
                        last.then_inc(tb_full, 1)
                        use += 1
                assert use - 1 == DF_LAST
                steps_under(6 * NK - done_by(UNDER_DIFF, NB, 1))
                if more:
                    df_turn_values(f, use, pair * 12 + (unit_of(n0) + 5))
                    use += 2
                pe.wait_ge(df_norm, h + 1)
                turn_blocks(f, use, df_st)
                steps_under(len(under))

            for j in range(3):
                for half in range(2):
                    product(W_DIFF + j, j % 2, half, unit_of(W_DIFF + j) + half)
            df_turn_values(F_DIFF, 0, unit_of(W_DIFF) + 5)
            with pe.Fori(0, DIFF_H // 2 - 1) as t:
                for par in range(2):
                    df_head(t, par, t * (2 * DIFF_USES) + (F_DIFF + 2 + par * DIFF_USES), 3, True)
            pair = DIFF_H // 2 - 1
            df_head(pair, 0, F_DIFF + 2 + 2 * pair * DIFF_USES, 3, True)
            df_head(pair, 1, F_DIFF + 2 + (2 * pair + 1) * DIFF_USES, LAST_GATES, False)

            def branch(t, split=None):
                u = t * 4 + unit_of(W_BRANCH)
                for half in range(2):
                    product(t * 2 + W_BRANCH, 0, half, u + half, hi=od_hi, lo=od_lo, kt=DIL_H)
                for half in range(2):
                    product(t * 2 + (W_BRANCH + 1), 1, half, u + (2 + half), before=None if half else split)

            pe.wait_ge(split_lo, DIL_H)
            branch(0, lambda k: pe.wait_ge(split_lo, DIL_H + k + 1))
            with pe.Fori(1, NK) as t:
                branch(t)

            def project_out(t, gated=None):
                for s in range(2):
                    for half in range(2):
                        product(t * 2 + (W_OUT + s), s, half, t * 4 + (unit_of(W_OUT) + 2 * s + half), x_in=t * 16 + 16,
                                hi=y_hi, lo=y_lo, add_x=x_back[0][s].rearrange("p (b d) -> p b d", b=NB),
                                before=None if s or half else gated)

            project_out(0, lambda k: pe.wait_ge(y_done, k + 2))
            with pe.Fori(1, NK // 2) as t:
                project_out(t)
            norm_sum(1)

            pe.wait_ge(mem_norm, 2)
            for k in range(NK):
                for j in range(2):
                    at = (k % 2) * MEM + j * P
                    last = pe.transpose(ps[:, SC + k // 2, at:at + P], mem_x[:, j, k * P:(k + 1) * P], idn[:, :])
                if k % 2:
                    last.then_inc(mem_turn, 1)
            pe.wait_ge(mem_lo, NK)
            norm_spread(1)
            with pe.Fori(0, NK // 2) as t:
                for s in range(2):
                    product(t * 2 + (W_MEM + s), s, 0, t * 2 + (U_MEM + s), hi=mn_hi, lo=mn_lo, cols=MEM)
            with pe.Fori(0, NK // 2) as t:
                for s in range(2):
                    product(t * 2 + (W_MEM + NK + s), s, 0, t * 2 + (U_MEM + NK + s), hi=mn_hi, lo=mn_lo, cols=MEM)
                for s in range(2):
                    pe.wait_ge(pj_free, t * 2 + (U_MEM + NK + s + 3))
                    turn(t * 2 + F_MEM, s, [mv_t[s][:, j * P:(j + 1) * P] for j in range(2)])

            with pe.Fori(0, X_H) as t:
                for s in range(2):
                    for half in range(2):
                        product(t * 2 + (W_CQ + s), s, half, t * 4 + (U_CQ + 2 * s + half))
                pe.wait_ge(pj_free, t * 4 + (U_CQ + 6))
                pe.wait_ge(x_lo, t * 4 + 1)
                pe.wait_ge(x_head, t * 2 + 2)
                for g in range(2):
                    for b in range(4):
                        q = 4 * g + b
                        for k in range(2):
                            last = pe.matmul(ps[:, SC + 2 * g + b // 2, (b % 2) * MEM:(b % 2 + 1) * MEM],
                                             qx[:, k, q * P:(q + 1) * P], mkh[:, k, :], start=(k == 0), stop=(k == 1))
                    last.then_inc(x_s, 1)
                for g in range(2):
                    pe.wait_ge(x_norm, t * 2 + (g + 1))
                    if g == 1:
                        pe.wait_ge(x_lo, t * 4 + 3)
                    for j in range(2):
                        turn(t * 8 + F_CROSS, 4 * g + j, [px[g][:, b, j * P:(j + 1) * P] for b in range(4)])
                    pe.wait_ge(tb_free, t * 8 + (F_CROSS + 4 * g + 4))
                    for e in range(2):
                        for j in range(2):
                            last = pe.matmul(bank(TB + e), mvh[:, j, e * P:(e + 1) * P], pxT[:, j, :],
                                             start=(j == 0), stop=(j == 1))
                        last.then_inc(tb_full, 1)

            pe.wait_ge(x_lo, 4 * X_H + 1)
            products(W_CO, NK, hi=co_hi, lo=co_lo)
            norm_sum(2)
            norm_spread(2)

            for c, (f0, m) in enumerate(FF_CHUNKS):
                products(W_FF_AT[c], 2 * m)
                pe.wait_ge(m_done, f0 + m + 1)
                products(W_FF_AT[c] + 2 * m, NK, hi=m_hi, lo=m_lo, kt=m)
            norm_sum(3)

            pe.wait_ge(fin_scaled, NK)
            for r in range(2 * NB):
                b, half = r // 2, r % 2
                if SC + r == NS:
                    pe.wait_ge(nf_ms, 4)
                if r >= 4:
                    pe.wait_ge(fin_row, r - 3)
                for j in range(4):
                    last = pe.transpose(ps[:, SC + r % 4, j * P:(j + 1) * P],
                                        xt[:, 4 * half + j, b * P:(b + 1) * P], idn[:, :])
                last.then_inc(fin_turn, 1)

        @block.vector
        def _(dve):
            def aside(value, loaded):
                dve.compute_val(value)
                dve.wait_ge(bias_in, loaded)
                return value

            def take(u, half, out, kind, scale=None, cols=HALF, other=None):
                dve.wait_ge(pj_ready, u + 1)
                src = bank(half, cols)
                if kind == "copy":
                    ins = dve.tensor_copy(out, src)
                elif kind == "add":
                    ins = dve.tensor_tensor(out, src, other, ALU.add)
                elif kind == "mult":
                    ins = dve.tensor_tensor(out, src, other, ALU.mult)
                else:
                    root = rstd_bc[:, half * HALF:(half + 1) * HALF]
                    if kind == "residue":
                        src, root = by_residue(src), by_residue(root)
                    if scale is None:
                        ins = dve.tensor_tensor(out, src, root, ALU.mult)
                    else:
                        ins = dve.scalar_tensor_tensor(out, src, scale, root, ALU.mult, ALU.mult)
                ins.then_inc(pj_free, 1)

            def halves(ap, half):
                return ap[:, half * HALF:(half + 1) * HALF]

            def norm_begin(i):
                dve.memset(acc[i], 0.0).then_inc(feed_dve[i], 1)

            def feed(i, k, gain, source, hi, lo):
                dve.wait_ge(feed_act[i], k * 2 + 2)
                dve.scalar_tensor_tensor(lo, source, gain, hi, ALU.mult, ALU.subtract).then_inc(feed_dve[i], 1)
                dve.wait_ge(feed_dve[i], k * 2 + 2)
                dve.tensor_tensor(acc[i], acc[i], sq[i], ALU.add).then_inc(feed_dve[i], 1)

            def norm_mean(i):
                dve.wait_ge(nf_sum, i + 1)
                dve.tensor_scalar(msq, ps[:, NS, 0:NB], 1.0 / D, EPS, ALU.mult, ALU.add).then_inc(nf_ms, 1)

            dve.memset(spare[:, 0:1], 0.0).then_inc(pj_free, 1)
            dve.memset(spare[:, 1:2], 0.0).then_inc(pj_free, 1)
            norm_begin(0)
            dve.memset(spare[:, 3:4], 0.0).then_inc(x0_free, 1)
            dve.memset(spare[:, 4:5], 0.0).then_inc(x0_free, 1)
            for half in range(2):
                dve.memset(gate_spare[:, half:half + 1], 0.0).then_inc(gate_out[half], 16)
            dve.wait_ge(const_in, 32)
            for i in range(2):
                q1, k1 = (col[:, C_LAM + 64 * (2 * i + j):C_LAM + 64 * (2 * i + j + 1)] for j in range(2))
                dve.tensor_tensor_reduce(lam_tmp[:, i, :], q1, k1, 1.0, 0.0, ALU.mult, ALU.add,
                                         lam_dot[:, i:i + 1]).then_inc(lam_dots, 1)
            dve.tensor_scalar(sub_gain, col[:, C_SUB:C_SUB + 1], 1.0 - LAM_INIT, None, ALU.mult).then_inc(lam_ok, 1)
            dve.wait_ge(lam_exps, 1)
            dve.scalar_tensor_tensor(neglam, lam_exp[:, 1:2], -LAM_INIT, lam_exp[:, 0:1], ALU.add,
                                     ALU.subtract).then_inc(lam_ok, 1)
            dve.wait_ge(feed_dve[0], 1)
            with dve.Fori(0, NK // 2) as t:
                for s in range(2):
                    k = t * 2 + s
                    dve.wait_ge(feed_act[0], t * 4 + (2 * s + 2))
                    dve.scalar_tensor_tensor(h_lo[:, k, :], banks(SC + 2 * s, S), col[:, bass.ds(t * 2 + (C_MIX + s), 1)],
                                             h_hi[:, k, :].bitcast(F32), ALU.mult, ALU.subtract).then_inc(x0_free, 1)
                    dve.tensor_tensor(acc[0], acc[0], sq[0], ALU.add).then_inc(feed_dve[0], 2)
                    dve.wait_ge(feed_dve[0], t * 4 + (2 * s + 3))
            norm_mean(0)

            def take_gate(g, u, half, buf):
                dve.wait_ge(gate_out[half], g * 16 + 16)
                take(u, half, halves(buf, half), "plain")

            dve.wait_ge(bias_in, 16)
            dve.tensor_scalar(dl_bias, dl_bias, 0.25, None, ALU.mult).then_inc(dl_slope, 1)
            dve.wait_ge(nf_bc, 1)
            with dve.Fori(0, DIL_H) as t:
                u = t * (2 * DIL_TILES)
                for j in range(QKV):
                    g, kind = j // 3, j % 3
                    for half in range(2):
                        if kind == 0:
                            take(u + (2 * j + half), half, half_by_residue(dl_q[g], half), "residue", DIL_SCALE)
                        else:
                            buf = dl_k[g] if kind == 1 else dl_vT
                            if g == 0:
                                take(u + (2 * j + half), half, halves(buf, half), "plain")
                            else:
                                take(u + (2 * j + half), half, half_by_residue(buf, half), "residue")
                gates = [(j, half) for j in range(DIL_GATES) for half in range(2)]

                def take_gates(steps):
                    while gates and 8 * (2 * DIL_GATES - len(gates) + 1) <= steps:
                        j, half = gates.pop(0)
                        take_gate(t * DIL_GATES + j, u + (2 * (QKV + j) + half), half, dl_gate)

                dve.wait_ge(dl_slope, t + 1)
                for b in range(NB + 1):
                    if b < NB:
                        rho, jb = b // 2, b % 2
                        near, far = (512, 256) if jb == 0 else (640, 512)
                        near0 = 131 - rho if jb == 0 else 3 - rho
                        sc = banks(SC, near + far)
                        pb = dl_p[b % 2]
                        dve.wait_ge(dl_s, aside(t * NB + (b + 1), 16))
                        dve.tensor_tensor_reduce(pb[:, 0:near], sc[:, 0:near], dl_near[:, near0:near0 + near],
                                                 1.0, -3e38, ALU.add, ALU.max, dl_mx[:, 2 * b:2 * b + 1]).then_inc(dl_max, 1)
                        dve.tensor_tensor_reduce(pb[:, near:near + far], sc[:, near:near + far], dl_far[jb],
                                                 1.0, -3e38, ALU.add, ALU.max, dl_mx[:, 2 * b + 1:2 * b + 2]).then_inc(dl_max, 1)
                        dve.wait_ge(dl_max, t * (2 * NB) + (2 * b + 2))
                        dve.tensor_scalar(dl_nm[:, b:b + 1], dl_mx[:, 2 * b:2 * b + 1], dl_mx[:, 2 * b + 1:2 * b + 2],
                                          -1.0, ALU.max, ALU.mult).then_inc(dl_neg, 1)
                    if b >= 1:
                        dve.wait_ge(dl_exp, t * NB + b)
                        dve.reciprocal(dl_rd[:, b - 1:b], dl_den[:, b - 1:b]).then_inc(dl_rec, 1)
                        take_gates(done_by(UNDER_DIL, b, 0))
                take_gates(8 * 2 * DIL_GATES)
                dve.tensor_scalar(dl_bias, dl_bias, 0.25, None, ALU.mult).then_inc(dl_slope, 1)

            def df_take(unit0, par, j, half):
                buf = (df_q[par], df_k[par], df_vT)[j]
                take(unit0 + (2 * j + half), half, halves(buf, half), "plain", DIFF_SCALE if j == 0 else None)

            def split_heads(order):
                for n, k in order:
                    hi, lo = head_parts(k)
                    dve.wait_ge(split_hi, n + 1)
                    dve.tensor_tensor(lo, oT[:, k, :], hi.bitcast(F32), ALU.subtract).then_inc(split_lo, 1)

            def df_head(pair, par, f, tiles_under, more):
                h = pair * 2 + par
                unit0 = pair * 12 + unit_of(W_DIFF + 3 + 3 * par)
                under = [(j, half) for j in range(tiles_under) for half in range(2)]
                use = 0

                def take_under(steps):
                    while under and 8 * (2 * tiles_under - len(under) + 1) <= steps:
                        j, half = under.pop(0)
                        if more:
                            df_take(unit0, 1 - par, j, half)
                        else:
                            take_gate(DIL_H * DIL_GATES + j, unit0 + (2 * j + half), half, df_gate)

                dve.wait_ge(df_slope, h + 1)
                for i in range(NB):
                    n = (i + 1) * P
                    if i >= 1:
                        dve.wait_ge(df_comb, h * NB + i)
                    for m in range(2):
                        dve.wait_ge(df_s, aside(h * (2 * NB) + (2 * i + m + 1), 32))
                        dve.tensor_tensor_reduce(df_p[m][:, 0:n], banks(SC + 2 * m, n), df_bias[:, S - n:S],
                                                 1.0, -3e38, ALU.add, ALU.max,
                                                 df_mx[:, 2 * i + m:2 * i + m + 1]).then_inc(df_max, 1)
                    dve.wait_ge(df_max, h * (2 * NB) + (2 * i + 2))
                    two = slice(2 * i, 2 * i + 2)
                    dve.tensor_scalar(df_nm[:, two], df_mx[:, two], -1.0, None, ALU.mult).then_inc(df_neg, 1)
                    take_under(done_by(UNDER_DIFF, i, 0))
                    dve.wait_ge(df_exp, h * (2 * NB) + (2 * i + 2))
                    dve.reciprocal(df_rd[:, two], df_den[:, two]).then_inc(df_rec, 1)
                    dve.wait_ge(df_rec, h * NB + (i + 1))
                    dve.scalar_tensor_tensor(df_cc[:, i:i + 1], df_rd[:, 2 * i + 1:2 * i + 2], neglam,
                                             df_den[:, 2 * i:2 * i + 1], ALU.mult, ALU.mult).then_inc(df_coef, 1)
                    dve.wait_ge(df_coef, h * NB + (i + 1))
                    dve.wait_ge(tb_full, f + use)
                    dve.scalar_tensor_tensor(df_a[:, 0:n], df_p[1][:, 0:n], df_cc[:, i:i + 1], df_p[0][:, 0:n],
                                             ALU.mult, ALU.add).then_inc(df_comb, 1)
                    use = (use + 1 if i else 0) + fills(i + 1)
                    take_under(done_by(UNDER_DIFF, i, 1))
                dve.wait_ge(df_comb, h * NB + NB)
                dve.tensor_scalar(df_bias, df_bias, 0.5, None, ALU.mult).then_inc(df_slope, 1)
                take_under(6 * NK)
                dve.wait_ge(df_pow, h + 1)
                dve.tensor_tensor(df_st, df_st, df_rs.unsqueeze(2).to_broadcast([P, NB, P]), ALU.mult).then_inc(df_norm, 1)
                if not more:
                    split_heads([(n, DIFF_H + n) for n in range(DIL_H)])
                take_under(NK * 2 * tiles_under)

            for j in range(3):
                for half in range(2):
                    df_take(unit_of(W_DIFF), 0, j, half)
            dve.wait_ge(bias_in, 32)
            dve.tensor_scalar(df_bias, df_bias, 0.5, None, ALU.mult).then_inc(df_slope, 1)
            dve.wait_ge(lam_ok, 2)
            for half in range(2):
                dve.wait_ge(gate_out[half], 16 * DIL_H * DIL_GATES + 16)
            with dve.Fori(0, DIFF_H // 2 - 1) as t:
                for par in range(2):
                    df_head(t, par, t * (2 * DIFF_USES) + (F_DIFF + 2 + par * DIFF_USES), 3, True)
            pair = DIFF_H // 2 - 1
            df_head(pair, 0, F_DIFF + 2 + 2 * pair * DIFF_USES, 3, True)
            df_head(pair, 1, F_DIFF + 2 + (2 * pair + 1) * DIFF_USES, LAST_GATES, False)

            split_heads([(DIL_H + k, k) for k in range(DIFF_H)])

            dve.memset(spare[:, 5:6], 0.0).then_inc(y_done, 1)
            with dve.Fori(0, NK) as t:
                u = t * 4 + unit_of(W_BRANCH)
                dve.wait_ge(z_sig, t * 2 + 2)
                dve.wait_ge(y_done, t + 1)
                for half in range(2):
                    take(u + half, half, halves(yl, half), "mult", other=halves(zb[1], half))
                for half in range(2):
                    take(u + (2 + half), half, halves(yd, half), "mult", other=halves(zb[0], half))
                dve.wait_ge(pj_free, u + 6)
                dve.tensor_tensor(yd, yd, yl, ALU.add).then_inc(y_sum, 1)
                dve.wait_ge(y_round, t + 1)
                dve.tensor_tensor(y_lo[:, t, :], yd, y_hi[:, t, :].bitcast(F32), ALU.subtract).then_inc(y_done, 1)

            dve.wait_ge(y_done, NK + 1)
            norm_begin(1)
            dve.wait_ge(feed_dve[1], 1)
            with dve.Fori(0, NK) as k:
                for half in range(2):
                    take(k * 2 + (unit_of(W_OUT) + half), half, xt[:, k, half * HALF:(half + 1) * HALF], "copy")
                dve.wait_ge(pj_free, k * 2 + (unit_of(W_OUT) + 4))
                feed(1, k, col[:, bass.ds(k + C_CROSS, 1)], xt[:, k, :], h_hi[:, k, :].bitcast(F32), h_lo[:, k, :])
            norm_mean(1)

            dve.wait_ge(mem_pow, 1)
            for j in range(2):
                dve.tensor_scalar(mem_x[:, j, :], mem_x[:, j, :], mem_rstd[:, j:j + 1], None,
                                  ALU.mult).then_inc(mem_norm, 1)
            for k in range(NK):
                dve.wait_ge(mem_hi, (k | 1) + 1)
                dve.scalar_tensor_tensor(mn_lo[:, k, :], ps[:, SC + k // 2, (k % 2) * MEM:(k % 2 + 1) * MEM],
                                         col[:, C_MEM + k:C_MEM + k + 1], mn_hi[:, k, :].bitcast(F32),
                                         ALU.mult, ALU.subtract).then_inc(mem_lo, 1)
            dve.wait_ge(x_spilled, 16 * NK)
            with dve.Fori(0, NK // 2) as t:
                for s in range(2):
                    take(t * 2 + (U_MEM + s), s, mk[:, t * 2 + s, :], "copy", cols=MEM)
            with dve.Fori(0, NK // 2) as t:
                for s in range(2):
                    take(t * 2 + (U_MEM + NK + s), s, mv_t[s], "copy", cols=MEM)

            dve.wait_ge(nf_bc, 2)
            dve.memset(small[:, 51:52], 0.0).then_inc(x_lo, 1)
            with dve.Fori(0, X_H) as t:
                for s in range(2):
                    for half in range(2):
                        take(t * 4 + (U_CQ + 2 * s + half), half, halves(qx[:, s, :], half), "plain", X_SCALE)
                for g in range(2):
                    four = slice(4 * g, 4 * g + 4)
                    dve.wait_ge(x_s, t * 2 + (g + 1))
                    dve.tensor_reduce(x_mx[:, four], banks(SC + 2 * g, S).rearrange("p (b m) -> p b m", b=4),
                                      AX_X, ALU.max).then_inc(x_max, 1)
                    dve.wait_ge(x_max, t * 2 + (g + 1))
                    dve.tensor_scalar(x_nm[:, four], x_mx[:, four], -1.0, None, ALU.mult).then_inc(x_neg, 1)
                for g in range(2):
                    four = slice(4 * g, 4 * g + 4)
                    dve.wait_ge(x_exp, t * 8 + (4 * g + 4))
                    dve.reciprocal(x_rd[:, four], x_den[:, four]).then_inc(x_rec, 1)
                    dve.wait_ge(x_rec, t * 2 + (g + 1))
                    dve.tensor_tensor(px[g], px[g], x_rd[:, four].unsqueeze(2).to_broadcast([P, 4, MEM]),
                                      ALU.mult).then_inc(x_norm, 1)
                for c in range(4):
                    dve.wait_ge(tb_free, t * 8 + (F_CROSS + 4 * (c // 2) + 2 + c % 2 + 3))
                    at = slice((c // 2) * HALF, (c // 2 + 1) * HALF)
                    dve.tensor_tensor(co_lo[:, t * 2 + c % 2, at], bank(TB + c % 2), co_hi[:, t * 2 + c % 2, at].bitcast(F32),
                                      ALU.subtract).then_inc(x_lo, 1)

            norm_begin(2)
            dve.wait_ge(feed_dve[2], 1)
            with dve.Fori(0, NK // 2) as t:
                for s in range(2):
                    k = t * 2 + s
                    dve.wait_ge(back_in[1][s], t * 16 + 16)
                    for half in range(2):
                        take(t * 4 + (unit_of(W_CO) + 2 * s + half), half, xt[:, k, half * HALF:(half + 1) * HALF],
                             "add", other=halves(x_back[1][s], half))
                    dve.wait_ge(pj_free, t * 4 + (unit_of(W_CO) + 2 * s + 4))
                    feed(2, k, col[:, bass.ds(t * 2 + (C_FFN + s), 1)], xt[:, k, :], h_hi[:, k, :].bitcast(F32),
                         h_lo[:, k, :])
            norm_mean(2)

            dve.memset(a_pad[:, 0:2], 0.0).then_inc(conv2, 1)
            dve.memset(c_buf, 0.0).then_inc(m_prod, 1)
            dve.memset(spare[:, 6:7], 0.0).then_inc(m_done, 1)
            dve.wait_ge(nf_bc, 3)
            for c, (f0, m) in enumerate(FF_CHUNKS):
                with dve.Fori(0, m) as t:
                    u = t * 4 + unit_of(W_FF_AT[c])
                    dve.wait_ge(conv2, t + (f0 + 1))
                    for half in range(2):
                        take(u + half, half, a_pad[:, 2 + half * HALF:2 + (half + 1) * HALF], "plain")
                    dve.wait_ge(conv0, t + (f0 + 1))
                    for tap, done in ((1, conv1), (2, conv2)):
                        w_tap = col[:, bass.ds(t + (C_CONVW + tap * FF_T + f0), 1)]
                        dve.scalar_tensor_tensor(c_buf, a_pad[:, tap:tap + S], w_tap, c_buf, ALU.mult,
                                                 ALU.add).then_inc(done, 1)
                        if tap == 1:
                            dve.wait_ge(conv1, t + (f0 + 1))
                    dve.wait_ge(m_done, t + (f0 + 1))
                    for half in range(2):
                        take(u + (2 + half), half, halves(b_buf, half), "plain")
                    dve.wait_ge(pj_free, u + 6)
                    dve.wait_ge(gelu_ok, t + (f0 + 1))
                    dve.tensor_tensor(b_buf, b_buf, c_buf, ALU.mult).then_inc(m_prod, 1)
                    dve.wait_ge(m_round, t + (f0 + 1))
                    dve.tensor_tensor(m_lo[:, t, :], b_buf, m_hi[:, t, :].bitcast(F32), ALU.subtract).then_inc(m_done, 1)
                last_chunk = c == len(FF_CHUNKS) - 1
                if last_chunk:
                    dve.wait_ge(m_done, FF_T + 1)
                    norm_begin(3)
                    dve.wait_ge(feed_dve[3], 1)
                with dve.Fori(0, NK) as k:
                    for half in range(2):
                        at = slice(half * HALF, (half + 1) * HALF)
                        take(k * 2 + (unit_of(W_FF_AT[c] + 2 * m) + half), half, xt[:, k, at], "add",
                             other=xt[:, k, at])
                    if last_chunk:
                        dve.wait_ge(feed_act[3], k + 1)
                        dve.tensor_tensor(acc[3], acc[3], sq[3], ALU.add).then_inc(feed_dve[3], 1)
                        dve.wait_ge(feed_dve[3], k + 2)
            norm_mean(3)

        @block.scalar
        def _(act):
            def aside(value):
                act.compute_val(value)
                act.wait_ge(const_in, 32)
                return value

            def turn_out(f, use, out, n=HALF, scale=None, shape=None, moving=False):
                act.wait_ge(tb_full, aside(f + (use + 1)) if moving else f + (use + 1))
                source = bank(TB + use % 2, n)
                if shape is not None:
                    source = shape(source)
                if scale is None:
                    act.activation(out, source, ACT.Copy).then_inc(tb_free, 1)
                else:
                    act.activation(out, source, ACT.Copy, scale=scale).then_inc(tb_free, 1)

            def store_gate(g, u, half, buf):
                act.wait_ge(pj_free, u + 3)
                at = slice(half * HALF, (half + 1) * HALF)
                act.dma_start(z_dram[g][:, at], buf[:, at]).then_inc(gate_out[half], 16)

            def rstd_out(i):
                act.wait_ge(nf_turn, i + 1)
                act.activation(rstd_bc[:, :], banks(SC, S), ACT.Copy).then_inc(nf_bc, 1)

            act.wait_ge(const_ok, 3)
            act.activation(spare[:, 2:3], zero_col, ACT.Copy).then_inc(tb_free, 1)
            act.activation(small[:, 50:51], zero_col, ACT.Copy).then_inc(tb_free, 1)

            act.wait_ge(lam_dots, 2)
            act.activation(lam_exp, lam_dot, ACT.Exp).then_inc(lam_exps, 1)

            act.wait_ge(const_in, 32)
            with act.Fori(0, NK // 2) as t:
                for s in range(2):
                    act.wait_ge(x0_turned, aside(t * 2 + (s + 1)))
                    act.activation(h_hi[:, t * 2 + s, :], banks(SC + 2 * s, S), ACT.Copy,
                                   scale=col[:, bass.ds(t * 2 + (C_MIX + s), 1)]).then_inc(feed_act[0], 1)
                    act.wait_ge(feed_dve[0], t * 4 + (2 * s + 1))
                    act.activation(sq[0], banks(SC + 2 * s, S), ACT.Square).then_inc(feed_act[0], 1)
            rstd_out(0)

            with act.Fori(0, DIL_H) as t:
                f = t * DIL_USES
                for use in range(2 * GROUPS):
                    turn_out(f, use, dl_v[use // 2][:, 4 * (use % 2):4 * (use % 2) + 4, :])
                use = 2 * GROUPS
                gates = [(j, half) for j in range(DIL_GATES) for half in range(2)]

                def store_gates(steps):
                    while gates and 8 * (2 * DIL_GATES - len(gates) + 1) <= steps:
                        j, half = gates.pop(0)
                        store_gate(t * DIL_GATES + j, t * (2 * DIL_TILES) + (2 * (QKV + j) + half), half, dl_gate)

                for b in range(NB + 1):
                    if b >= 1:
                        n = dil_tiles((b - 1) % 2)
                        for k in range(fills(n)):
                            m = min(4, n - 4 * k)
                            turn_out(f, use, dl_pT[:, 4 * k:4 * k + m, :], m * P)
                            use += 1
                    if b < NB:
                        act.wait_ge(dl_neg, t * NB + (b + 1))
                        pb = dl_p[b % 2][:, 0:dil_tiles(b % 2) * P]
                        act.activation(pb, pb, ACT.Exp, bias=dl_nm[:, b:b + 1],
                                       accum_out=dl_den[:, b:b + 1]).then_inc(dl_exp, 1)
                    if b >= 1:
                        act.wait_ge(dl_rec, t * NB + b)
                        turn_out(f, use, dl_st[:, b - 1, :], P, scale=dl_rd[:, b - 1:b])
                        use += 1
                        store_gates(done_by(UNDER_DIL, b - 1, 1))
                for part in range(2):
                    turn_out(f, use + part, by_residue(oT[:, t + DIFF_H, :])[:, 2 * part:2 * part + 2, :],
                             shape=lambda ap: ap.rearrange("p (r j) -> p r j", r=2), moving=True)
                store_gates(8 * 2 * DIL_GATES)

            def round_heads(heads):
                act.wait_ge(tb_free, F_MEM + 2)
                for k in heads:
                    act.activation(head_parts(k)[0], oT[:, k, :], ACT.Copy).then_inc(split_hi, 1)

            def df_values(f, use, par):
                for part in range(2):
                    turn_out(f, use + part, df_v[par][:, 4 * part:4 * part + 4, :])

            def df_head(pair, par, f, tiles_under, more):
                h = pair * 2 + par
                unit0 = pair * 12 + unit_of(W_DIFF + 3 + 3 * par)
                gates = [] if more else [(j, half) for j in range(tiles_under) for half in range(2)]
                use = 0

                def store_gates(steps):
                    while gates and 8 * (2 * tiles_under - len(gates) + 1) <= steps:
                        j, half = gates.pop(0)
                        store_gate(DIL_H * DIL_GATES + j, unit0 + (2 * j + half), half, df_gate)

                for i in range(NB + 1):
                    for k in range(fills(i)):
                        m = min(4, i - 4 * k)
                        turn_out(f, use, df_aT[:, 4 * k:4 * k + m, :], m * P)
                        use += 1
                    if i < NB:
                        n = (i + 1) * P
                        act.wait_ge(df_neg, h * NB + (i + 1))
                        for m in range(2):
                            at = slice(2 * i + m, 2 * i + m + 1)
                            act.activation(df_p[m][:, 0:n], df_p[m][:, 0:n], ACT.Exp, bias=df_nm[:, at],
                                           accum_out=df_den[:, at]).then_inc(df_exp, 1)
                    if i >= 1:
                        j = i - 1
                        act.wait_ge(df_rec, h * NB + i)
                        act.wait_ge(tb_full, f + (use + 1))
                        scale = df_rd[:, 2 * j:2 * j + 1]
                        act.activation(df_st[:, j, :], bank(TB + use % 2, P), ACT.Copy, scale=scale)
                        act.activation(df_sq, bank(TB + use % 2, P), ACT.Square, scale=scale,
                                       accum_out=df_ssq[:, j:j + 1]).then_inc(tb_free, 1)
                        use += 1
                        store_gates(done_by(UNDER_DIFF, i - 1, 1))
                if more:
                    df_values(f, use, 1 - par)
                    use += 2
                store_gates(5 * NK)
                for part in range(2):
                    turn_out(f, use + part, oT[:, h, part * HALF:(part + 1) * HALF], scale=sub_gain, moving=True)
                if not more:
                    round_heads([DIFF_H + i for i in range(DIL_H)])
                    store_gates(NK * 2 * tiles_under)

            act.wait_ge(lam_ok, 2)
            df_values(F_DIFF, 0, 0)
            with act.Fori(0, DIFF_H // 2 - 1) as t:
                for par in range(2):
                    df_head(t, par, t * (2 * DIFF_USES) + (F_DIFF + 2 + par * DIFF_USES), 3, True)
            pair = DIFF_H // 2 - 1
            df_head(pair, 0, F_DIFF + 2 + 2 * pair * DIFF_USES, 3, True)
            df_head(pair, 1, F_DIFF + 2 + (2 * pair + 1) * DIFF_USES, LAST_GATES, False)

            act.wait_ge(pj_ready, unit_of(W_BRANCH))
            round_heads(range(DIFF_H))
            for half in range(2):
                act.wait_ge(gate_out[half], 16 * 2 * NK + 16)

            with act.Fori(0, NK) as t:
                for i in range(2):
                    act.dma_start(zb[i], z_dram[t + i * NK]).then_inc(z_in, 16)
                act.wait_ge(z_in, aside(t * 32 + 32))
                for i in range(2):
                    act.activation(zb[i], zb[i], ACT.Sigmoid,
                                   bias=col[:, bass.ds(t + (C_GATE + i * NK), 1)]).then_inc(z_sig, 1)
                act.wait_ge(y_sum, aside(t + 1))
                act.activation(y_hi[:, t, :], yd, ACT.Copy).then_inc(y_round, 1)

            def feed(i, k, gain):
                act.activation(h_hi[:, k, :], xt[:, k, :], ACT.Copy, scale=gain).then_inc(feed_act[i], 1)
                act.wait_ge(feed_dve[i], aside(k * 2 + 1))
                act.activation(sq[i], xt[:, k, :], ACT.Square).then_inc(feed_act[i], 1)

            def residual(i, first, gains, source):
                for s in range(2):
                    act.dma_start(x_slot(i, s), source(s)).then_inc(back_in[i][s], 16)

                def step(t, more):
                    for s in range(2):
                        act.wait_ge(pj_free, t * 4 + (unit_of(first) + 2 * s + 4))
                        if more:
                            act.dma_start(x_slot(i, s), source(t * 2 + (s + 2))).then_inc(back_in[i][s], 16)
                        if i == 0:
                            act.dma_start(x_spill[t * 2 + s], xt[:, t * 2 + s, :]).then_inc(x_spilled, 16)
                        feed(i + 1, t * 2 + s, col[:, bass.ds(t * 2 + (gains + s), 1)])

                with act.Fori(0, NK // 2 - 1) as t:
                    step(t, True)
                step(NK // 2 - 1, False)

            def x_slot(i, s):
                return x_back[i][s].rearrange("p (b d) -> p b d", b=NB) if i == 0 else x_back[i][s]

            act.wait_ge(y_done, NK + 1)
            residual(0, W_OUT, C_CROSS, lambda k: x_cols[k])

            act.dma_start(mem_x, mem_rows).then_inc(mem_in, 16)
            act.wait_ge(mem_in, 16)
            for j in range(2):
                if j:
                    act.wait_ge(mem_sums, 1)
                act.activation(mem_sq, mem_x[:, j, :], ACT.Square, accum_out=mem_ssq[:, j:j + 1]).then_inc(mem_sums, 1)
            for k in range(NK):
                act.wait_ge(mem_turn, k // 2 + 1)
                act.activation(mn_hi[:, k, :], ps[:, SC + k // 2, (k % 2) * MEM:(k % 2 + 1) * MEM], ACT.Copy,
                               scale=col[:, C_MEM + k:C_MEM + k + 1]).then_inc(mem_hi, 1)
            rstd_out(1)
            with act.Fori(0, NK // 2) as t:
                for s in range(2):
                    turn_out(t * 2 + F_MEM, s, mv[:, :, bass.ds(t * MEM + s * P, P)], MEM,
                             shape=lambda ap: ap.rearrange("p (j e) -> p j e", j=2), moving=True)

            act.wait_ge(pj_free, U_CQ + 2)
            with act.Fori(0, X_H) as t:
                act.activation(mkh, mk[:, bass.ds(t * 2, 2), :], ACT.Copy).then_inc(x_head, 1)
                act.activation(mvh, mv[:, :, bass.ds(t * MEM, MEM)], ACT.Copy).then_inc(x_head, 1)
                for g in range(2):
                    act.wait_ge(x_neg, t * 2 + (g + 1))
                    for b in range(4):
                        at = slice(4 * g + b, 4 * g + b + 1)
                        act.activation(px[g][:, b, :], ps[:, SC + 2 * g + b // 2, (b % 2) * MEM:(b % 2 + 1) * MEM],
                                       ACT.Exp, bias=x_nm[:, at], accum_out=x_den[:, at]).then_inc(x_exp, 1)
                for g in range(2):
                    for j in range(2):
                        turn_out(t * 8 + F_CROSS, 4 * g + j, pxT[:, j, :])
                    for e in range(2):
                        turn_out(t * 8 + F_CROSS, 4 * g + 2 + e, co_hi[:, t * 2 + e, g * HALF:(g + 1) * HALF],
                                 moving=True)

            act.wait_ge(x_lo, 4 * X_H + 1)
            residual(1, W_CO, C_FFN, lambda k: x_spill[k])
            rstd_out(2)

            for c, (f0, m) in enumerate(FF_CHUNKS):
                with act.Fori(0, m) as t:
                    act.wait_ge(pj_free, t * 4 + (unit_of(W_FF_AT[c]) + 4))
                    act.wait_ge(m_prod, aside(t + (f0 + 1)))
                    act.activation(c_buf, a_pad[:, 0:S], ACT.Identity, scale=col[:, bass.ds(t + (C_CONVW + f0), 1)],
                                   bias=col[:, bass.ds(t + (C_CONVB + f0), 1)]).then_inc(conv0, 1)
                    act.wait_ge(conv2, t + (f0 + 2))
                    act.activation(c_buf, c_buf, ACT.Gelu).then_inc(gelu_ok, 1)
                    act.wait_ge(m_prod, aside(t + (f0 + 2)))
                    act.activation(m_hi[:, t, :], b_buf, ACT.Copy).then_inc(m_round, 1)
            with act.Fori(0, NK) as k:
                act.wait_ge(pj_free, k * 2 + (unit_of(W_TOTAL - NK) + 4))
                act.wait_ge(feed_dve[3], aside(k + 1))
                act.activation(sq[3], xt[:, k, :], ACT.Square).then_inc(feed_act[3], 1)
                act.wait_ge(feed_act[3], aside(k + 1))
                act.activation(xt[:, k, :], xt[:, k, :], ACT.Copy,
                               scale=col[:, bass.ds(k + C_FINAL, 1)]).then_inc(fin_scaled, 1)

            act.wait_ge(nf_rstd, 4)
            for r in range(2 * NB):
                act.wait_ge(fin_turn, r + 1)
                act.activation(o_rows[:, r, :], bank(SC + r % 4), ACT.Copy,
                               scale=rstd_tok[:, r // 2:r // 2 + 1]).then_inc(fin_row, 1)


def tiles_of(w, cols):
    kt = w.shape[0] // P
    t = w.reshape(kt, P, -1, P).transpose(2, 1, 0, 3)[cols]
    if kt < NK:
        t = np.concatenate([t, np.zeros((t.shape[0], P, NK - kt, P), t.dtype)], axis=2)
    return t


def weight_stream(a):
    w_in, w_up, w_down, w_ckv = (a[n][0] for n in ("w_in", "w_up", "w_down", "w_ckv"))
    dil0, gate0 = 3 * DIFF_H, 3 * DIFF_H + 3 * GROUPS * DIL_H
    order = []
    for s in range(DIL_H):
        for g in range(GROUPS):
            order += [dil0 + kind * GROUPS * DIL_H + g * DIL_H + s for kind in range(3)]
        order += [gate0 + DIL_GATES * s + i for i in range(DIL_GATES)]
    for h in range(DIFF_H):
        order += [kind * DIFF_H + h for kind in range(3)]
    order += range(gate0 + DIL_H * DIL_GATES, gate0 + 2 * NK)
    parts = [tiles_of(w_in, order)]
    both = [tiles_of(a[n][0], slice(None)) for n in ("w_branch_dil", "w_branch_diff")]
    parts.append(np.stack(both, axis=1).reshape(2 * NK, P, NK, P))
    parts += [tiles_of(a["w_out"][0], slice(None)), tiles_of(w_ckv, slice(None)),
              tiles_of(a["w_cq"][0], slice(None)), tiles_of(a["w_co"][0], slice(None))]
    for f0, m in FF_CHUNKS:
        parts.append(tiles_of(w_up, [f for i in range(f0, f0 + m) for f in (i, FF_T + i)]))
        parts.append(tiles_of(w_down[f0 * P:(f0 + m) * P], slice(None)))
    return np.ascontiguousarray(np.concatenate(parts))


def alibi_tables():
    p = np.arange(P)[:, None]
    dist = p + S - P - np.arange(S)[None]
    diff = np.where(dist >= 0, -dist, NEG)
    dist = 4 * p + 131 - np.arange(NEAR_W + 1)[None]
    near = np.where((dist >= 0) & (dist <= 128), -dist, NEG)
    far = []
    for jb in range(2):
        step = p + P * jb - np.arange(P * (jb + 1))[None]
        far.append(np.where((step >= 0) & (step <= 128), -step, NEG))
        far.append(np.where((step >= 0) & (step % 4 == 0), -(step / 4), NEG))
    return diff.astype(np.float32), np.concatenate([near] + far, axis=1).astype(np.float32)


def column_table(a):
    def cols(v):
        return v.reshape(-1, P).T

    parts = [cols(a[n][0]) for n in ("mix_norm_g", "cross_norm_g", "mem_norm_g", "ffn_norm_g")]
    parts += [cols(a["final_norm_g"]), cols(a["b_gate"][0]), cols(a["conv_w"][0].reshape(-1)), cols(a["conv_b"][0]),
              cols(a["diff_subln_g"][0])]
    lam = np.concatenate([a[n][0] for n in ("lam_q1", "lam_k1", "lam_q2", "lam_k2")])
    parts.append(np.broadcast_to(lam[None], (P, 256)))
    return np.ascontiguousarray(np.concatenate(parts, axis=1))


def kernel(**inputs):
    import concourse.bacc as bacc
    from concourse.bass_utils import run_bass_kernel_spmd

    a = {k: np.asarray(v) for k, v in inputs.items()}
    diff, dil = alibi_tables()
    arrays = {
        "x_in": np.ascontiguousarray(a["x"][0]),
        "mem_in": np.ascontiguousarray(a["mem"][0]),
        "w_stream": weight_stream(a),
        "columns": column_table(a),
        "ident": np.eye(P, dtype=np.float32),
        "alibi_diff": diff,
        "alibi_dil": dil,
    }
    nc = bacc.Bacc("TRN2", target_bir_lowering=False, num_devices=1)
    args = [nc.dram_tensor(f"{n}_dram", v.shape, mybir.dt.from_np(v.dtype), kind="ExternalInput").ap()
            for n, v in arrays.items()]
    args.append(nc.dram_tensor("result_dram", (S, D), F32, kind="ExternalOutput").ap())
    trunk_layer(nc, *args)
    r = run_bass_kernel_spmd(nc, [{f"{n}_dram": v for n, v in arrays.items()}], core_ids=[0])
    return r.results[0]["result_dram"].reshape(1, S, D)
```

```python
import math
from contextlib import ExitStack

import numpy as np

import concourse.bass as bass
from concourse import mybir

ALU = mybir.AluOpType
ACT = mybir.ActivationFunctionType
AX_X = mybir.AxisListType.X
F32 = mybir.dt.float32
F32R = mybir.dt.float32r

P = 128
D = 1024
S = 1024
MEM = 256
EPS = 1e-5
NK = D // P
NB = S // P
HALF = 512
DIFF_H = 8
DIL_H = 4
GROUPS = 3
X_H = 4
FF = 2816
FF_T = FF // P
CHUNK = 8
LAM_INIT = 0.8 - 0.6 * math.exp(-0.3 * 0)
DIFF_SCALE = 64 ** -0.5
DIL_SCALE = 128 ** -0.5
X_SCALE = 256 ** -0.5
NEG = -1e30

DIL_GATES = 3
LAST_GATES = 2 * NK - DIL_H * DIL_GATES
QKV = 3 * GROUPS
DIL_TILES = QKV + DIL_GATES
W_MEM = 0
W_DIL = W_MEM + 2 * NK
W_DIFF = W_DIL + DIL_H * DIL_TILES
W_GATE = W_DIFF + 3 * DIFF_H
W_BRANCH = W_GATE + LAST_GATES
W_OUT = W_BRANCH + 2 * NK
W_CQ = W_OUT + NK
W_CO = W_CQ + NK
W_FF = W_CO + NK
FF_CHUNKS = [(f, min(CHUNK, FF_T - f)) for f in range(0, FF_T, CHUNK)]
W_FF_AT = [W_FF + sum(2 * m + NK for _, m in FF_CHUNKS[:c]) for c in range(len(FF_CHUNKS))]
W_TOTAL = W_FF + sum(2 * m + NK for _, m in FF_CHUNKS)

def unit_of(tile):
    return tile if tile < W_DIL else W_DIL + 2 * (tile - W_DIL)


def dil_tiles(jb):
    return (4 if jb == 0 else 5) + 2 * (jb + 1)


def fills(n):
    return -(-n // 4)


DIL_USES = 2 * GROUPS + sum(fills(dil_tiles(b % 2)) + 1 for b in range(NB)) + 2
DIFF_USES = 2 + sum(fills(i + 1) + 1 for i in range(NB)) + 2
F_MEM = 0
F_DIL = F_MEM + NK
F_DIFF = F_DIL + DIL_H * DIL_USES
DF_LAST = sum(fills(i + 1) + 1 for i in range(NB)) - 1
F_CROSS = F_DIFF + DIFF_H * DIFF_USES

UNDER_DIL = [(4, 0), (3, 2), (2, 3), (3, 2), (2, 3), (3, 2), (2, 3), (3, 2), (2, 4)]
UNDER_DIFF = [(4, 0), (3, 3), (3, 3), (3, 2), (2, 2), (2, 2), (2, 2), (2, 1), (4, 3)]


def done_by(under, block, part):
    return sum(a + b for a, b in under[:block]) + sum(under[block][:part + 1])


UNDER_X = (6, 4, 6, 4)

CO_EARLY = 3

C_MIX, C_CROSS, C_MEM, C_FFN, C_FINAL = (NK * i for i in range(5))
C_GATE = 5 * NK
C_CONVW = C_GATE + 2 * NK
C_CONVB = C_CONVW + 3 * FF_T
C_SUB = C_CONVB + FF_T
C_LAM = C_SUB + 1
C_ALL = C_LAM + 4 * 64

NEAR_W = 640 + 3
DIL_BIAS_W = NEAR_W + 1 + 256 + 512
REGION = 28928


def trunk_layer(nc, x, mem, w_stream, columns, ident, alibi_diff, alibi_dil, out):
    z_dram = nc.dram_tensor("gate_spill", [2 * NK, P, S], F32, kind="Internal").ap()
    mem_kv = nc.dram_tensor("mem_kv", [P, 4 * S], F32, kind="Internal").ap()
    mem_rows = mem.rearrange("(j p) d -> p j d", p=P)
    x_cols = x.rearrange("(b p) (k d) -> k p b d", p=P, d=P)
    out_rows = out.rearrange("(b p) d -> b p d", p=P)

    with ExitStack() as ctx:
        def sb(name, shape, dt=F32, scope=ctx):
            return scope.enter_context(nc.sbuf_tensor(name, shape, dt))

        def sem(name):
            return ctx.enter_context(nc.semaphore(name))

        ps = ctx.enter_context(nc.psum_tensor("ps", [P, 8, HALF], F32))
        PJ = 0
        SC = 2
        TB = 6
        MEM_BANKS = (PJ, PJ + 1, TB, TB + 1)
        NS = 5

        h_hi = sb("h_hi", [P, NK, S], F32R)
        h_lo = sb("h_lo", [P, NK, S], F32R)
        w_raw = sb("w_raw", [P, 2, NK, P])
        w_hi = sb("w_hi", [P, 2, NK, P], F32R)
        w_lo = sb("w_lo", [P, 2, NK, P], F32R)
        rstd_bc = sb("rstd_bc", [P, S])
        idn = sb("idn", [P, P])
        col = sb("col", [P, C_ALL])
        lam_tmp = sb("lam_tmp", [P, 2, 64])
        small = sb("small", [P, 64])
        ones = small[:, 0:1]
        neg_half = small[:, 8:16]
        neglam = small[:, 16:17]
        sub_gain = small[:, 17:18]
        lam_dot = small[:, 20:22]
        lam_exp = small[:, 22:24]
        msq = small[:, 24:32]
        rstd_tok = small[:, 32:40]
        mem_ssq = small[:, 40:42]
        mem_msq = small[:, 42:44]
        mem_rstd = small[:, 44:46]
        spare = small[:, 56:63]
        gate_spare, tb_spare = small[:, 48:50], small[:, 50:51]
        zero_col = small[:, 52:53]

        def phase(*parts):
            with ExitStack() as scope:
                return [sb(p[0] or f"gap{nc.next_id()}", [P, p[1]], p[2] if len(p) > 2 else F32, scope)
                        for p in parts]

        def tiles(t, n):
            return t[:, :].rearrange("p (k s) -> p k s", k=n)

        LOW, OT, HIGH = 8 * S, (DIFF_H + DIL_H) * S, REGION - 20 * S
        TOP = REGION - 24 * S
        low, oT_, high = phase(("attn_low", LOW), ("oT", OT), ("attn_high", HIGH))
        oT = tiles(oT_, DIFF_H + DIL_H)
        df_parts = phase(("df_parts", 6 * S, F32R))[0]
        od_hi, od_lo, y_hi, y_lo, top = phase(
            ("od_hi", 4 * S, F32R), ("od_lo", 4 * S, F32R), ("y_hi", 8 * S, F32R), ("y_lo", 8 * S, F32R), ("top", TOP))
        od_hi, od_lo, y_hi, y_lo = tiles(od_hi, DIL_H), tiles(od_lo, DIL_H), tiles(y_hi, NK), tiles(y_lo, NK)
        xt = tiles(phase(("xt", LOW))[0], NK)
        _, mem_x, mem_sq, mn_hi, mn_lo, mv_t, _ = phase(
            (None, LOW), ("mem_x", 2 * S), ("mem_sq", S), ("mn_hi", 2 * S, F32R), ("mn_lo", 2 * S, F32R), ("mv_t", S),
            (None, 4 * S))
        mem_x, mn_hi, mn_lo, mv_t = tiles(mem_x, 2), tiles(mn_hi, NK), tiles(mn_lo, NK), tiles(mv_t, 4)
        _, co, x_buf = phase((None, LOW), ("co", 8 * S), ("x_buf", REGION - 16 * S))
        co = tiles(co, NK)
        _, g_hi, g_lo, ff = phase(
            (None, LOW), ("g_hi", 8 * S, F32R), ("g_lo", 8 * S, F32R), ("ff", TOP))
        g_hi, g_lo = tiles(g_hi, NK), tiles(g_lo, NK)
        o_rows = tiles(phase((None, LOW), ("o_rows", 8 * S))[1], 2 * NB)

        def view(t, at, n):
            return t[:, at:at + n]

        dl_q = [view(low, g * S, S) for g in range(3)]
        dl_k = [view(low, (3 + g) * S, S) for g in range(3)]
        dl_vT = view(low, 6 * S, S)
        dl_st = dl_vT.rearrange("p (b e) -> p b e", b=NB)
        dl_gate = view(low, 7 * S, S)
        df_gate = view(high, 0, S)
        dl_v = [view(high, g * S, S).rearrange("p (b e) -> p b e", b=NB) for g in range(3)]
        dl_p = [view(high, 3 * S + 1152 * i, 1152) for i in range(2)]
        dl_pT = view(high, 3 * S + 2304, 1152).rearrange("p (b q) -> p b q", b=9)
        dl_bias = view(high, 3 * S + 3456, DIL_BIAS_W)
        dl_near = dl_bias[:, 0:NEAR_W]
        dl_far = [dl_bias[:, NEAR_W + 1:NEAR_W + 257], dl_bias[:, NEAR_W + 257:NEAR_W + 769]]
        stat = view(high, 3 * S + 3456 + DIL_BIAS_W, 160)
        dl_mx, dl_nm, dl_den, dl_rd = stat[:, 0:16], stat[:, 16:24], stat[:, 24:32], stat[:, 32:40]
        df_k_hi, df_k_lo = ([view(df_parts, (2 * j + i) * S, S) for i in range(2)] for j in range(2))
        df_q_hi, df_q_lo = (view(df_parts, (4 + i) * S, S) for i in range(2))
        df_k = [view(low, (2 + i) * S, S) for i in range(2)]
        df_q = view(low, 5 * S, S)
        df_v = [view(high, (5 + i) * S, S).rearrange("p (b e) -> p b e", b=NB) for i in range(2)]
        df_p = [view(low, (6 + i) * S, S) for i in range(2)]
        df_vT = view(high, 0, S)
        df_a = view(high, S, S)
        df_aT = view(high, 2 * S, S).rearrange("p (b q) -> p b q", b=NB)
        df_bias = view(high, 3 * S, S)
        df_st = view(high, 4 * S, S).rearrange("p (b e) -> p b e", b=NB)
        df_sq = view(high, 7 * S, P)
        df_mx, df_nm, df_den, df_rd = (stat[:, 40 + 16 * i:56 + 16 * i] for i in range(4))
        df_cc, df_ssq, df_ms, df_rs = (stat[:, 104 + 8 * i:112 + 8 * i] for i in range(4))
        x0 = [view(low, i * S, S).rearrange("p (b d) -> p b d", b=NB) for i in range(2)]
        sq = [view(low, 2 * S, S), view(top, 2 * S, S), view(ff, 0, S), view(ff, S + 8, S)]
        acc = [view(low, 3 * S, S), view(top, 3 * S, S), view(ff, S, S), view(ff, 2 * S + 8, S)]
        mem_k_v = view(high, 0, 4 * S)

        def keys_values(t, at):
            return (view(t, at, 2 * S).rearrange("p (t m) -> p t m", t=NK),
                    view(t, at + 2 * S, 2 * S).rearrange("p (j e) -> p j e", j=2))

        mk0, mv0 = keys_values(high, 0)

        def head_parts(k):
            return (h_hi[:, k, :], h_lo[:, k, :]) if k < DIFF_H else (od_hi[:, k - DIFF_H, :], od_lo[:, k - DIFF_H, :])

        zb = [[view(top, (2 * s + i) * S, S) for i in range(2)] for s in range(2)]
        x_back = [view(top, i * S, S).rearrange("p (b d) -> p b d", b=NB) for i in range(2)]
        mk, mv = keys_values(x_buf, 0)
        qx = view(x_buf, 4 * S, 2 * S).rearrange("p (j s) -> p j s", j=2)
        px = [view(x_buf, (6 + i) * S, S).rearrange("p (b m) -> p b m", b=4) for i in range(2)]
        pxT = view(x_buf, 8 * S, S).rearrange("p (j q) -> p j q", j=2)
        mvh = view(x_buf, 9 * S, HALF).rearrange("p (j e) -> p j e", j=2)
        x_st = view(x_buf, 9 * S + HALF, 32)
        x_mx, x_nm, x_den, x_rd = (x_st[:, 8 * i:8 * i + 8] for i in range(4))
        before_last = NK - NK // X_H
        a_pad = view(ff, 0, S + 2)
        c_buf = view(ff, S + 8, S)
        b_buf = view(ff, 2 * S + 8, S)

        const_in = sem("const_in")
        const_ok = sem("const_ok")
        lam_dots, lam_exps, lam_ok = sem("lam_dots"), sem("lam_exps"), sem("lam_ok")
        w_in = [sem("w_in0"), sem("w_in1")]
        w_rounded, w_ready = sem("w_rounded"), sem("w_ready")
        pj_ready, pj_free = sem("pj_ready"), sem("pj_free")
        tb_full, tb_free = sem("tb_full"), sem("tb_free")
        x0_in = [sem("x0_in0"), sem("x0_in1")]
        x0_turned, x0_free = sem("x0_turned"), sem("x0_free")
        back_in = [sem("back_in0"), sem("back_in1")]
        feed_act = [sem(f"feed_act{i}") for i in range(4)]
        feed_dve = [sem(f"feed_dve{i}") for i in range(4)]
        nf_sum, nf_ms, nf_rstd = sem("nf_sum"), sem("nf_ms"), sem("nf_rstd")
        nf_turn, nf_bc = sem("nf_turn"), sem("nf_bc")
        bias_in = sem("bias_in")
        dl_s, dl_max, dl_neg, dl_exp = sem("dl_s"), sem("dl_max"), sem("dl_neg"), sem("dl_exp")
        dl_rec, dl_slope = sem("dl_rec"), sem("dl_slope")
        gate_out = [sem("gate_out0"), sem("gate_out1")]
        df_s, df_max, df_neg, df_exp = sem("df_s"), sem("df_max"), sem("df_neg"), sem("df_exp")
        df_rec, df_coef, df_comb, df_slope = sem("df_rec"), sem("df_coef"), sem("df_comb"), sem("df_slope")
        df_mean, df_pow, df_norm = sem("df_mean"), sem("df_pow"), sem("df_norm")
        df_hi, df_lo = sem("df_hi"), sem("df_lo")
        split_hi, split_lo = sem("split_hi"), sem("split_lo")
        z_sig, y_sum, y_round, y_done = sem("z_sig"), sem("y_sum"), sem("y_round"), sem("y_done")
        z_in = [sem("z_in0"), sem("z_in1")]
        mem_out, kv_in = sem("mem_out"), sem("kv_in")
        mem_in, mem_sums, mem_mean, mem_pow = sem("mem_in"), sem("mem_sums"), sem("mem_mean"), sem("mem_pow")
        mem_norm, mem_turn, mem_hi, mem_lo = sem("mem_norm"), sem("mem_turn"), sem("mem_hi"), sem("mem_lo")
        x_head, x_s, x_max, x_neg, x_exp = sem("x_head"), sem("x_s"), sem("x_max"), sem("x_neg"), sem("x_exp")
        x_rec, x_norm = sem("x_rec"), sem("x_norm")
        co_round, co_split = sem("co_round"), sem("co_split")
        conv0, conv1, conv2, gelu_ok = sem("conv0"), sem("conv1"), sem("conv2"), sem("gelu_ok")
        m_prod, m_round, m_done = sem("m_prod"), sem("m_round"), sem("m_done")
        fin_scaled, fin_turn, fin_out = sem("fin_scaled"), sem("fin_turn"), sem("fin_out")
        fin_row = [sem("fin_row_act"), sem("fin_row_dve")]


        block = ctx.enter_context(nc.Block())

        def bank(b, n=HALF):
            return ps[:, b, 0:n]

        def banks(b, n):
            return ps[:, b:b + -(-n // HALF), :].rearrange("p b n -> p (b n)")[:, 0:n]

        def by_residue(ap):
            return ap.rearrange("p (j r) -> p r j", r=4)

        def half_by_residue(ap, half):
            return ap.rearrange("p (r j) -> p r j", r=4)[:, :, half * P:(half + 1) * P]

        @block.sync
        def _(sp):
            sp.dma_start(mem_x, mem_rows).then_inc(mem_in, 16)
            sp.dma_start(idn[:, :], ident).then_inc(const_in, 16)
            sp.dma_start(col[:, :], columns).then_inc(const_in, 16)
            for n in range(2):
                sp.dma_start(w_raw[:, n], w_stream[n]).then_inc(w_in[n], 16)
                sp.dma_start(x0[n], x_cols[n]).then_inc(x0_in[n], 16)

            def load_weights(first, last):
                with sp.Fori(first // 2, last // 2) as t:
                    for s in range(2):
                        sp.wait_ge(w_ready, t * 2 + (s - 1))
                        sp.dma_start(w_raw[:, s], w_stream[t * 2 + s]).then_inc(w_in[s], 16)

            with sp.Fori(1, NK // 2) as t:
                for s in range(2):
                    for n in range(2):
                        sp.wait_ge(w_ready, t * 4 + (2 * s + n - 3))
                        sp.dma_start(w_raw[:, n], w_stream[t * 4 + (2 * s + n - 2)]).then_inc(w_in[n], 16)
                    sp.wait_ge(x0_turned, t * 2 + (s - 1))
                    sp.dma_start(x0[s], x_cols[t * 2 + s]).then_inc(x0_in[s], 16)
            load_weights(W_DIL - 2, W_DIL + 2)
            sp.wait_ge(pj_free, W_DIL + 2)
            sp.wait_ge(tb_free, F_DIL + 2)
            sp.dma_start(mem_kv, mem_k_v).then_inc(mem_out, 16)
            sp.dma_start(dl_bias, alibi_dil).then_inc(bias_in, 16)
            load_weights(W_DIL + 2, W_DIFF + 2)
            sp.wait_ge(tb_free, F_DIFF + 2)
            sp.dma_start(df_bias, alibi_diff).then_inc(bias_in, 16)
            load_weights(W_DIFF + 2, W_TOTAL)
            for r in range(2 * NB):
                sp.wait_ge(fin_row[r % 2], r // 2 + 1)
                sp.dma_start(out_rows[r // 2, :, (r % 2) * HALF:(r % 2 + 1) * HALF],
                             o_rows[:, r, :]).then_inc(fin_out, 16)
            sp.wait_ge(fin_out, 16 * 2 * NB)
            for half in range(2):
                sp.wait_ge(gate_out[half], 16 * 2 * NK + 16)
            sp.wait_ge(mem_out, 16)

        @block.gpsimd
        def _(pool):
            def aside(*values):
                for value in values:
                    pool.compute_val(value)
                pool.wait_ge(const_ok, 3)
                return values

            def split_tile(n, s, used):
                loaded = (n - s) * 8 + 16
                if used is not None:
                    loaded, used = aside(loaded, used)
                pool.wait_ge(w_in[s], loaded)
                if used is not None:
                    pool.wait_ge(pj_ready, used)
                pool.tensor_scalar(w_hi[:, s], w_raw[:, s], 1.0, 1.0, ALU.mult, ALU.mult).then_inc(w_rounded, 1)
                pool.wait_ge(w_rounded, n + 1)
                pool.tensor_tensor(w_lo[:, s], w_raw[:, s], w_hi[:, s].bitcast(F32),
                                   ALU.subtract).then_inc(w_ready, 1)

            def split_tiles(first, last):
                each = 1 if last <= W_DIL + 2 else 2
                base = unit_of(first - 2) + each
                with pool.Fori(0, (last - first) // 2) as t:
                    for s in range(2):
                        split_tile(t * 2 + (first + s), s, t * (2 * each) + (base + s * each))

            def split_now(n):
                split_tile(n, n % 2, unit_of(n - 2) + 2 if n >= 2 else None)

            def norm_root(i):
                pool.wait_ge(nf_ms, i + 1)
                pool.tensor_tensor(rstd_tok, msq, neg_half, ALU.pow).then_inc(nf_rstd, 1)

            def head_root(h):
                pool.wait_ge(tb_free, *aside(h * DIFF_USES + (F_DIFF + 2 + DF_LAST + 3)))
                pool.tensor_scalar(df_ms, df_ssq, 1.0 / P, EPS, ALU.mult, ALU.add).then_inc(df_mean, 1)
                pool.wait_ge(df_mean, h + 1)
                pool.tensor_tensor(df_rs, df_ms, neg_half, ALU.pow).then_inc(df_pow, 1)

            pool.memset(ones, 1.0).then_inc(const_ok, 1)
            pool.memset(neg_half, -0.5).then_inc(const_ok, 1)
            pool.memset(zero_col, 0.0).then_inc(const_ok, 1)
            pool.wait_ge(const_ok, 3)
            pool.wait_ge(mem_sums, 2)
            pool.tensor_scalar(mem_msq, mem_ssq, 1.0 / D, EPS, ALU.mult, ALU.add).then_inc(mem_mean, 1)
            pool.wait_ge(mem_mean, 1)
            pool.tensor_tensor(mem_rstd, mem_msq, neg_half[:, 0:2], ALU.pow).then_inc(mem_pow, 1)
            split_now(0)
            split_now(1)
            split_tiles(2, W_DIL + 2)
            norm_root(0)
            split_tiles(W_DIL + 2, W_DIFF)
            for n in range(W_DIFF, W_DIFF + 4):
                split_now(n)
            with pool.Fori(0, DIFF_H // 2 - 1) as t:
                for par in range(2):
                    for j in range(3):
                        n = W_DIFF + 4 + 3 * par + j
                        split_tile(t * 6 + n, n % 2, t * 12 + unit_of(n - 1))
                    head_root(t * 2 + par)
            for n in range(W_GATE - 2, W_GATE + 1):
                split_now(n)
            head_root(DIFF_H - 2)
            for n in range(W_GATE + 1, W_BRANCH):
                split_now(n)
            head_root(DIFF_H - 1)
            for n in range(W_BRANCH, W_BRANCH + 2):
                split_now(n)
            split_tiles(W_BRANCH + 2, W_CQ)
            for n in range(W_CQ, W_CQ + 2):
                split_now(n)
            norm_root(1)
            split_tiles(W_CQ + 2, W_FF)
            for n in range(W_FF, W_FF + 2):
                split_now(n)
            norm_root(2)
            split_tiles(W_FF + 2, W_TOTAL)
            norm_root(3)

        @block.tensor
        def _(pe):
            def product(n, s, half, u, hi=h_hi, lo=h_lo, kt=NK, cols=HALF, add_x=None, x_in=None, steps=None,
                        before=None):
                steps = range(kt) if steps is None else steps
                if half == 0 and steps[0] == 0:
                    pe.wait_ge(w_ready, n + 1)
                if steps[0] == 0:
                    pe.wait_ge(pj_free, u + 1)
                b = half if cols == HALF else s
                at = slice(half * cols, half * cols + cols)
                for k in steps:
                    if before is not None:
                        before(k)
                    pe.matmul(bank(b, cols), w_hi[:, s, k, :], hi[:, k, at], start=(k == 0), stop=False)
                    pe.matmul(bank(b, cols), w_hi[:, s, k, :], lo[:, k, at], start=False, stop=False)
                    last = pe.matmul(bank(b, cols), w_lo[:, s, k, :], hi[:, k, at], start=False,
                                     stop=(k == kt - 1 and add_x is None))
                if add_x is not None:
                    pe.wait_ge(back_in[s], x_in)
                    for j in range(4):
                        last = pe.matmul(ps[:, b, j * P:(j + 1) * P], add_x[:, 4 * half + j, :], idn[:, :],
                                         start=False, stop=(j == 3))
                if steps[-1] == kt - 1:
                    last.then_inc(pj_ready, 1)

            def products(first, tiles_n, before=None, **kw):
                def pair(t, gated):
                    for s in range(2):
                        for half in range(2):
                            product(t * 2 + (first + s), s, half, t * 4 + (unit_of(first) + 2 * s + half),
                                    before=None if s or half else gated, **kw)

                if before is not None:
                    pair(0, before)
                with pe.Fori(0 if before is None else 1, tiles_n // 2) as t:
                    pair(t, None)

            def turn(f, use, sources):
                pe.wait_ge(tb_free, f + (use + 1))
                for j, source in enumerate(sources):
                    last = pe.transpose(ps[:, TB + use % 2, j * P:(j + 1) * P], source, idn[:, :])
                last.then_inc(tb_full, 1)

            def turn_blocks(f, use, buf):
                for part in range(2):
                    turn(f, use + part, [buf[:, 4 * part + i, :] for i in range(4)])

            def norm_sum(i):
                pe.wait_ge(feed_dve[i], (NK if i == 3 else 2 * NK) + 1)
                for b in range(NB):
                    last = pe.matmul(ps[:, NS, b:b + 1], acc[i][:, b * P:(b + 1) * P], ones, start=True, stop=True)
                last.then_inc(nf_sum, 1)

            def norm_spread(i):
                pe.wait_ge(nf_rstd, i + 1)
                for b in range(NB):
                    last = pe.transpose(ps[:, SC + b // 4, (b % 4) * P:(b % 4 + 1) * P],
                                        rstd_tok[:, b:b + 1].to_broadcast([P, P]), idn[:, :])
                last.then_inc(nf_turn, 1)

            pe.wait_ge(const_in, 32)
            pe.wait_ge(const_ok, 3)
            pe.wait_ge(mem_norm, 2)
            for k in range(NK):
                for j in range(2):
                    at = (k % 2) * MEM + j * P
                    last = pe.transpose(ps[:, MEM_BANKS[k // 2], at:at + P], mem_x[:, j, k * P:(k + 1) * P], idn[:, :])
                if k % 2:
                    last.then_inc(mem_turn, 1)

            with pe.Fori(0, NK // 2) as t:
                for s in range(2):
                    pe.wait_ge(x0_in[s], t * 16 + 16)
                    pe.wait_ge(x0_free, t * 2 + (s + 1))
                    for b in range(NB):
                        last = pe.transpose(ps[:, SC + 2 * s + b // 4, (b % 4) * P:(b % 4 + 1) * P],
                                            x0[s][:, b, :], idn[:, :])
                    last.then_inc(x0_turned, 1)
                    pe.wait_ge(mem_lo, NK)
                    for n in range(2):
                        product(t * 4 + (2 * s + n), n, 0, t * 4 + (2 * s + n), hi=mn_hi, lo=mn_lo, cols=MEM)
                    pe.wait_ge(pj_free, t * 4 + (2 * s + 3))
                    turn(t * 2 + F_MEM, s, [mv_t[:, s, j * P:(j + 1) * P] for j in range(2)])
            norm_sum(0)
            norm_spread(0)

            def dil_scores(b):
                rho, jb = b // 2, b % 2
                sc = banks(SC, 1152)
                near0, near = (0, 512) if jb == 0 else (384, 640)
                at = 0
                for g, k0, n in ((0, near0, near), (1, rho * 256, (jb + 1) * P), (2, rho * 256, (jb + 1) * P)):
                    while n:
                        m = min(n, HALF - at % HALF)
                        last = pe.matmul(sc[:, at:at + m], dl_q[g][:, b * P:(b + 1) * P], dl_k[g][:, k0:k0 + m],
                                         start=True, stop=True)
                        at, k0, n = at + m, k0 + m, n - m
                last.then_inc(dl_s, 1)

            def dil_values(b):
                rho, jb = b // 2, b % 2
                return ([dl_v[0][:, i, :] for i in (range(4) if jb == 0 else range(3, 8))]
                        + [dl_v[g][:, 2 * rho + j, :] for g in (1, 2) for j in range(jb + 1)])

            with pe.Fori(0, DIL_H) as t:
                f = t * DIL_USES + F_DIL
                u = t * (2 * DIL_TILES) + unit_of(W_DIL)
                for j in range(QKV):
                    for half in range(2):
                        product(t * DIL_TILES + (W_DIL + j), j % 2, half, u + (2 * j + half))
                        if half == 0 and j in (3, 6):
                            pe.wait_ge(pj_free, u + (2 * j + 2))
                            turn_blocks(f, 2 * (j // 3 - 1), dl_vT.rearrange("p (b e) -> p b e", b=NB))
                gates = [(QKV + j, half, k) for j in range(DIL_GATES) for half in range(2) for k in range(NK)]

                def gate_steps(count):
                    for _ in range(count):
                        j, half, k = gates.pop(0)
                        product(t * DIL_TILES + (W_DIL + j), j % 2, half, u + (2 * j + half), steps=(k,))

                use = 2 * GROUPS
                for b in range(NB + 1):
                    if b < NB:
                        if b >= 1:
                            pe.wait_ge(dl_max, t * (2 * NB) + 2 * b)
                        dil_scores(b)
                    gate_steps(UNDER_DIL[b][0])
                    if b == 0:
                        pe.wait_ge(pj_free, u + (2 * QKV + 2))
                        turn_blocks(f, use - 2, dl_vT.rearrange("p (b e) -> p b e", b=NB))
                    if b >= 1:
                        n = dil_tiles((b - 1) % 2)
                        pe.wait_ge(dl_exp, t * NB + b)
                        for k in range(fills(n)):
                            if k == 2:
                                gate_steps(1)
                            turn(f, use, [dl_p[(b - 1) % 2][:, i * P:(i + 1) * P]
                                          for i in range(4 * k, min(n, 4 * k + 4))])
                            use += 1
                        gate_steps(UNDER_DIL[b][1] - (1 if fills(n) > 2 else 0))
                        pe.wait_ge(tb_free, f + (use + 2))
                        for i, v in enumerate(dil_values(b - 1)):
                            last = pe.matmul(ps[:, TB + use % 2, 0:P], dl_pT[:, i, :], v, start=(i == 0),
                                             stop=(i == n - 1))
                        last.then_inc(tb_full, 1)
                        use += 1
                gate_steps(len(gates))
                pe.wait_ge(tb_free, f + (use + 2))
                turn_blocks(f, use, dl_st)
                assert use + 2 == DIL_USES

            def df_scores(h, i, par):
                if i in (0, NB // 2):
                    pe.wait_ge(df_lo, h * 4 + (4 if i else 3))
                for m in range(2):
                    if i >= 1:
                        pe.wait_ge(df_max, h * (2 * NB) + (2 * i - 1 + m))
                    rows = slice(64 * m, 64 * m + 64)
                    n = (i + 1) * P
                    for at in range(0, n, HALF):
                        w = min(HALF, n - at)
                        for n_pass, (q, k) in enumerate(((df_q_hi, df_k_hi), (df_q_hi, df_k_lo), (df_q_lo, df_k_hi))):
                            last = pe.matmul(ps[:, SC + 2 * m + at // HALF, 0:w], q[rows, i * P:(i + 1) * P],
                                             k[par][rows, at:at + w], start=(n_pass == 0),
                                             stop=(n_pass == 2))
                    last.then_inc(df_s, 1)

            def df_turn_values(f, use, u):
                pe.wait_ge(pj_free, u + 3)
                turn_blocks(f, use, df_vT.rearrange("p (b e) -> p b e", b=NB))

            def df_head(pair, par, f, tiles_under, more):
                h = pair * 2 + par
                n0 = W_DIFF + 3 + 3 * par
                under = [(j, half, k) for j in range(tiles_under) for half in range(2) for k in range(NK)]
                use = 0

                def steps_under(count):
                    for _ in range(count):
                        j, half, k = under.pop(0)
                        product(pair * 6 + (n0 + j), (n0 + j) % 2, half, pair * 12 + (unit_of(n0 + j) + half), steps=(k,))

                for i in range(NB + 1):
                    if i < NB:
                        df_scores(h, i, par)
                    steps_under(UNDER_DIFF[i][0])
                    if i >= 1:
                        pe.wait_ge(df_comb, h * NB + i)
                        for k in range(fills(i)):
                            turn(f, use, [df_a[:, j * P:(j + 1) * P] for j in range(4 * k, min(i, 4 * k + 4))])
                            use += 1
                        steps_under(UNDER_DIFF[i][1])
                        pe.wait_ge(tb_free, f + (use + 2))
                        for j in range(i):
                            last = pe.matmul(ps[:, TB + use % 2, 0:P], df_aT[:, j, :], df_v[par][:, j, :],
                                             start=(j == 0), stop=(j == i - 1))
                        last.then_inc(tb_full, 1)
                        use += 1
                assert use - 1 == DF_LAST
                if more:
                    df_turn_values(f, use, pair * 12 + (unit_of(n0) + 1))
                    use += 2
                steps_under(6 * NK - done_by(UNDER_DIFF, NB, 1))
                pe.wait_ge(df_norm, h + 1)
                turn_blocks(f, use, df_st)
                steps_under(len(under))

            for j in range(3):
                for half in range(2):
                    product(W_DIFF + j, j % 2, half, unit_of(W_DIFF + j) + half)
                    if (j, half) == (1, 0):
                        df_turn_values(F_DIFF, 0, unit_of(W_DIFF) + 1)
            with pe.Fori(0, DIFF_H // 2 - 1) as t:
                for par in range(2):
                    df_head(t, par, t * (2 * DIFF_USES) + (F_DIFF + 2 + par * DIFF_USES), 3, True)
            pair = DIFF_H // 2 - 1
            df_head(pair, 0, F_DIFF + 2 + 2 * pair * DIFF_USES, 3, True)
            df_head(pair, 1, F_DIFF + 2 + (2 * pair + 1) * DIFF_USES, LAST_GATES, False)

            def branch(t, split=None):
                u = t * 4 + unit_of(W_BRANCH)
                for half in range(2):
                    product(t * 2 + W_BRANCH, 0, half, u + half, hi=od_hi, lo=od_lo, kt=DIL_H)
                for half in range(2):
                    product(t * 2 + (W_BRANCH + 1), 1, half, u + (2 + half), before=None if half else split)

            pe.wait_ge(split_lo, DIL_H)
            branch(0, lambda k: pe.wait_ge(split_lo, DIL_H + k + 1))
            with pe.Fori(1, NK) as t:
                branch(t)

            def project_out(t, gated=None):
                for s in range(2):
                    for half in range(2):
                        product(t * 2 + (W_OUT + s), s, half, t * 4 + (unit_of(W_OUT) + 2 * s + half), x_in=t * 16 + 16,
                                hi=y_hi, lo=y_lo, add_x=x_back[s],
                                before=None if s or half else gated)

            project_out(0, lambda k: pe.wait_ge(y_done, k + 2))
            with pe.Fori(1, NK // 2) as t:
                project_out(t)

            def queries(t, steps):
                for step in steps:
                    q, k = step // NK, step % NK
                    product(t * 2 + (W_CQ + q // 2), q // 2, q % 2, t * 4 + (unit_of(W_CQ) + q), steps=(k,))

            def x_scores(t):
                for g in range(2):
                    pe.wait_ge(pj_free, t * 4 + (unit_of(W_CQ) + 5 + g))
                    for b in range(4):
                        q = 4 * g + b
                        for k in range(2):
                            last = pe.matmul(ps[:, SC + 2 * g + b // 2, (b % 2) * MEM:(b % 2 + 1) * MEM],
                                             qx[:, k, q * P:(q + 1) * P], mk[:, t * 2 + k, :],
                                             start=(k == 0), stop=(k == 1))
                    last.then_inc(x_s, 1)

            def x_turn(t, g):
                pe.wait_ge(x_norm, t * 2 + (g + 1))
                for j in range(2):
                    turn(t * 8 + F_CROSS, 4 * g + j, [px[g][:, b, j * P:(j + 1) * P] for b in range(4)])

            def x_output(t, g):
                pe.wait_ge(tb_free, t * 8 + (F_CROSS + 4 * g + 4))
                pe.wait_ge(x_head, t + 1)
                for e in range(2):
                    for j in range(2):
                        last = pe.matmul(bank(TB + e), mvh[:, j, e * P:(e + 1) * P], pxT[:, j, :],
                                         start=(j == 0), stop=(j == 1))
                    last.then_inc(tb_full, 1)

            product(W_CQ, 0, 0, unit_of(W_CQ), before=lambda k: pe.wait_ge(feed_dve[1], 2 * k + 2))
            norm_sum(1)
            product(W_CQ, 0, 1, unit_of(W_CQ) + 1)
            norm_spread(1)
            for half in range(2):
                product(W_CQ + 1, 1, half, unit_of(W_CQ) + 2 + half)
            pe.wait_ge(kv_in, 16)
            with pe.Fori(0, X_H - 1) as t:
                x_scores(t)
                at = 0
                for g in range(2):
                    queries(t + 1, range(at, at + UNDER_X[2 * g]))
                    at += UNDER_X[2 * g]
                    x_turn(t, g)
                    queries(t + 1, range(at, at + UNDER_X[2 * g + 1]))
                    at += UNDER_X[2 * g + 1]
                    x_output(t, g)
                queries(t + 1, range(at, 4 * NK))

            def first_tile(half, steps):
                product(W_CO, 0, half, unit_of(W_CO) + half, steps=steps,
                        before=lambda k: pe.wait_ge(co_split, k + 1))

            x_scores(X_H - 1)
            first_tile(0, range(CO_EARLY))
            x_turn(X_H - 1, 0)
            first_tile(0, range(CO_EARLY, CO_EARLY + 1))
            first_tile(1, range(CO_EARLY))
            x_output(X_H - 1, 0)
            first_tile(0, range(CO_EARLY + 1, before_last))
            x_turn(X_H - 1, 1)
            first_tile(1, range(CO_EARLY, before_last))
            x_output(X_H - 1, 1)
            for half in range(2):
                first_tile(half, range(before_last, NK))
            for half in range(2):
                product(W_CO + 1, 1, half, unit_of(W_CO) + 2 + half)
            products(W_CO + 2, NK - 2)

            product(W_FF, 0, 0, unit_of(W_FF), hi=g_hi, lo=g_lo, before=lambda k: pe.wait_ge(feed_dve[2], 2 * k + 2))
            norm_sum(2)
            product(W_FF, 0, 1, unit_of(W_FF) + 1, hi=g_hi, lo=g_lo)
            norm_spread(2)
            for half in range(2):
                product(W_FF + 1, 1, half, unit_of(W_FF) + 2 + half, hi=g_hi, lo=g_lo)
            for c, (f0, m) in enumerate(FF_CHUNKS):
                done = 0 if c else 2
                products(W_FF_AT[c] + done, 2 * m - done, hi=g_hi, lo=g_lo)
                products(W_FF_AT[c] + 2 * m, NK, hi=h_hi, lo=h_lo, kt=m,
                         before=lambda k: pe.wait_ge(m_done, f0 + k + 2))
            norm_sum(3)

            pe.wait_ge(fin_scaled, NK)
            for r in range(2 * NB):
                b, half = r // 2, r % 2
                if SC + r == NS:
                    pe.wait_ge(nf_ms, 4)
                if r >= 4:
                    pe.wait_ge(fin_row[r % 2], r // 2 - 1)
                for j in range(4):
                    last = pe.transpose(ps[:, SC + r % 4, j * P:(j + 1) * P],
                                        xt[:, 4 * half + j, b * P:(b + 1) * P], idn[:, :])
                last.then_inc(fin_turn, 1)

        @block.vector
        def _(dve):
            def aside(value, loaded):
                dve.compute_val(value)
                dve.wait_ge(bias_in, loaded)
                return value

            def take(u, half, out, kind, scale=None, cols=HALF, other=None):
                dve.wait_ge(pj_ready, u + 1)
                src = bank(half, cols)
                if kind == "copy":
                    ins = dve.tensor_copy(out, src)
                elif kind == "add":
                    ins = dve.tensor_tensor(out, src, other, ALU.add)
                elif kind == "mult":
                    ins = dve.tensor_tensor(out, src, other, ALU.mult)
                else:
                    root = rstd_bc[:, half * HALF:(half + 1) * HALF]
                    if kind == "residue":
                        src, root = by_residue(src), by_residue(root)
                    if scale is None:
                        ins = dve.tensor_tensor(out, src, root, ALU.mult)
                    else:
                        ins = dve.scalar_tensor_tensor(out, src, scale, root, ALU.mult, ALU.mult)
                ins.then_inc(pj_free, 1)

            def halves(ap, half):
                return ap[:, half * HALF:(half + 1) * HALF]

            def norm_begin(i):
                dve.memset(acc[i], 0.0).then_inc(feed_dve[i], 1)

            def feed(i, k, gain, source, hi, lo):
                dve.wait_ge(feed_act[i], k * 2 + 2)
                dve.scalar_tensor_tensor(lo, source, gain, hi, ALU.mult, ALU.subtract).then_inc(feed_dve[i], 1)
                dve.wait_ge(feed_dve[i], k * 2 + 2)
                dve.tensor_tensor(acc[i], acc[i], sq[i], ALU.add).then_inc(feed_dve[i], 1)

            def norm_mean(i):
                dve.wait_ge(nf_sum, i + 1)
                dve.tensor_scalar(msq, ps[:, NS, 0:NB], 1.0 / D, EPS, ALU.mult, ALU.add).then_inc(nf_ms, 1)

            dve.memset(spare[:, 0:1], 0.0).then_inc(pj_free, 1)
            dve.memset(spare[:, 1:2], 0.0).then_inc(pj_free, 1)
            norm_begin(0)
            dve.memset(spare[:, 3:4], 0.0).then_inc(x0_free, 1)
            dve.memset(spare[:, 4:5], 0.0).then_inc(x0_free, 1)
            for half in range(2):
                dve.memset(gate_spare[:, half:half + 1], 0.0).then_inc(gate_out[half], 16)
            dve.wait_ge(mem_pow, 1)
            for j in range(2):
                dve.tensor_scalar(mem_x[:, j, :], mem_x[:, j, :], mem_rstd[:, j:j + 1], None,
                                  ALU.mult).then_inc(mem_norm, 1)
            dve.wait_ge(const_in, 32)
            for i in range(2):
                q1, k1 = (col[:, C_LAM + 64 * (2 * i + j):C_LAM + 64 * (2 * i + j + 1)] for j in range(2))
                dve.tensor_tensor_reduce(lam_tmp[:, i, :], q1, k1, 1.0, 0.0, ALU.mult, ALU.add,
                                         lam_dot[:, i:i + 1]).then_inc(lam_dots, 1)
            dve.tensor_scalar(sub_gain, col[:, C_SUB:C_SUB + 1], 1.0 - LAM_INIT, None, ALU.mult).then_inc(lam_ok, 1)
            for k in range(NK):
                dve.wait_ge(mem_hi, (k | 1) + 1)
                dve.scalar_tensor_tensor(mn_lo[:, k, :], ps[:, MEM_BANKS[k // 2], (k % 2) * MEM:(k % 2 + 1) * MEM],
                                         col[:, C_MEM + k:C_MEM + k + 1], mn_hi[:, k, :].bitcast(F32),
                                         ALU.mult, ALU.subtract).then_inc(mem_lo, 1)
            dve.wait_ge(lam_exps, 1)
            dve.scalar_tensor_tensor(neglam, lam_exp[:, 1:2], -LAM_INIT, lam_exp[:, 0:1], ALU.add,
                                     ALU.subtract).then_inc(lam_ok, 1)

            dve.wait_ge(feed_dve[0], 1)
            with dve.Fori(0, NK // 2) as t:
                for s in range(2):
                    k = t * 2 + s
                    dve.wait_ge(feed_act[0], t * 4 + (2 * s + 2))
                    dve.scalar_tensor_tensor(h_lo[:, k, :], banks(SC + 2 * s, S), col[:, bass.ds(t * 2 + (C_MIX + s), 1)],
                                             h_hi[:, k, :].bitcast(F32), ALU.mult, ALU.subtract).then_inc(x0_free, 1)
                    dve.tensor_tensor(acc[0], acc[0], sq[0], ALU.add).then_inc(feed_dve[0], 2)
                    take(t * 4 + 2 * s, 0, mv_t[:, s, :], "copy", cols=MEM)
                    take(t * 4 + (2 * s + 1), 1, mk0[:, k, :], "copy", cols=MEM)
                    dve.wait_ge(feed_dve[0], t * 4 + (2 * s + 3))
            norm_mean(0)

            def take_gate(g, u, half, buf):
                dve.wait_ge(gate_out[half], g * 16 + 16)
                take(u, half, halves(buf, half), "plain")

            dve.wait_ge(bias_in, 16)
            dve.tensor_scalar(dl_bias, dl_bias, 0.25, None, ALU.mult).then_inc(dl_slope, 1)
            dve.wait_ge(mem_out, 16)
            dve.wait_ge(nf_bc, 1)
            with dve.Fori(0, DIL_H) as t:
                u = t * (2 * DIL_TILES) + unit_of(W_DIL)
                for j in range(QKV):
                    g, kind = j // 3, j % 3
                    for half in range(2):
                        if kind == 0:
                            take(u + (2 * j + half), half, half_by_residue(dl_q[g], half), "residue", DIL_SCALE)
                        else:
                            buf = dl_k[g] if kind == 1 else dl_vT
                            if g == 0:
                                take(u + (2 * j + half), half, halves(buf, half), "plain")
                            else:
                                take(u + (2 * j + half), half, half_by_residue(buf, half), "residue")
                gates = [(j, half) for j in range(DIL_GATES) for half in range(2)]

                def take_gates(steps):
                    while gates and 8 * (2 * DIL_GATES - len(gates) + 1) <= steps:
                        j, half = gates.pop(0)
                        take_gate(t * DIL_GATES + j, u + (2 * (QKV + j) + half), half, dl_gate)

                dve.wait_ge(dl_slope, t + 1)
                for b in range(NB + 1):
                    if b < NB:
                        rho, jb = b // 2, b % 2
                        near, far = (512, 256) if jb == 0 else (640, 512)
                        near0 = 131 - rho if jb == 0 else 3 - rho
                        sc = banks(SC, near + far)
                        pb = dl_p[b % 2]
                        dve.wait_ge(dl_s, aside(t * NB + (b + 1), 16))
                        dve.tensor_tensor_reduce(pb[:, 0:near], sc[:, 0:near], dl_near[:, near0:near0 + near],
                                                 1.0, -3e38, ALU.add, ALU.max, dl_mx[:, 2 * b:2 * b + 1]).then_inc(dl_max, 1)
                        dve.tensor_tensor_reduce(pb[:, near:near + far], sc[:, near:near + far], dl_far[jb],
                                                 1.0, -3e38, ALU.add, ALU.max, dl_mx[:, 2 * b + 1:2 * b + 2]).then_inc(dl_max, 1)
                        dve.wait_ge(dl_max, t * (2 * NB) + (2 * b + 2))
                        dve.tensor_scalar(dl_nm[:, b:b + 1], dl_mx[:, 2 * b:2 * b + 1], dl_mx[:, 2 * b + 1:2 * b + 2],
                                          -1.0, ALU.max, ALU.mult).then_inc(dl_neg, 1)
                    if b >= 1:
                        dve.wait_ge(dl_exp, t * NB + b)
                        dve.reciprocal(dl_rd[:, b - 1:b], dl_den[:, b - 1:b]).then_inc(dl_rec, 1)
                        take_gates(done_by(UNDER_DIL, b, 0))
                take_gates(8 * 2 * DIL_GATES)
                dve.tensor_scalar(dl_bias, dl_bias, 0.25, None, ALU.mult).then_inc(dl_slope, 1)

            def df_take(unit0, par, j, half):
                buf = (df_vT, df_k[par], df_q)[j]
                take(unit0 + (2 * j + half), half, halves(buf, half), "plain", DIFF_SCALE if j == 2 else None)

            def df_split(h, par, j, half):
                whole, hi, lo = ((df_k[par], df_k_hi[par], df_k_lo[par]), (df_q, df_q_hi, df_q_lo))[j - 1]
                dve.wait_ge(df_hi, h * 4 + (2 * j + half - 1))
                dve.tensor_tensor(halves(lo, half), halves(whole, half), halves(hi, half).bitcast(F32),
                                  ALU.subtract).then_inc(df_lo, 1)

            def df_take_all(h, unit0, par, projections):
                for j, half in projections:
                    df_take(unit0, par, j, half)
                    before = 2 * j + half - 1
                    if before in (2, 3):
                        df_split(h, par, before // 2, before % 2)

            def split_heads(order):
                for n, k in order:
                    hi, lo = head_parts(k)
                    dve.wait_ge(split_hi, n + 1)
                    dve.tensor_tensor(lo, oT[:, k, :], hi.bitcast(F32), ALU.subtract).then_inc(split_lo, 1)

            def df_head(pair, par, f, tiles_under, more):
                h = pair * 2 + par
                unit0 = pair * 12 + unit_of(W_DIFF + 3 + 3 * par)
                under = [(j, half) for j in range(tiles_under) for half in range(2)]
                use = 0

                def take_under(steps):
                    while under and 8 * (2 * tiles_under - len(under) + 1) <= steps:
                        j, half = under.pop(0)
                        if more:
                            df_take_all(h + 1, unit0, 1 - par, [(j, half)])
                        else:
                            take_gate(DIL_H * DIL_GATES + j, unit0 + (2 * j + half), half, df_gate)

                dve.wait_ge(df_slope, h + 1)
                for i in range(NB):
                    n = (i + 1) * P
                    if i >= 1:
                        dve.wait_ge(df_comb, h * NB + i)
                    for m in range(2):
                        dve.wait_ge(df_s, aside(h * (2 * NB) + (2 * i + m + 1), 32))
                        dve.tensor_tensor_reduce(df_p[m][:, 0:n], banks(SC + 2 * m, n), df_bias[:, S - n:S],
                                                 1.0, -3e38, ALU.add, ALU.max,
                                                 df_mx[:, 2 * i + m:2 * i + m + 1]).then_inc(df_max, 1)
                    dve.wait_ge(df_max, h * (2 * NB) + (2 * i + 2))
                    two = slice(2 * i, 2 * i + 2)
                    dve.tensor_scalar(df_nm[:, two], df_mx[:, two], -1.0, None, ALU.mult).then_inc(df_neg, 1)
                    take_under(done_by(UNDER_DIFF, i, 0))
                    dve.wait_ge(df_exp, h * (2 * NB) + (2 * i + 2))
                    dve.reciprocal(df_rd[:, two], df_den[:, two]).then_inc(df_rec, 1)
                    dve.wait_ge(df_rec, h * NB + (i + 1))
                    dve.scalar_tensor_tensor(df_cc[:, i:i + 1], df_rd[:, 2 * i + 1:2 * i + 2], neglam,
                                             df_den[:, 2 * i:2 * i + 1], ALU.mult, ALU.mult).then_inc(df_coef, 1)
                    dve.wait_ge(df_coef, h * NB + (i + 1))
                    dve.wait_ge(tb_full, f + use)
                    dve.scalar_tensor_tensor(df_a[:, 0:n], df_p[1][:, 0:n], df_cc[:, i:i + 1], df_p[0][:, 0:n],
                                             ALU.mult, ALU.add).then_inc(df_comb, 1)
                    use = (use + 1 if i else 0) + fills(i + 1)
                    take_under(done_by(UNDER_DIFF, i, 1))
                dve.wait_ge(df_comb, h * NB + NB)
                dve.tensor_scalar(df_bias, df_bias, 0.5, None, ALU.mult).then_inc(df_slope, 1)
                take_under(5 * NK)
                if more:
                    df_split(h + 1, 1 - par, 2, 0)
                dve.wait_ge(df_pow, h + 1)
                dve.tensor_tensor(df_st, df_st, df_rs.unsqueeze(2).to_broadcast([P, NB, P]), ALU.mult).then_inc(df_norm, 1)
                if more:
                    take_under(6 * NK)
                    df_split(h + 1, 1 - par, 2, 1)
                else:
                    split_heads([(n, DIFF_H + n) for n in range(DIL_H)])
                take_under(NK * 2 * tiles_under)

            df_take_all(0, unit_of(W_DIFF), 0, [(j, half) for j in range(3) for half in range(2)])
            for half in range(2):
                df_split(0, 0, 2, half)
            dve.wait_ge(bias_in, 32)
            dve.tensor_scalar(df_bias, df_bias, 0.5, None, ALU.mult).then_inc(df_slope, 1)
            dve.wait_ge(lam_ok, 2)
            for half in range(2):
                dve.wait_ge(gate_out[half], 16 * DIL_H * DIL_GATES + 16)
            with dve.Fori(0, DIFF_H // 2 - 1) as t:
                for par in range(2):
                    df_head(t, par, t * (2 * DIFF_USES) + (F_DIFF + 2 + par * DIFF_USES), 3, True)
            pair = DIFF_H // 2 - 1
            df_head(pair, 0, F_DIFF + 2 + 2 * pair * DIFF_USES, 3, True)
            df_head(pair, 1, F_DIFF + 2 + (2 * pair + 1) * DIFF_USES, LAST_GATES, False)


            dve.memset(spare[:, 5:6], 0.0).then_inc(y_done, 1)
            EARLY = 3

            def branch(t, first=False):
                for s in range(2):
                    u = t * 8 + (unit_of(W_BRANCH) + 4 * s)
                    gate, gate_dil = zb[s]
                    dve.wait_ge(z_sig, t * 4 + (2 * s + 1))
                    for half in range(2):
                        take(u + half, half, halves(gate_dil, half), "mult", other=halves(gate_dil, half))
                    if first and s == 0:
                        split_heads([(DIL_H + k, k) for k in range(EARLY, DIFF_H)])
                    dve.wait_ge(z_sig, t * 4 + (2 * s + 2))
                    for half in range(2):
                        take(u + (2 + half), half, halves(gate, half), "mult", other=halves(gate, half))
                    dve.wait_ge(pj_free, u + 6)
                    dve.tensor_tensor(gate, gate, gate_dil, ALU.add).then_inc(y_sum, 1)
                    dve.wait_ge(y_round, t * 2 + (s + 1))
                    dve.tensor_tensor(y_lo[:, t * 2 + s, :], gate, y_hi[:, t * 2 + s, :].bitcast(F32),
                                      ALU.subtract).then_inc(y_done, 1)

            split_heads([(DIL_H + k, k) for k in range(EARLY)])
            branch(0, first=True)
            with dve.Fori(1, NK // 2) as t:
                branch(t)

            dve.wait_ge(y_done, NK + 1)
            norm_begin(1)
            dve.wait_ge(feed_dve[1], 1)
            with dve.Fori(0, NK) as k:
                for half in range(2):
                    take(k * 2 + (unit_of(W_OUT) + half), half, xt[:, k, half * HALF:(half + 1) * HALF], "copy")
                dve.wait_ge(pj_free, k * 2 + (unit_of(W_OUT) + 4))
                feed(1, k, col[:, bass.ds(k + C_CROSS, 1)], xt[:, k, :], h_hi[:, k, :].bitcast(F32), h_lo[:, k, :])
            norm_mean(1)

            def take_query(t, q):
                take(t * 4 + (unit_of(W_CQ) + q), q % 2, halves(qx[:, q // 2, :], q % 2), "plain", X_SCALE)

            def x_maxima(t):
                for g in range(2):
                    four = slice(4 * g, 4 * g + 4)
                    dve.wait_ge(x_s, t * 2 + (g + 1))
                    dve.tensor_reduce(x_mx[:, four], banks(SC + 2 * g, S).rearrange("p (b m) -> p b m", b=4),
                                      AX_X, ALU.max).then_inc(x_max, 1)
                    dve.wait_ge(x_max, t * 2 + (g + 1))
                    dve.tensor_scalar(x_nm[:, four], x_mx[:, four], -1.0, None, ALU.mult).then_inc(x_neg, 1)

            def x_divide(t, g):
                four = slice(4 * g, 4 * g + 4)
                dve.wait_ge(x_exp, t * 8 + (4 * g + 4))
                dve.reciprocal(x_rd[:, four], x_den[:, four]).then_inc(x_rec, 1)
                dve.wait_ge(x_rec, t * 2 + (g + 1))
                dve.tensor_tensor(px[g], px[g], x_rd[:, four].unsqueeze(2).to_broadcast([P, 4, MEM]),
                                  ALU.mult).then_inc(x_norm, 1)

            def split_co(tiles_k):
                for k in tiles_k:
                    dve.wait_ge(co_round, k + 1)
                    dve.tensor_tensor(h_lo[:, k, :], co[:, k, :], h_hi[:, k, :].bitcast(F32),
                                      ALU.subtract).then_inc(co_split, 1)

            dve.wait_ge(nf_bc, 2)
            for q in range(4):
                take_query(0, q)
            with dve.Fori(0, X_H - 1) as t:
                x_maxima(t)
                for g in range(2):
                    x_divide(t, g)
                    take_query(t + 1, g)
                for q in range(2, 4):
                    take_query(t + 1, q)
            split_co(range(CO_EARLY - 1))
            x_maxima(X_H - 1)
            split_co(range(CO_EARLY - 1, CO_EARLY))
            x_divide(X_H - 1, 0)
            split_co(range(CO_EARLY, CO_EARLY + 1))
            x_divide(X_H - 1, 1)
            split_co(range(CO_EARLY + 1, NK))

            norm_begin(2)
            dve.wait_ge(feed_dve[2], 1)
            with dve.Fori(0, NK) as k:
                for half in range(2):
                    at = slice(half * HALF, (half + 1) * HALF)
                    take(k * 2 + (unit_of(W_CO) + half), half, xt[:, k, at], "add", other=xt[:, k, at])
                dve.wait_ge(pj_free, k * 2 + (unit_of(W_CO) + 4))
                feed(2, k, col[:, bass.ds(k + C_FFN, 1)], xt[:, k, :], g_hi[:, k, :].bitcast(F32), g_lo[:, k, :])
            norm_mean(2)

            dve.memset(a_pad[:, 0:2], 0.0).then_inc(conv2, 1)
            dve.memset(c_buf, 0.0).then_inc(m_prod, 1)
            dve.memset(spare[:, 6:7], 0.0).then_inc(m_done, 1)
            dve.wait_ge(nf_bc, 3)
            for c, (f0, m) in enumerate(FF_CHUNKS):
                with dve.Fori(0, m) as t:
                    u = t * 4 + unit_of(W_FF_AT[c])
                    dve.wait_ge(conv2, t + (f0 + 1))
                    for half in range(2):
                        take(u + half, half, a_pad[:, 2 + half * HALF:2 + (half + 1) * HALF], "plain")
                    dve.wait_ge(conv0, t + (f0 + 1))
                    for tap, done in ((1, conv1), (2, conv2)):
                        w_tap = col[:, bass.ds(t + (C_CONVW + tap * FF_T + f0), 1)]
                        dve.scalar_tensor_tensor(c_buf, a_pad[:, tap:tap + S], w_tap, c_buf, ALU.mult,
                                                 ALU.add).then_inc(done, 1)
                        if tap == 1:
                            dve.wait_ge(conv1, t + (f0 + 1))
                    dve.wait_ge(m_done, t + (f0 + 1))
                    for half in range(2):
                        take(u + (2 + half), half, halves(b_buf, half), "plain")
                    dve.wait_ge(pj_free, u + 6)
                    dve.wait_ge(gelu_ok, t + (f0 + 1))
                    dve.tensor_tensor(b_buf, b_buf, c_buf, ALU.mult).then_inc(m_prod, 1)
                    dve.wait_ge(m_round, t + (f0 + 1))
                    dve.tensor_tensor(h_lo[:, t, :], b_buf, h_hi[:, t, :].bitcast(F32), ALU.subtract).then_inc(m_done, 1)
                last_chunk = c == len(FF_CHUNKS) - 1
                if last_chunk:
                    dve.wait_ge(m_done, FF_T + 1)
                    norm_begin(3)
                    dve.wait_ge(feed_dve[3], 1)
                with dve.Fori(0, NK) as k:
                    for half in range(2):
                        at = slice(half * HALF, (half + 1) * HALF)
                        take(k * 2 + (unit_of(W_FF_AT[c] + 2 * m) + half), half, xt[:, k, at], "add",
                             other=xt[:, k, at])
                    if last_chunk:
                        dve.wait_ge(feed_act[3], k + 1)
                        dve.tensor_tensor(acc[3], acc[3], sq[3], ALU.add).then_inc(feed_dve[3], 1)
                        dve.wait_ge(feed_dve[3], k + 2)
            norm_mean(3)

            dve.wait_ge(nf_rstd, 4)
            for r in range(1, 2 * NB, 2):
                dve.wait_ge(fin_turn, r + 1)
                dve.tensor_scalar(o_rows[:, r, :], bank(SC + r % 4), rstd_tok[:, r // 2:r // 2 + 1], None,
                                  ALU.mult).then_inc(fin_row[1], 1)

        @block.scalar
        def _(act):
            def aside(value):
                act.compute_val(value)
                act.wait_ge(const_in, 32)
                return value

            def turn_out(f, use, out, n=HALF, scale=None, shape=None, moving=False):
                act.wait_ge(tb_full, aside(f + (use + 1)) if moving else f + (use + 1))
                source = bank(TB + use % 2, n)
                if shape is not None:
                    source = shape(source)
                if scale is None:
                    act.activation(out, source, ACT.Copy).then_inc(tb_free, 1)
                else:
                    act.activation(out, source, ACT.Copy, scale=scale).then_inc(tb_free, 1)

            def store_gate(g, u, half, buf):
                act.wait_ge(pj_free, u + 3)
                at = slice(half * HALF, (half + 1) * HALF)
                act.dma_start(z_dram[g][:, at], buf[:, at]).then_inc(gate_out[half], 16)

            def rstd_out(i):
                act.wait_ge(nf_turn, i + 1)
                act.activation(rstd_bc[:, :], banks(SC, S), ACT.Copy).then_inc(nf_bc, 1)

            act.wait_ge(const_ok, 3)
            act.activation(spare[:, 2:3], zero_col, ACT.Copy).then_inc(tb_free, 1)
            act.activation(tb_spare, zero_col, ACT.Copy).then_inc(tb_free, 1)

            act.wait_ge(mem_in, 16)
            for j in range(2):
                if j:
                    act.wait_ge(mem_sums, 1)
                act.activation(mem_sq[:, :], mem_x[:, j, :], ACT.Square, accum_out=mem_ssq[:, j:j + 1]).then_inc(mem_sums, 1)
            act.wait_ge(lam_dots, 2)
            act.activation(lam_exp, lam_dot, ACT.Exp).then_inc(lam_exps, 1)
            act.wait_ge(const_in, 32)
            for k in range(NK):
                act.wait_ge(mem_turn, k // 2 + 1)
                act.activation(mn_hi[:, k, :], ps[:, MEM_BANKS[k // 2], (k % 2) * MEM:(k % 2 + 1) * MEM], ACT.Copy,
                               scale=col[:, C_MEM + k:C_MEM + k + 1]).then_inc(mem_hi, 1)

            with act.Fori(0, NK // 2) as t:
                for s in range(2):
                    act.wait_ge(x0_turned, aside(t * 2 + (s + 1)))
                    act.activation(h_hi[:, t * 2 + s, :], banks(SC + 2 * s, S), ACT.Copy,
                                   scale=col[:, bass.ds(t * 2 + (C_MIX + s), 1)]).then_inc(feed_act[0], 1)
                    act.wait_ge(feed_dve[0], t * 4 + (2 * s + 1))
                    act.activation(sq[0], banks(SC + 2 * s, S), ACT.Square).then_inc(feed_act[0], 1)
                    turn_out(t * 2 + F_MEM, s, mv0[:, :, bass.ds(t * MEM + s * P, P)], MEM,
                             shape=lambda ap: ap.rearrange("p (j e) -> p j e", j=2), moving=True)
            rstd_out(0)

            act.wait_ge(mem_out, 16)
            with act.Fori(0, DIL_H) as t:
                f = t * DIL_USES + F_DIL
                for use in range(2 * GROUPS):
                    turn_out(f, use, dl_v[use // 2][:, 4 * (use % 2):4 * (use % 2) + 4, :])
                use = 2 * GROUPS
                gates = [(j, half) for j in range(DIL_GATES) for half in range(2)]

                def store_gates(steps):
                    while gates and 8 * (2 * DIL_GATES - len(gates) + 1) <= steps:
                        j, half = gates.pop(0)
                        store_gate(t * DIL_GATES + j, t * (2 * DIL_TILES) + (unit_of(W_DIL) + 2 * (QKV + j) + half), half, dl_gate)

                for b in range(NB + 1):
                    if b >= 1:
                        n = dil_tiles((b - 1) % 2)
                        for k in range(fills(n)):
                            m = min(4, n - 4 * k)
                            turn_out(f, use, dl_pT[:, 4 * k:4 * k + m, :], m * P)
                            use += 1
                    if b < NB:
                        act.wait_ge(dl_neg, t * NB + (b + 1))
                        pb = dl_p[b % 2][:, 0:dil_tiles(b % 2) * P]
                        act.activation(pb, pb, ACT.Exp, bias=dl_nm[:, b:b + 1],
                                       accum_out=dl_den[:, b:b + 1]).then_inc(dl_exp, 1)
                    if b >= 1:
                        act.wait_ge(dl_rec, t * NB + b)
                        turn_out(f, use, dl_st[:, b - 1, :], P, scale=dl_rd[:, b - 1:b])
                        use += 1
                        store_gates(done_by(UNDER_DIL, b - 1, 1))
                for part in range(2):
                    turn_out(f, use + part, by_residue(oT[:, t + DIFF_H, :])[:, 2 * part:2 * part + 2, :],
                             shape=lambda ap: ap.rearrange("p (r j) -> p r j", r=2), moving=True)
                store_gates(8 * 2 * DIL_GATES)

            def round_heads(heads):
                act.wait_ge(tb_free, F_CROSS + 2)
                for k in heads:
                    act.activation(head_parts(k)[0], oT[:, k, :], ACT.Copy).then_inc(split_hi, 1)

            def df_values(f, use, par):
                for part in range(2):
                    turn_out(f, use + part, df_v[par][:, 4 * part:4 * part + 4, :])

            def df_round(h, unit0, par, j, half):
                whole, hi = ((df_k[par], df_k_hi[par]), (df_q, df_q_hi))[j - 1]
                at = slice(half * HALF, (half + 1) * HALF)
                act.wait_ge(pj_free, unit0 + (2 * j + half + 3))
                act.activation(hi[:, at], whole[:, at], ACT.Copy).then_inc(df_hi, 1)

            def df_head(pair, par, f, tiles_under, more):
                h = pair * 2 + par
                unit0 = pair * 12 + unit_of(W_DIFF + 3 + 3 * par)
                rounds = [(j, half) for j in (1, 2) for half in range(2)] if more else []
                gates = [] if more else [(j, half) for j in range(tiles_under) for half in range(2)]
                use = 0

                def store_gates(steps):
                    while gates and 8 * (2 * tiles_under - len(gates) + 1) <= steps:
                        j, half = gates.pop(0)
                        store_gate(DIL_H * DIL_GATES + j, unit0 + (2 * j + half), half, df_gate)

                for i in range(NB + 1):
                    for k in range(fills(i)):
                        m = min(4, i - 4 * k)
                        turn_out(f, use, df_aT[:, 4 * k:4 * k + m, :], m * P)
                        use += 1
                    if i < NB:
                        n = (i + 1) * P
                        act.wait_ge(df_neg, h * NB + (i + 1))
                        for m in range(2):
                            at = slice(2 * i + m, 2 * i + m + 1)
                            act.activation(df_p[m][:, 0:n], df_p[m][:, 0:n], ACT.Exp, bias=df_nm[:, at],
                                           accum_out=df_den[:, at]).then_inc(df_exp, 1)
                    if i >= 1:
                        j = i - 1
                        act.wait_ge(df_rec, h * NB + i)
                        act.wait_ge(tb_full, f + (use + 1))
                        scale = df_rd[:, 2 * j:2 * j + 1]
                        act.activation(df_st[:, j, :], bank(TB + use % 2, P), ACT.Copy, scale=scale)
                        act.activation(df_sq, bank(TB + use % 2, P), ACT.Square, scale=scale,
                                       accum_out=df_ssq[:, j:j + 1]).then_inc(tb_free, 1)
                        use += 1
                        store_gates(done_by(UNDER_DIFF, i - 1, 1))
                        while rounds and 8 * (7 - len(rounds)) <= done_by(UNDER_DIFF, i - 1, 1):
                            df_round(h + 1, unit0, 1 - par, *rounds.pop(0))
                if more:
                    for part in rounds[:-1]:
                        df_round(h + 1, unit0, 1 - par, *part)
                    df_values(f, use, 1 - par)
                    use += 2
                    df_round(h + 1, unit0, 1 - par, *rounds[-1])
                store_gates(5 * NK)
                for part in range(2):
                    turn_out(f, use + part, oT[:, h, part * HALF:(part + 1) * HALF], scale=sub_gain, moving=True)
                if not more:
                    round_heads([DIFF_H + i for i in range(DIL_H)])
                    store_gates(NK * (2 * tiles_under - 1))

            act.wait_ge(lam_ok, 2)
            df_values(F_DIFF, 0, 0)
            for j in (1, 2):
                for half in range(2):
                    df_round(0, unit_of(W_DIFF), 0, j, half)
            with act.Fori(0, DIFF_H // 2 - 1) as t:
                for par in range(2):
                    df_head(t, par, t * (2 * DIFF_USES) + (F_DIFF + 2 + par * DIFF_USES), 3, True)
            pair = DIFF_H // 2 - 1
            df_head(pair, 0, F_DIFF + 2 + 2 * pair * DIFF_USES, 3, True)
            df_head(pair, 1, F_DIFF + 2 + (2 * pair + 1) * DIFF_USES, LAST_GATES, False)

            def load_gates(t, s):
                for i in range(2):
                    act.dma_start(zb[s][i], z_dram[t + i * NK]).then_inc(z_in[s], 16)

            for half in range(2):
                act.wait_ge(gate_out[half], 16 * (NK + 1) + 16)
            load_gates(0, 0)

            def sigmoids(t, s, loads):
                act.wait_ge(z_in[s], aside(loads))
                for i in (1, 0):
                    act.activation(zb[s][i], zb[s][i], ACT.Sigmoid,
                                   bias=col[:, bass.ds(t + (C_GATE + i * NK), 1)]).then_inc(z_sig, 1)

            def branch_pair(t, more):
                for s in range(2):
                    if more or s == 0:
                        sigmoids(t * 2 + (s + 1), 1 - s, t * 32 + (32 + 32 * s))
                    act.wait_ge(y_sum, aside(t * 2 + (s + 1)))
                    act.activation(y_hi[:, t * 2 + s, :], zb[s][0], ACT.Copy).then_inc(y_round, 1)
                    act.wait_ge(y_done, t * 2 + (s + 2))
                    if more:
                        load_gates(t * 2 + (s + 2), s)
                    elif s == 0:
                        for i in range(2):
                            act.dma_start(x_back[i], x_cols[i]).then_inc(back_in[i], 16)

            act.wait_ge(pj_ready, unit_of(W_BRANCH))
            round_heads(range(2))
            store_gate(2 * NK - 1, unit_of(W_BRANCH) - 1, 1, df_gate)
            sigmoids(0, 0, 32)
            round_heads(range(2, DIFF_H))
            for half in range(2):
                act.wait_ge(gate_out[half], 16 * 2 * NK + 16)
            load_gates(1, 1)
            with act.Fori(0, NK // 2 - 1) as t:
                branch_pair(t, True)
            branch_pair(NK // 2 - 1, False)

            def feed(i, k, gain, out):
                act.activation(out, xt[:, k, :], ACT.Copy, scale=gain).then_inc(feed_act[i], 1)
                act.wait_ge(feed_dve[i], aside(k * 2 + 1))
                act.activation(sq[i], xt[:, k, :], ACT.Square).then_inc(feed_act[i], 1)

            def residual(t, more):
                for s in range(2):
                    act.wait_ge(pj_free, aside(t * 4 + (unit_of(W_OUT) + 2 * s + 4)))
                    if more:
                        act.dma_start(x_back[s], x_cols[t * 2 + (s + 2)]).then_inc(back_in[s], 16)
                    feed(1, t * 2 + s, col[:, bass.ds(t * 2 + (C_CROSS + s), 1)], h_hi[:, t * 2 + s, :])

            with act.Fori(0, NK // 2 - 1) as t:
                residual(t, True)
            residual(NK // 2 - 1, False)
            act.dma_start(x_buf[:, 0:4 * S], mem_kv).then_inc(kv_in, 16)
            rstd_out(1)

            def x_values(t):
                act.activation(mvh, mv[:, :, bass.ds(t * MEM, MEM)], ACT.Copy).then_inc(x_head, 1)

            def x_exponentials(t, g):
                act.wait_ge(x_neg, t * 2 + (g + 1))
                for b in range(4):
                    at = slice(4 * g + b, 4 * g + b + 1)
                    act.activation(px[g][:, b, :], ps[:, SC + 2 * g + b // 2, (b % 2) * MEM:(b % 2 + 1) * MEM],
                                   ACT.Exp, bias=x_nm[:, at], accum_out=x_den[:, at]).then_inc(x_exp, 1)

            def x_turned(t, g):
                for j in range(2):
                    turn_out(t * 8 + F_CROSS, 4 * g + j, pxT[:, j, :])

            def x_outputs(t, g):
                for e in range(2):
                    turn_out(t * 8 + F_CROSS, 4 * g + 2 + e, co[:, t * 2 + e, g * HALF:(g + 1) * HALF], moving=True)

            def round_co(tiles_k):
                for k in tiles_k:
                    act.activation(h_hi[:, k, :], co[:, k, :], ACT.Copy).then_inc(co_round, 1)

            act.wait_ge(kv_in, 16)
            with act.Fori(0, X_H - 1) as t:
                x_values(t)
                for g in range(2):
                    x_exponentials(t, g)
                for g in range(2):
                    x_turned(t, g)
                    x_outputs(t, g)
            x_values(X_H - 1)
            act.wait_ge(pj_ready, unit_of(W_CO))
            act.wait_ge(tb_free, F_CROSS + 8 * (X_H - 1) + 2)
            round_co(range(CO_EARLY))
            x_exponentials(X_H - 1, 0)
            round_co(range(CO_EARLY, CO_EARLY + 1))
            x_exponentials(X_H - 1, 1)
            x_turned(X_H - 1, 0)
            round_co(range(CO_EARLY + 1, before_last))
            x_outputs(X_H - 1, 0)
            x_turned(X_H - 1, 1)
            x_outputs(X_H - 1, 1)
            act.wait_ge(tb_free, F_CROSS + 8 * X_H + 2)
            round_co(range(before_last, NK))

            with act.Fori(0, NK) as k:
                act.wait_ge(pj_free, aside(k * 2 + (unit_of(W_CO) + 4)))
                feed(2, k, col[:, bass.ds(k + C_FFN, 1)], g_hi[:, k, :])
            rstd_out(2)

            for c, (f0, m) in enumerate(FF_CHUNKS):
                with act.Fori(0, m) as t:
                    act.wait_ge(pj_free, t * 4 + (unit_of(W_FF_AT[c]) + 4))
                    act.wait_ge(m_prod, aside(t + (f0 + 1)))
                    act.activation(c_buf, a_pad[:, 0:S], ACT.Identity, scale=col[:, bass.ds(t + (C_CONVW + f0), 1)],
                                   bias=col[:, bass.ds(t + (C_CONVB + f0), 1)]).then_inc(conv0, 1)
                    act.wait_ge(conv2, t + (f0 + 2))
                    act.activation(c_buf, c_buf, ACT.Gelu).then_inc(gelu_ok, 1)
                    act.wait_ge(m_prod, aside(t + (f0 + 2)))
                    act.activation(h_hi[:, t, :], b_buf, ACT.Copy).then_inc(m_round, 1)
            with act.Fori(0, NK) as k:
                act.wait_ge(pj_free, k * 2 + (unit_of(W_TOTAL - NK) + 4))
                act.wait_ge(feed_dve[3], aside(k + 1))
                act.activation(sq[3], xt[:, k, :], ACT.Square).then_inc(feed_act[3], 1)
                act.wait_ge(feed_act[3], aside(k + 1))
                act.activation(xt[:, k, :], xt[:, k, :], ACT.Copy,
                               scale=col[:, bass.ds(k + C_FINAL, 1)]).then_inc(fin_scaled, 1)

            act.wait_ge(nf_rstd, 4)
            for r in range(0, 2 * NB, 2):
                act.wait_ge(fin_turn, r + 1)
                act.activation(o_rows[:, r, :], bank(SC + r % 4), ACT.Copy,
                               scale=rstd_tok[:, r // 2:r // 2 + 1]).then_inc(fin_row[0], 1)


def tiles_of(w, cols):
    kt = w.shape[0] // P
    t = w.reshape(kt, P, -1, P).transpose(2, 1, 0, 3)[cols]
    if kt < NK:
        t = np.concatenate([t, np.zeros((t.shape[0], P, NK - kt, P), t.dtype)], axis=2)
    return t


def weight_stream(a):
    w_in, w_up, w_down, w_ckv = (a[n][0] for n in ("w_in", "w_up", "w_down", "w_ckv"))
    dil0, gate0 = 3 * DIFF_H, 3 * DIFF_H + 3 * GROUPS * DIL_H
    order = []
    for s in range(DIL_H):
        for g in range(GROUPS):
            order += [dil0 + kind * GROUPS * DIL_H + g * DIL_H + s for kind in range(3)]
        order += [gate0 + DIL_GATES * s + i for i in range(DIL_GATES)]
    for h in range(DIFF_H):
        order += [kind * DIFF_H + h for kind in (2, 1, 0)]
    order += range(gate0 + DIL_H * DIL_GATES, gate0 + 2 * NK)
    values_keys = [t for k in range(NK) for t in (NK + k, k)]
    parts = [tiles_of(w_ckv, values_keys), tiles_of(w_in, order)]
    both = [tiles_of(a[n][0], slice(None)) for n in ("w_branch_dil", "w_branch_diff")]
    parts.append(np.stack(both, axis=1).reshape(2 * NK, P, NK, P))
    parts += [tiles_of(a[n][0], slice(None)) for n in ("w_out", "w_cq", "w_co")]
    for f0, m in FF_CHUNKS:
        parts.append(tiles_of(w_up, [f for i in range(f0, f0 + m) for f in (i, FF_T + i)]))
        parts.append(tiles_of(w_down[f0 * P:(f0 + m) * P], slice(None)))
    return np.ascontiguousarray(np.concatenate(parts))


def alibi_tables():
    p = np.arange(P)[:, None]
    dist = p + S - P - np.arange(S)[None]
    diff = np.where(dist >= 0, -dist, NEG)
    dist = 4 * p + 131 - np.arange(NEAR_W + 1)[None]
    near = np.where((dist >= 0) & (dist <= 128), -dist, NEG)
    far = []
    for jb in range(2):
        step = p + P * jb - np.arange(P * (jb + 1))[None]
        far.append(np.where((step >= 0) & (step <= 128), -step, NEG))
        far.append(np.where((step >= 0) & (step % 4 == 0), -(step / 4), NEG))
    return diff.astype(np.float32), np.concatenate([near] + far, axis=1).astype(np.float32)


def column_table(a):
    def cols(v):
        return v.reshape(-1, P).T

    parts = [cols(a[n][0]) for n in ("mix_norm_g", "cross_norm_g", "mem_norm_g", "ffn_norm_g")]
    parts += [cols(a["final_norm_g"]), cols(a["b_gate"][0]), cols(a["conv_w"][0].reshape(-1)), cols(a["conv_b"][0]),
              cols(a["diff_subln_g"][0])]
    lam = np.concatenate([a[n][0] for n in ("lam_q1", "lam_k1", "lam_q2", "lam_k2")])
    parts.append(np.broadcast_to(lam[None], (P, 256)))
    return np.ascontiguousarray(np.concatenate(parts, axis=1))


def kernel(**inputs):
    import concourse.bacc as bacc
    from concourse.bass_utils import run_bass_kernel_spmd

    a = {k: np.asarray(v) for k, v in inputs.items()}
    diff, dil = alibi_tables()
    arrays = {
        "x_in": np.ascontiguousarray(a["x"][0]),
        "mem_in": np.ascontiguousarray(a["mem"][0]),
        "w_stream": weight_stream(a),
        "columns": column_table(a),
        "ident": np.eye(P, dtype=np.float32),
        "alibi_diff": diff,
        "alibi_dil": dil,
    }
    nc = bacc.Bacc("TRN2", target_bir_lowering=False, num_devices=1)
    args = [nc.dram_tensor(f"{n}_dram", v.shape, mybir.dt.from_np(v.dtype), kind="ExternalInput").ap()
            for n, v in arrays.items()]
    args.append(nc.dram_tensor("result_dram", (S, D), F32, kind="ExternalOutput").ap())
    trunk_layer(nc, *args)
    r = run_bass_kernel_spmd(nc, [{f"{n}_dram": v for n, v in arrays.items()}], core_ids=[0])
    return r.results[0]["result_dram"].reshape(1, S, D)
```
